# Optimizing a Trainium2 kernel written in Bass

```python
import jax, jax.numpy as jnp
from jax import lax
import numpy as np

D_MODEL = 1024
BATCH = 1
SEQ = 512
DEPTH = 1

CHUNK = 64
Q_BLOCK = 128
HEAD_DIM = 64
FOX_HEADS = D_MODEL // 2 // HEAD_DIM
RWKV_HEADS = D_MODEL // 2 // HEAD_DIM
FOX_WIDTH = FOX_HEADS * HEAD_DIM
RWKV_WIDTH = RWKV_HEADS * HEAD_DIM
MIX_WIDTH = FOX_WIDTH + RWKV_WIDTH
DECAY_LORA = 64
AAA_LORA = 64
GATE_LORA = 160
D_FF = ((8 * D_MODEL // 3 + 255) // 256) * 256
NORM_EPS = 1e-6
LNX_EPS = 64e-5

FOX_COLS = 3 * FOX_WIDTH + FOX_HEADS
RWKV_COLS = 3 * RWKV_WIDTH + DECAY_LORA + AAA_LORA + GATE_LORA
W_IN_COLS = FOX_COLS + RWKV_COLS


def rmsnorm(x, g):
    x32 = x.astype(jnp.float32)
    y = x32 * lax.rsqrt(jnp.mean(x32 * x32, axis=-1, keepdims=True) + NORM_EPS)
    return y.astype(x.dtype) * g

def forgetting_attention(q, k, v, f_logit, f_bias):
    B, T, H, D = q.shape
    q = jnp.transpose(q, (0, 2, 1, 3))
    k = jnp.transpose(k, (0, 2, 1, 3))
    v = jnp.transpose(v, (0, 2, 1, 3))
    log_f = jax.nn.log_sigmoid(f_logit.astype(jnp.float32) + f_bias.astype(jnp.float32))
    c = jnp.cumsum(jnp.transpose(log_f, (0, 2, 1)), axis=-1)
    scale = D ** -0.5
    outs = []
    for i in range(T // Q_BLOCK):
        q0, q1 = i * Q_BLOCK, (i + 1) * Q_BLOCK
        s = jnp.einsum('bhqd,bhkd->bhqk', q[:, :, q0:q1], k[:, :, :q1]).astype(jnp.float32) * scale
        s = s + c[:, :, q0:q1, None] - c[:, :, None, :q1]
        mask = jnp.arange(q1)[None, :] <= (q0 + jnp.arange(Q_BLOCK))[:, None]
        s = jnp.where(mask, s, -jnp.inf)
        p = jax.nn.softmax(s, axis=-1).astype(v.dtype)
        outs.append(jnp.einsum('bhqk,bhkd->bhqd', p, v[:, :, :q1]))
    o = jnp.concatenate(outs, axis=2)
    return jnp.transpose(o, (0, 2, 1, 3)).reshape(B, T, H * D)

def rwkv7_scan(r, w, k, v, a, b):
    B, T, H, D = r.shape
    tm = lambda z: jnp.moveaxis(z.astype(jnp.float32), 1, 0)

    def step(S, inp):
        r_t, w_t, k_t, v_t, a_t, b_t = inp
        Sa = jnp.einsum('bhij,bhj->bhi', S, a_t)
        S = S * w_t[:, :, None, :] + Sa[..., None] * b_t[:, :, None, :] + v_t[..., None] * k_t[:, :, None, :]
        return S, jnp.einsum('bhij,bhj->bhi', S, r_t)

    S0 = jnp.zeros((B, H, D, D), jnp.float32)
    _, y = lax.scan(step, S0, (tm(r), tm(w), tm(k), tm(v), tm(a), tm(b)))
    return jnp.moveaxis(y, 0, 1).astype(r.dtype)

def rwkv7_time_mix(p, shift_mu, w0, w_up, a0, a_up, g_up, k_k, k_a, r_k, ln_w, ln_b):
    B, T, _ = p.shape
    H, D = RWKV_HEADS, HEAD_DIM
    p_prev = jnp.concatenate([jnp.zeros_like(p[:, :1]), p[:, :-1]], axis=1)
    p = p + shift_mu * (p_prev - p)
    r, k, v, w_lat, a_lat, g_lat = jnp.split(
        p, np.cumsum([RWKV_WIDTH, RWKV_WIDTH, RWKV_WIDTH, DECAY_LORA, AAA_LORA]).tolist(), axis=-1)
    w = -jax.nn.softplus(-(w0 + jnp.tanh(w_lat) @ w_up)) - 0.5
    decay = jnp.exp(-jnp.exp(w.astype(jnp.float32)))
    a = jax.nn.sigmoid(a0 + a_lat @ a_up)
    g = jax.nn.sigmoid(g_lat) @ g_up
    heads = lambda z: z.reshape(B, T, H, D)
    kk = heads(k * k_k).astype(jnp.float32)
    kk = kk / jnp.maximum(jnp.linalg.norm(kk, axis=-1, keepdims=True), 1e-12)
    k = k * (1.0 + (a - 1.0) * k_a)
    rh, kh, vh, ah = heads(r), heads(k), heads(v), heads(a)
    y = rwkv7_scan(rh, heads(decay), kh, vh, -kk, kk * ah.astype(jnp.float32))
    y32 = y.astype(jnp.float32)
    mu = jnp.mean(y32, axis=-1, keepdims=True)
    var = jnp.mean(jnp.square(y32 - mu), axis=-1, keepdims=True)
    y = ((y32 - mu) * lax.rsqrt(var + LNX_EPS)).astype(r.dtype).reshape(B, T, H * D) * ln_w + ln_b
    bonus = jnp.sum(rh * kh * r_k, axis=-1, keepdims=True) * vh
    return (y + bonus.reshape(B, T, H * D)) * g

def first_inputs(seed: int = 0) -> dict:
    key = jax.random.key(seed)
    ks = jax.random.split(key, 24)
    L = DEPTH
    nrm = lambda k, shape, s: jax.random.normal(k, shape, jnp.float32) * s
    gain = lambda k, n: 1.0 + nrm(k, (L, n), 0.02)
    return {
        "x": jax.random.normal(ks[0], (BATCH, SEQ, D_MODEL), jnp.float32),
        "attn_norm_pre": gain(ks[1], D_MODEL),
        "attn_norm_post": gain(ks[2], D_MODEL),
        "w_in": nrm(ks[3], (L, D_MODEL, W_IN_COLS), D_MODEL ** -0.5),
        "fox_forget_bias": 2.0 + nrm(ks[4], (L, FOX_HEADS), 0.5),
        "shift_mu": jax.random.uniform(ks[5], (L, RWKV_COLS), jnp.float32),
        "rwkv_w0": -6.5 + 5.0 * jax.random.uniform(ks[6], (L, RWKV_WIDTH), jnp.float32),
        "rwkv_w_up": nrm(ks[7], (L, DECAY_LORA, RWKV_WIDTH), 0.1 * DECAY_LORA ** -0.5),
        "rwkv_a0": nrm(ks[8], (L, RWKV_WIDTH), 0.1),
        "rwkv_a_up": nrm(ks[9], (L, AAA_LORA, RWKV_WIDTH), AAA_LORA ** -0.5),
        "rwkv_g_up": nrm(ks[10], (L, GATE_LORA, RWKV_WIDTH), GATE_LORA ** -0.5),
        "rwkv_k_k": 0.85 + nrm(ks[11], (L, RWKV_WIDTH), 0.05),
        "rwkv_k_a": 1.0 + nrm(ks[12], (L, RWKV_WIDTH), 0.05),
        "rwkv_r_k": nrm(ks[13], (L, RWKV_HEADS, HEAD_DIM), 0.1),
        "rwkv_ln_w": 1.0 + nrm(ks[14], (L, RWKV_WIDTH), 0.02),
        "rwkv_ln_b": nrm(ks[15], (L, RWKV_WIDTH), 0.02),
        "w_out": nrm(ks[16], (L, MIX_WIDTH, D_MODEL), MIX_WIDTH ** -0.5),
        "ffn_norm_pre": gain(ks[17], D_MODEL),
        "ffn_norm_post": gain(ks[18], D_MODEL),
        "ffn_w_gate": nrm(ks[19], (L, D_MODEL, D_FF), D_MODEL ** -0.5),
        "ffn_w_up": nrm(ks[20], (L, D_MODEL, D_FF), D_MODEL ** -0.5),
        "ffn_w_down": nrm(ks[21], (L, D_FF, D_MODEL), D_FF ** -0.5),
    }

def first_block(x, attn_norm_pre, attn_norm_post, w_in, fox_forget_bias, shift_mu,
              rwkv_w0, rwkv_w_up, rwkv_a0, rwkv_a_up, rwkv_g_up, rwkv_k_k, rwkv_k_a,
              rwkv_r_k, rwkv_ln_w, rwkv_ln_b, w_out, ffn_norm_pre, ffn_norm_post,
              ffn_w_gate, ffn_w_up, ffn_w_down):
    B, T, _ = x.shape
    h = x
    for l in range(DEPTH):
        u = rmsnorm(h, attn_norm_pre[l])
        proj = u @ w_in[l]
        p_fox, p_rwkv = proj[..., :FOX_COLS], proj[..., FOX_COLS:]
        fq, fk, fv, ff = jnp.split(p_fox, [FOX_WIDTH, 2 * FOX_WIDTH, 3 * FOX_WIDTH], axis=-1)
        fh = lambda z: z.reshape(B, T, FOX_HEADS, HEAD_DIM)
        o_fox = forgetting_attention(fh(fq), fh(fk), fh(fv), ff, fox_forget_bias[l])
        o_rwkv = rwkv7_time_mix(p_rwkv, shift_mu[l], rwkv_w0[l], rwkv_w_up[l], rwkv_a0[l],
                                rwkv_a_up[l], rwkv_g_up[l], rwkv_k_k[l], rwkv_k_a[l],
                                rwkv_r_k[l], rwkv_ln_w[l], rwkv_ln_b[l])
        mix = jnp.concatenate([o_fox, o_rwkv], axis=-1) @ w_out[l]
        h = h + rmsnorm(mix, attn_norm_post[l])
        z = rmsnorm(h, ffn_norm_pre[l])
        f = (jax.nn.silu(z @ ffn_w_gate[l]) * (z @ ffn_w_up[l])) @ ffn_w_down[l]
        h = h + rmsnorm(f, ffn_norm_post[l])
    return h


HG_HEADS = 8
HG_DK = 128
HG_DV = 128
HG_CHUNK = 64
RET_HEADS = 4
RET_DK = 256
RET_DV = 512
RET_CHUNK = 128
ROPE_BASE = 10000.0
PEER_HEADS = 8
PEER_NKEYS = 128
PEER_N_EXPERTS = PEER_NKEYS * PEER_NKEYS
PEER_QDIM = 256
PEER_HALF = PEER_QDIM // 2
PEER_TOPK = 16
PEER_BLOCK = 128

IN_SIZES = (HG_HEADS * HG_DK, HG_HEADS * HG_DK, HG_HEADS * HG_DV, HG_HEADS * HG_DV,
            RET_HEADS * RET_DK, RET_HEADS * RET_DK, RET_HEADS * RET_DV, RET_HEADS * RET_DV,
            D_MODEL, D_MODEL)
IN_WIDTH = (2 * HG_HEADS * HG_DK + 2 * HG_HEADS * HG_DV + 2 * RET_HEADS * RET_DK
            + 2 * RET_HEADS * RET_DV + 2 * D_MODEL)


def rmsnorm_2(x, w):
    xf = x.astype(jnp.float32)
    y = xf * lax.rsqrt(jnp.mean(xf * xf, axis=-1, keepdims=True) + NORM_EPS)
    return (y * w.astype(jnp.float32)).astype(x.dtype)

def head_rms(x):
    return x * lax.rsqrt(jnp.mean(x * x, axis=-1, keepdims=True) + NORM_EPS)

def split_cols(t, sizes):
    outs, start = [], 0
    for n in sizes:
        outs.append(t[..., start:start + n])
        start += n
    return outs

def to_chunks(t, chunk):
    B, S, H, d = t.shape
    return t.reshape(B, S // chunk, chunk, H, d).transpose(1, 0, 3, 2, 4)

def from_chunks(t):
    nc, B, H, C, d = t.shape
    return t.transpose(1, 0, 3, 2, 4).reshape(B, nc * C, H, d)

def hgrn2_mix(q, f_logit, i, lb):
    B, S, _ = q.shape
    f = lb + (1.0 - lb) * jax.nn.sigmoid(f_logit)
    k = 1.0 - f
    logf = jnp.log(f)
    qc = to_chunks((q * HG_DK ** -0.5).reshape(B, S, HG_HEADS, HG_DK), HG_CHUNK)
    kc = to_chunks(k.reshape(B, S, HG_HEADS, HG_DK), HG_CHUNK)
    gc = to_chunks(logf.reshape(B, S, HG_HEADS, HG_DK), HG_CHUNK)
    vc = to_chunks(i.reshape(B, S, HG_HEADS, HG_DV), HG_CHUNK)
    causal = jnp.tril(jnp.ones((HG_CHUNK, HG_CHUNK), dtype=bool))

    def step(state, inp):
        qb, kb, gb, vb = inp
        b = jnp.cumsum(gb, axis=2)
        diff = b[:, :, :, None, :] - b[:, :, None, :, :]
        decay = jnp.exp(jnp.where(causal[:, :, None], diff, -jnp.inf))
        a = jnp.einsum('bhtd,bhsd,bhtsd->bhts', qb, kb, decay)
        o = (jnp.einsum('bhts,bhsv->bhtv', a, vb)
             + jnp.einsum('bhtd,bhdv->bhtv', qb * jnp.exp(b), state))
        b_last = b[:, :, -1:, :]
        state = (jnp.exp(b_last[:, :, 0, :])[..., None] * state
                 + jnp.einsum('bhsd,bhsv->bhdv', kb * jnp.exp(b_last - b), vb))
        return state, o

    s0 = jnp.zeros((B, HG_HEADS, HG_DK, HG_DV), jnp.float32)
    _, o = lax.scan(step, s0, (qc, kc, gc, vc))
    return from_chunks(o)

def rotary(x, pos):
    half = x.shape[-1] // 2
    inv = ROPE_BASE ** (-jnp.arange(half, dtype=jnp.float32) / half)
    ang = pos[:, None] * inv[None, :]
    cos = jnp.cos(ang)[None, :, None, :]
    sin = jnp.sin(ang)[None, :, None, :]
    x1, x2 = x[..., :half], x[..., half:]
    return jnp.concatenate([x1 * cos - x2 * sin, x1 * sin + x2 * cos], axis=-1)

def retention_mix(q, k, v):
    C = RET_CHUNK
    log_g = jnp.log(1.0 - jnp.exp2(-5.0 - jnp.arange(RET_HEADS, dtype=jnp.float32)))
    idx = jnp.arange(C, dtype=jnp.float32)
    rel = idx[:, None] - idx[None, :]
    dmask = jnp.where(rel >= 0, jnp.exp(log_g[:, None, None] * jnp.maximum(rel, 0.0)), 0.0)
    q_decay = jnp.exp(log_g[:, None] * (idx + 1.0))[None, :, :, None]
    k_decay = jnp.exp(log_g[:, None] * (C - 1.0 - idx))[None, :, :, None]
    chunk_decay = jnp.exp(log_g * C)[None, :, None, None]
    qc, kc, vc = to_chunks(q, C), to_chunks(k, C), to_chunks(v, C)

    def step(state, inp):
        qb, kb, vb = inp
        a = jnp.einsum('bhtd,bhsd->bhts', qb, kb) * dmask[None]
        o = (jnp.einsum('bhts,bhsv->bhtv', a, vb)
             + jnp.einsum('bhtd,bhdv->bhtv', qb * q_decay, state))
        state = chunk_decay * state + jnp.einsum('bhsd,bhsv->bhdv', kb * k_decay, vb)
        return state, o

    B = q.shape[0]
    s0 = jnp.zeros((B, RET_HEADS, RET_DK, RET_DV), jnp.float32)
    _, o = lax.scan(step, s0, (qc, kc, vc))
    return from_chunks(o)

def peer_ffn(h, w_q, sub_keys, expert_u, expert_v):
    B, S, D = h.shape
    T = B * S
    ht = h.reshape(T, D)
    q = (ht @ w_q).astype(jnp.float32).reshape(T, PEER_HEADS, 2, PEER_HALF)
    s = jnp.einsum('thpd,hpkd->thpk', q, sub_keys.astype(jnp.float32))
    top_s, top_i = lax.top_k(s, PEER_TOPK)
    cand = top_s[:, :, 0, :, None] + top_s[:, :, 1, None, :]
    cand_idx = top_i[:, :, 0, :, None] * PEER_NKEYS + top_i[:, :, 1, None, :]
    best_s, best_c = lax.top_k(cand.reshape(T, PEER_HEADS, PEER_TOPK * PEER_TOPK), PEER_TOPK)
    expert_idx = jnp.take_along_axis(
        cand_idx.reshape(T, PEER_HEADS, PEER_TOPK * PEER_TOPK), best_c, axis=-1)
    gates = jax.nn.softmax(best_s, axis=-1)
    nb = T // PEER_BLOCK

    def block_fn(args):
        xb, ib, gb = args
        u = jnp.take(expert_u, ib, axis=0)
        act = jax.nn.gelu(jnp.einsum('td,thkd->thk', xb, u).astype(jnp.float32))
        w = (gb * act).astype(xb.dtype)
        v = jnp.take(expert_v, ib, axis=0)
        return jnp.einsum('thk,thkd->td', w, v)

    out = lax.map(block_fn, (ht.reshape(nb, PEER_BLOCK, D),
                             expert_idx.reshape(nb, PEER_BLOCK, PEER_HEADS, PEER_TOPK),
                             gates.reshape(nb, PEER_BLOCK, PEER_HEADS, PEER_TOPK)))
    return out.reshape(B, S, D)

def second_inputs(seed: int = 0) -> dict:
    key = jax.random.key(seed)
    ks = jax.random.split(key, 14)
    f32 = jnp.float32

    def nrm(k, shape, scale):
        return jax.random.normal(k, shape, f32) * scale

    return {
        "x": nrm(ks[0], (BATCH, SEQ, D_MODEL), 1.0),
        "norm_mix_w": 1.0 + nrm(ks[1], (DEPTH, D_MODEL), 0.02),
        "w_in": nrm(ks[2], (DEPTH, D_MODEL, IN_WIDTH), D_MODEL ** -0.5),
        "hg_lower_bounds": nrm(ks[3], (DEPTH + 1, HG_HEADS * HG_DK), 0.1),
        "hg_norm_w": 1.0 + nrm(ks[4], (DEPTH, HG_HEADS * HG_DV), 0.02),
        "w_branch_hg": nrm(ks[5], (DEPTH, HG_HEADS * HG_DV, D_MODEL), (HG_HEADS * HG_DV) ** -0.5),
        "w_branch_ret": nrm(ks[6], (DEPTH, RET_HEADS * RET_DV, D_MODEL), (RET_HEADS * RET_DV) ** -0.5),
        "w_out": nrm(ks[7], (DEPTH, D_MODEL, D_MODEL), D_MODEL ** -0.5),
        "norm_ffn_w": 1.0 + nrm(ks[8], (DEPTH, D_MODEL), 0.02),
        "peer_w_q": nrm(ks[9], (DEPTH, D_MODEL, PEER_HEADS * PEER_QDIM), D_MODEL ** -0.5),
        "peer_sub_keys": nrm(ks[10], (DEPTH, PEER_HEADS, 2, PEER_NKEYS, PEER_HALF), PEER_HALF ** -0.5),
        "expert_u": nrm(ks[11], (DEPTH, PEER_N_EXPERTS, D_MODEL), D_MODEL ** -0.5),
        "expert_v": nrm(ks[12], (DEPTH, PEER_N_EXPERTS, D_MODEL), PEER_HEADS ** -0.5),
        "final_norm_w": 1.0 + nrm(ks[13], (D_MODEL,), 0.02),
    }

def second_block(x, norm_mix_w, w_in, hg_lower_bounds, hg_norm_w, w_branch_hg, w_branch_ret,
              w_out, norm_ffn_w, peer_w_q, peer_sub_keys, expert_u, expert_v, final_norm_w):
    B, S, _ = x.shape
    f32 = jnp.float32
    lbs = jnp.cumsum(jax.nn.softmax(hg_lower_bounds.astype(f32), axis=0), axis=0)
    pos = jnp.arange(S, dtype=f32)
    for l in range(DEPTH):
        h = rmsnorm_2(x, norm_mix_w[l])
        proj = h @ w_in[l]
        hq, hf, hi, hg, rq, rk, rv, rg, gate_a, gate_b = split_cols(proj, IN_SIZES)

        o_hg = hgrn2_mix(hq.astype(f32), hf.astype(f32), hi.astype(f32), lbs[l])
        o_hg = (head_rms(o_hg).reshape(B, S, HG_HEADS * HG_DV) * hg_norm_w[l].astype(f32)
                * jax.nn.silu(hg.astype(f32)))

        q = rotary(rq.astype(f32).reshape(B, S, RET_HEADS, RET_DK), pos)
        k = rotary(rk.astype(f32).reshape(B, S, RET_HEADS, RET_DK), pos) * RET_DK ** -0.5
        v = rv.astype(f32).reshape(B, S, RET_HEADS, RET_DV)
        o_ret = retention_mix(q, k, v)
        o_ret = head_rms(o_ret).reshape(B, S, RET_HEADS * RET_DV) * jax.nn.silu(rg.astype(f32))

        y_hg = o_hg.astype(x.dtype) @ w_branch_hg[l]
        y_ret = o_ret.astype(x.dtype) @ w_branch_ret[l]
        merged = jax.nn.sigmoid(gate_a) * y_hg + jax.nn.sigmoid(gate_b) * y_ret
        x = x + merged @ w_out[l]

        h = rmsnorm_2(x, norm_ffn_w[l])
        x = x + peer_ffn(h, peer_w_q[l], peer_sub_keys[l], expert_u[l], expert_v[l])
    return rmsnorm_2(x, final_norm_w)


def setup_inputs(seed=0):
    out = dict(first_inputs(seed))
    for name, value in second_inputs(seed + 1).items():
        if name != "x":
            out[name + "_2"] = value
    return out


def reference(
    x, attn_norm_pre, attn_norm_post, w_in, fox_forget_bias, shift_mu, rwkv_w0, rwkv_w_up,
    rwkv_a0, rwkv_a_up, rwkv_g_up, rwkv_k_k, rwkv_k_a, rwkv_r_k, rwkv_ln_w, rwkv_ln_b, w_out,
    ffn_norm_pre, ffn_norm_post, ffn_w_gate, ffn_w_up, ffn_w_down, norm_mix_w_2, w_in_2,
    hg_lower_bounds_2, hg_norm_w_2, w_branch_hg_2, w_branch_ret_2, w_out_2, norm_ffn_w_2,
    peer_w_q_2, peer_sub_keys_2, expert_u_2, expert_v_2, final_norm_w_2,
):
    x = first_block(
        x, attn_norm_pre, attn_norm_post, w_in, fox_forget_bias, shift_mu, rwkv_w0, rwkv_w_up,
        rwkv_a0, rwkv_a_up, rwkv_g_up, rwkv_k_k, rwkv_k_a, rwkv_r_k, rwkv_ln_w, rwkv_ln_b,
        w_out, ffn_norm_pre, ffn_norm_post, ffn_w_gate, ffn_w_up, ffn_w_down,
    )
    return second_block(
        x, norm_mix_w_2, w_in_2, hg_lower_bounds_2, hg_norm_w_2, w_branch_hg_2, w_branch_ret_2,
        w_out_2, norm_ffn_w_2, peer_w_q_2, peer_sub_keys_2, expert_u_2, expert_v_2,
        final_norm_w_2,
    )


_drawn_inputs = setup_inputs


def setup_inputs(seed=0):
    import zlib

    import numpy as np

    out = dict(_drawn_inputs(seed))
    spreads = {}
    factors = {'rwkv_w_up': 8.0,
     'rwkv_ln_w': 2.92,
     'rwkv_ln_b': 2.941,
     'ffn_norm_post': 3.296,
     'norm_mix_w_2': 3.634,
     'hg_norm_w_2': 22.739,
     'norm_ffn_w_2': 29.352,
     'final_norm_w_2': 7.695}
    for name, (base, spread) in spreads.items():
        noise = np.random.default_rng([zlib.crc32(name.encode()), seed]).standard_normal(out[name].shape)
        drawn = base * np.exp(spread * noise) if base else spread * noise
        out[name] = __import__('jax').numpy.asarray(drawn.astype(out[name].dtype))
    for name, factor in factors.items():
        out[name] = (out[name] * factor).astype(out[name].dtype)
    return out
```

```python
from contextlib import ExitStack

import numpy as np
import concourse.bass as bass
from concourse import mybir

ALU = mybir.AluOpType
ACT = mybir.ActivationFunctionType
AX = mybir.AxisListType
F32 = mybir.dt.float32
U32 = mybir.dt.uint32

P = 128
T = 512
D = 1024
KD = D // P
TT = T // P
C = 64
NCH = T // C
HD = 64
NPAIR = 4
FF = 2816
KF = FF // P
HG_H, HG_D = 8, 128
RET_H, RET_DK, RET_DV = 4, 256, 512
PEER_H, PEER_K, NKEY = 8, 16, 128
TG = 32
NTG = T // TG
JG = 8
NJG = NKEY // JG
RING = 4
NBANK = 4
MID = C // 2 - 1
NEG = -1.0e30
E_HALF = float(np.exp(-0.5))

N_FOX = 13
N_RW = 14
B_FOX = 0
B_RW = B_FOX + N_FOX
B_WOUT = B_RW + N_RW
B_FFN = B_WOUT + KD
B_DOWN = B_FFN + 2 * KF
B_HG = B_DOWN + 3 * KD
B_RET = B_HG + 4 * HG_H
B_MERGE = B_RET + 12 * RET_H
B_WOUT2 = B_MERGE + 5 * KD
B_PQ = B_WOUT2 + KD
B_SUB = B_PQ + 2 * PEER_H
B_EXP = B_SUB + 2
N_BLOCKS = B_EXP + 2 * NKEY
N_LOADED = -(-N_BLOCKS // RING) * RING

PARAMS = [("attn_pre", 8), ("attn_post", 8), ("mu", 15), ("w0", 4), ("a0", 4), ("k_k", 4), ("k_a", 4),
          ("r_k", 4), ("ln_w", 4), ("ln_b", 4), ("ffn_pre", 8), ("ffn_post", 8), ("mix_norm", 8),
          ("lb0", 8), ("lb1", 8), ("hg_norm", 8), ("ffn_norm", 8), ("final_norm", 8), ("f_bias", 1),
          ("eps", 1), ("ln_eps", 1)]
PCOL, NPAR = {}, 0
for _n, _w in PARAMS:
    PCOL[_n] = NPAR
    NPAR += _w

CONSTS = [("ident", 128), ("ones", 128), ("bones", 128), ("bmean", 128), ("strict_T", 128),
          ("strict", 128), ("incl_T", 128), ("neg", 128), ("iota", 128), ("reset", 512), ("one_row", 512)]
CCOL, NCST = {}, 0
for _n, _w in CONSTS:
    CCOL[_n] = (NCST, _w)
    NCST += _w


class Steps:

    def __init__(self, eng, sem):
        self.eng, self.sem, self.n, self.loop = eng, sem, 0, 0

    def go(self, ins):
        self.n += 1
        ins.then_inc(self.sem, 1)

    def sync(self):
        self.eng.wait_ge(self.sem, self.n + self.loop)

    def __call__(self, ins):
        self.go(ins)
        self.sync()

    def enter(self, it, per, count):
        self.loop, self.at, self.per, self.count = it * per, self.n, per, count

    def leave(self):
        assert self.n - self.at == self.per, (self.n - self.at, self.per)
        self.n = self.at + self.per * self.count
        self.loop = 0


def build(nc, xt, par_d, cst_d, sel_d, rot_d, rmask_d, small_d, wstream, gates_d, out):
    with ExitStack() as ctx:
        def sb(name, shape, dt=F32):
            return ctx.enter_context(nc.sbuf_tensor(name, shape, dt))

        def sem(name):
            return ctx.enter_context(nc.semaphore(name))

        NT = 90
        arena = sb("arena", [P, NT, T])
        ring = sb("ring", [P, RING, D])
        par = sb("par", [P, NPAR])
        cst = sb("cst", [P, NCST])
        bank = [ctx.enter_context(nc.psum_tensor(f"bank{b}", [P, 512], F32)) for b in range(8)]
        stat = sb("stat", [P, 96])
        lbt = sb("lbt", [P, 4, 8])
        dch = sb("dch", [P, 6, 4 * NCH])

        def tile(i):
            return arena[:, i, :]

        def cc(name):
            a, w = CCOL[name]
            return cst[:, a:a + w]

        def pp(name, i=0):
            return par[:, PCOL[name] + i:PCOL[name] + i + 1]

        def mask4(name):
            return cc(name).unsqueeze(1).to_broadcast([P, 4, 128])

        def small(a, n, dt=None):
            ap = arena[:, 67:71, :].rearrange("p a b -> p (a b)")[:, a:a + n]
            return ap if dt is None else ap.bitcast(dt)

        topv = small(0, 256).rearrange("p (n k) -> p n k", n=16)
        topi = small(256, 256, U32).rearrange("p (n k) -> p n k", n=16)
        topf = small(512, 256).rearrange("p (n k) -> p n k", n=16)
        bestv = small(768, 128).rearrange("p (h k) -> p h k", h=8)
        besti = small(896, 128, U32).rearrange("p (h k) -> p h k", h=8)
        bests = small(1024, 128, U32).rearrange("p (h k) -> p h k", h=8)
        bestf = small(1152, 256).rearrange("p (s h k) -> p s h k", s=2, h=8)
        pairs = small(1408, 384).rearrange("p (j n) -> p j n", j=3)
        gsum = small(1792, 16).rearrange("p (s h) -> p s h", s=2)
        oneA = arena[:, 71:73, :].rearrange("p u (j n) -> p u j n", j=4)
        oneB = arena[:, 73:75, :].rearrange("p u (j n) -> p u j n", j=4)

        def v4(ap):
            return ap.rearrange("p (g t) -> p g t", g=4)

        def ch(ap):
            return ap.rearrange("p (c t) -> p c t", t=C)

        loaded = [sem(f"loaded{r}") for r in range(RING)]
        block_used = sem("block_used")
        evac = sem("evac")
        in_x, in_par, in_cst, in_small = sem("in_x"), sem("in_par"), sem("in_cst"), sem("in_small")
        in_rot = sem("in_rot")
        act_s, dve_s, pe_s = sem("act_steps"), sem("dve_steps"), sem("pe_steps")
        sq_ready, sum_ready, root_ready = sem("squares_ready"), sem("sums_ready"), sem("root_ready")
        sq_used = sem("squares_used")
        root_used = sem("root_used")
        fc_z, fc_ln = sem("forget_z"), sem("forget_ln")
        cum_ready, exp_ready, hg_exp = sem("decays_cumulated"), sem("decays_exp"), sem("hg_chunk_decays")
        lb_ready = sem("lower_bound")
        tk_sub, tk_exp = sem("route_shifted"), sem("route_exp")
        norm_ready = sem("norm_ready")
        resid_ready = sem("resid_ready")
        shifted = sem("shifted")
        ffn_pair = sem("ffn_pair")
        fc_ready, vt_ready, vt_out = sem("fox_cum_ready"), sem("fox_vt_psum"), sem("fox_v_tokens")
        fs_ready, fmax, fexp, fnorm = sem("fox_scores"), sem("fox_max"), sem("fox_exp"), sem("fox_probs")
        ft_ready, ft_out, fo_ready, fo_out = sem("fox_pT_psum"), sem("fox_pT"), sem("fox_out_psum"), sem("fox_out")
        rw_pe, rw_act, rw_dve = sem("rwkv_products"), sem("rwkv_act"), sem("rwkv_dve")
        hg_pe, hg_act, hg_dve = sem("hg_products"), sem("hg_act"), sem("hg_dve")
        rt_pe, rt_act, rt_dve = sem("ret_products"), sem("ret_act"), sem("ret_dve")
        mg_dve = sem("merged")
        tk_pe, tk_act, tk_dve = sem("route_products"), sem("route_act"), sem("route_dve")
        oh_dve, oh_pe, oh_act = sem("onehots"), sem("gate_psum"), sem("gate_tokens")
        gst = [sem("gates_stored0"), sem("gates_stored1")]
        gld = [sem("gates_loaded0"), sem("gates_loaded1")]
        ex_gelu, ex_prod, ex_acc = sem("gelu"), sem("gated_hidden"), sem("accumulated")
        out_ready, stored = sem("out_ready"), sem("stored")

        X, XN = 0, 8
        X_T = [tile(X + k) for k in range(KD)]
        XN_T = [tile(XN + k) for k in range(KD)]
        Q0, K0, VF0, VT0 = 16, 20, 24, 28
        RR, RK, RV, LAT, GL, GFT, RAW = 32, 36, 40, 44, 45, 46, 47
        DTMP = 49
        RA, LW, RG, KKT, BON, OF = 50, 54, 58, 62, 66, 70
        TA, TR, TB, TK = 8, 12, 16, 20
        MA, MB, MK, MV = 24, 28, 32, 36
        WT, U0, UU, SH = 40, 44, 54, 50
        HS = [[62, 63, 64, 65, 74, 75, 76, 77], [78, 79, 80, 81, 82, 83, 84, 85]]
        ORW = 66
        SMALL = 87
        SELT = 80
        PT0 = 74
        PR0 = 78
        NT1, RSQ = 84, 86
        MO, YY = 52, 24
        HGT = dict(F=40, LF=41, K=42, CU=43, CC=44, EP=45, EM=46, I=47, G=48, Q=49, KD=50, QD=51, IT=52, KT=53,
                   AM=54, SQ=55, RT=56, R2=57, X=58, S=lambda c: tile(59 + c // 4)[:, (c % 4) * P:(c % 4 + 1) * P])
        OHG, ORET = 16, 24
        RTT = dict(Q=40, K=42, VF=44, QR=48, KR=50, VT=52, AM=56, O=60, SQ=64, RT=65, R2=66, G=67, T=71, COS=75, MASK=77)
        PST, PBIG, PTT, GBUF = 40, 56, 64, 24
        EXT = dict(W=40, GW=56, TMP=72, ACC=16)
        RW_PE, RW_ACT, RW_DVE = 28, 16, 12
        FT = 47

        block = ctx.enter_context(nc.Block())

        @block.sync
        def _(sp):
            for r in range(RING):
                sp.dma_start(ring[:, r, :], wstream[r]).then_inc(loaded[r], 16)
            with sp.Fori(1, N_LOADED // RING) as i:
                for r in range(RING):
                    sp.wait_ge(block_used, i * RING + (r + 1 - RING))
                    sp.dma_start(ring[:, r, :], wstream[bass.ds(i * RING + r, 1)].rearrange("a p n -> (a p) n")
                                 ).then_inc(loaded[r], 16)
            sp.wait_ge(out_ready, KD)
            sp.dma_start(out.rearrange("(k p) t -> p k t", p=P), arena[:, XN:XN + KD, :]).then_inc(stored, 16)
            sp.wait_ge(stored, 16)

        @block.tensor
        def _(pe):
            st = Steps(pe, pe_s)
            q_at = [0]

            def ready(n, it=0, per=0):
                pe.wait_ge(loaded[n % RING], it * (16 * per // RING) + 16 * (n // RING + 1))

            def w(n, k):
                return ring[:, n % RING, k * P:(k + 1) * P]

            def product(q, blocks, rhs, it=0, per_q=0, per_n=0):
                if q >= NBANK:
                    pe.wait_ge(evac, it * per_q + q - NBANK + 1)
                k = 0
                total = sum(c for _, c in blocks)
                for n, c in blocks:
                    ready(n, it, per_n)
                    for j in range(c):
                        mm = pe.matmul(bank[q % NBANK][:, :], w(n, j), rhs[k], start=(k == 0), stop=(k == total - 1))
                        k += 1
                    mm.then_inc(block_used, 1)

            def norm_sums(i, parts, mat="ones"):
                for k in range(parts):
                    pe.wait_ge(sq_ready, KD * i + k + 1)
                    mm = pe.matmul(bank[4][:, :], cc(mat), tile(NT1 + k % 2), start=(k == 0), stop=(k == parts - 1))
                    if k < parts - 1:
                        mm.then_inc(sq_used, 1)
                mm.then_inc(sum_ready, 1)

            pe.wait_ge(in_cst, 16)
            norm_sums(0, KD)
            pe.wait_ge(norm_ready, KD)
            for n in range(N_FOX + N_RW):
                product(n, [(n, KD)], XN_T)
            q = N_FOX + N_RW

            for s in range(TT):
                pe.wait_ge(evac, 12)
                for m in range(NPAIR):
                    tr = pe.transpose(bank[4 + s][:, m * P:(m + 1) * P], tile(VF0 + m)[:, s * P:(s + 1) * P], cc("ident"))
                tr.then_inc(vt_ready, 1)
            units = [(h, t) for h in range(8) for t in range(TT)]

            def fox_scores(u):
                h, t = units[u]
                m, e = h // 2, h % 2
                n = (t + 1) * P
                b = bank[u % 2]
                if u == 0:
                    pe.wait_ge(evac, q)
                    pe.wait_ge(fc_ready, 1)
                    pe.wait_ge(in_small, 32)
                if u >= 2:
                    pe.wait_ge(fexp, u - 1)
                    pe.wait_ge(fmax, u - 1)
                rows = slice(e * HD, (e + 1) * HD)
                pe.matmul(b[:, 0:n], tile(Q0 + m)[rows, t * P:(t + 1) * P], tile(K0 + m)[rows, 0:n],
                          start=True, stop=False, skip_group_check=True)
                pe.matmul(b[:, 0:n], arena[32:40, SELT:SELT + 2, :].rearrange("p a b -> p (a b)")[:, h * P:(h + 1) * P],
                          tile(GFT)[32:40, 0:n], start=False, stop=False, skip_group_check=True)
                pe.matmul(b[:, t * P:n], cc("ident"), cc("neg"), start=False, stop=True,
                          skip_group_check=True).then_inc(fs_ready, 1)

            def fox_out(u):
                h, t = units[u]
                m, e = h // 2, h % 2
                bt, bo = bank[2 + u % 2], bank[4 + m % 2]
                pe.wait_ge(fnorm, u + 1)
                if u >= 2:
                    pe.wait_ge(ft_out, u - 1)
                for s in range(t + 1):
                    tr = pe.transpose(bt[:, s * P:(s + 1) * P], tile(PR0 + u % 2)[:, s * P:(s + 1) * P], cc("ident"))
                tr.then_inc(ft_ready, 1)
                pe.wait_ge(ft_out, u + 1)
                if u == 0:
                    pe.wait_ge(vt_out, TT)
                if e == 0 and t == 0 and m >= 2:
                    pe.wait_ge(fo_out, m - 1)
                for s in range(t + 1):
                    mm = pe.matmul(bo[e * HD:(e + 1) * HD, t * P:(t + 1) * P], tile(VT0 + s)[:, h * HD:(h + 1) * HD],
                                   tile(PT0 + u % 2)[:, s * P:(s + 1) * P], start=(s == 0), stop=(s == t),
                                   skip_group_check=True)
                mm.then_inc(fo_ready, 1)

            fox_scores(0)
            for u in range(len(units)):
                if u + 1 < len(units):
                    fox_scores(u + 1)
                fox_out(u)

            su = arena[:, SMALL:SMALL + 3, :]
            pe.wait_ge(in_small, 32)
            pe.wait_ge(fo_out, NPAIR)
            pe.wait_ge(rw_act, 3)
            for m in range(NPAIR):
                cols = slice(m * P, (m + 1) * P)
                if m >= 1:
                    pe.wait_ge(rw_act, 3 + 3 * m)
                pe.matmul(bank[0][:, :], su[0:64, 0, cols], tile(LAT)[0:64, :], start=True, stop=True).then_inc(rw_pe, 1)
                pe.matmul(bank[1][:, :], su[64:128, 0, cols], tile(LAT)[64:128, :], start=True, stop=True).then_inc(rw_pe, 1)
                pe.matmul(bank[2][:, :], su[:, 1, cols], tile(GL), start=True, stop=False)
                pe.matmul(bank[2][:, :], su[0:32, 2, cols], tile(GFT)[0:32, :], start=False, stop=True).then_inc(rw_pe, 1)
            for m in range(NPAIR):
                pe.wait_ge(rw_act, 16 + 2 * m)
                pe.matmul(bank[4][:, :], cc("bones"), tile(DTMP), start=True, stop=True).then_inc(rw_pe, 1)
                pe.wait_ge(rw_dve, 2 * m + 1)
                pe.matmul(bank[5][:, :], cc("bones"), tile(RAW), start=True, stop=True).then_inc(rw_pe, 1)
            pe.wait_ge(rw_dve, 8)
            for i, (src, _) in enumerate(((TA, MA), (TB, MB), (TK, MK), (RV, MV))):
                for m in range(NPAIR):
                    j = 4 * i + m
                    if j >= 2:
                        pe.wait_ge(rw_act, 23 + j - 1)
                    for g in range(TT):
                        tr = pe.transpose(bank[j % 2][:, g * P:(g + 1) * P], tile(src + m)[:, g * P:(g + 1) * P], cc("ident"))
                    tr.then_inc(rw_pe, 1)
            for m in range(NPAIR):
                for e in range(2):
                    rows = slice(e * HD, (e + 1) * HD)
                    if m == 0:
                        pe.wait_ge(rw_act, 39)
                    else:
                        pe.wait_ge(rw_act, 39 + RW_ACT * m)
                        pe.wait_ge(rw_dve, 8 + RW_DVE * m)
                    b0 = 3 * e
                    for k, (l, r) in enumerate(((TA, TB), (TB, TA), (TK, TA))):
                        for g in range(TT):
                            cols = slice(g * P, (g + 1) * P)
                            mm = pe.matmul(bank[b0 + k][:, cols], tile(l + m)[rows, cols], tile(r + m)[rows, cols],
                                           start=True, stop=True, skip_group_check=True)
                    mm.then_inc(rw_pe, 1)
                for lev in range(5):
                    for e in range(2):
                        hs, b0 = HS[e], 3 * e
                        a, b = (0, 1) if lev % 2 == 0 else (1, 0)
                        pe.wait_ge(rw_dve, 8 + RW_DVE * m + 2 * lev + e + 1)
                        for g in range(TT):
                            cols = slice(g * P, (g + 1) * P)
                            pe.matmul(bank[b0][:, cols], tile(hs[2 + a])[:, cols], tile(hs[a])[:, cols],
                                      start=True, stop=True, skip_group_check=True)
                            mm = pe.matmul(bank[b0 + 1][:, cols], tile(hs[a])[:, cols], tile(hs[2 + a])[:, cols],
                                           start=True, stop=True, skip_group_check=True)
                        mm.then_inc(rw_pe, 1)
                    for e in range(2):
                        hs, b0 = HS[e], 3 * e
                        a, b = (0, 1) if lev % 2 == 0 else (1, 0)
                        pe.wait_ge(rw_act, 39 + RW_ACT * m + 2 * lev + e + 1)
                        for g in range(TT):
                            cols = slice(g * P, (g + 1) * P)
                            mm = pe.matmul(bank[b0 + 2][:, cols], tile(hs[b])[:, cols], tile(hs[4 + a])[:, cols],
                                           start=True, stop=True, skip_group_check=True)
                        mm.then_inc(rw_pe, 1)
                for e in range(2):
                    hs, b0 = HS[e], 3 * e
                    cols_h = slice(e * HD, (e + 1) * HD)
                    pe.wait_ge(rw_dve, 8 + RW_DVE * m + 10 + e + 1)
                    for g in range(TT):
                        mm = pe.matmul(bank[b0][:, g * HD:(g + 1) * HD], tile(hs[6])[:, g * P:(g + 1) * P],
                                       v4(tile(MV + m))[:, g, cols_h], start=True, stop=True, skip_group_check=True)
                    mm.then_inc(rw_pe, 1)
                    for g in range(TT):
                        mm = pe.matmul(bank[b0 + 1][e * HD:(e + 1) * HD, g * P:(g + 1) * P], v4(tile(MA + m))[:, g, cols_h],
                                       tile(hs[5])[:, g * P:(g + 1) * P], start=True, stop=True, skip_group_check=True)
                    mm.then_inc(rw_pe, 1)
                for e in range(2):
                    hs, b0 = HS[e], 3 * e
                    pe.wait_ge(rw_act, 39 + RW_ACT * m + 10 + 2 * e + 1)
                    for g in range(TT):
                        mm = pe.matmul(bank[b0 + 2][:, g * HD:(g + 1) * HD], tile(hs[5])[:, g * P:(g + 1) * P],
                                       tile(hs[7])[:, g * HD:(g + 1) * HD], start=True, stop=True, skip_group_check=True)
                    mm.then_inc(rw_pe, 1)
            base_pe, base_act, base_dve = 36 + RW_PE * 4, 39 + RW_ACT * 4, 8 + RW_DVE * 4
            shv = arena[:, SH:SH + 4, :].rearrange("p a b -> p (a b)").rearrange("p (c n) -> p c n", c=NCH)
            for c in range(NCH):
                g, p = c // 2, c % 2
                trow = slice(p * HD, (p + 1) * HD)
                if c == 0:
                    pe.wait_ge(rw_act, base_act)
                    pe.wait_ge(rw_dve, base_dve)
                if c > 0:
                    pe.wait_ge(rw_dve, base_dve + 2 * c)
                    for h in range(8):
                        m, e = h // 2, h % 2
                        rows = slice(e * HD, (e + 1) * HD)
                        mm = pe.matmul(bank[6 - e][trow, m * HD:(m + 1) * HD], tile(WT + m)[rows, c * C:(c + 1) * C],
                                       shv[rows, c, m * HD:(m + 1) * HD], start=True, stop=True, skip_group_check=True)
                    mm.then_inc(rw_pe, 1)
                if c == NCH - 1:
                    continue
                pe.wait_ge(rw_dve, base_dve + 2 * c + 1)
                for h in range(8):
                    m, e = h // 2, h % 2
                    rows = slice(e * HD, (e + 1) * HD)
                    dst = bank[7][rows, m * HD:(m + 1) * HD]
                    pe.matmul(dst, v4(tile(MK + m))[trow, g, rows], v4(tile(MV + m))[trow, g, rows],
                              start=True, stop=False, skip_group_check=True)
                    mm = pe.matmul(dst, v4(tile(MB + m))[trow, g, rows], tile(UU + g)[trow, h * HD:(h + 1) * HD],
                                   start=False, stop=True, skip_group_check=True)
                mm.then_inc(rw_pe, 1)
            bp, bd, ba = base_pe + 14, base_dve + 15, base_act
            pe.wait_ge(rw_dve, bd)
            for h in range(8):
                m, e = h // 2, h % 2
                rows = slice(e * HD, (e + 1) * HD)
                if h >= 1:
                    pe.wait_ge(rw_dve, bd + 2 * h)
                for k, l in enumerate((TK, TB)):
                    for g in range(TT):
                        cols = slice(g * P, (g + 1) * P)
                        mm = pe.matmul(bank[k][:, cols], tile(l + m)[rows, cols], tile(TR + m)[rows, cols],
                                       start=True, stop=True, skip_group_check=True)
                    mm.then_inc(rw_pe, 1)
                pe.wait_ge(rw_dve, bd + 2 * h + 2)
                hs = HS[h % 2]
                yb = bank[4 + m % 2]
                if e == 0 and m >= 2:
                    pe.wait_ge(rw_act, ba + m - 1)
                for g in range(TT):
                    cols = slice(g * P, (g + 1) * P)
                    pe.matmul(yb[rows, cols], v4(tile(MV + m))[:, g, rows], tile(hs[0])[:, cols],
                              start=True, stop=False, skip_group_check=True)
                    mm = pe.matmul(yb[rows, cols], tile(UU + g)[:, h * HD:(h + 1) * HD], tile(hs[1])[:, cols],
                                   start=False, stop=False, skip_group_check=True)
                    for c in (2 * g, 2 * g + 1):
                        if c:
                            mm = pe.matmul(yb[rows, c * C:(c + 1) * C], shv[rows, c, m * HD:(m + 1) * HD],
                                           tile(TR + m)[rows, c * C:(c + 1) * C], start=False, stop=(c % 2 == 1),
                                           skip_group_check=True)
                mm.then_inc(rw_pe, 1)
            bp, bd = bp + 24, bd + 16
            ba += 4
            for m in range(NPAIR):
                pe.wait_ge(rw_act, ba + 2 * m)
                if m:
                    pe.wait_ge(rw_dve, bd + 2 * m)
                pe.matmul(bank[0][:, :], cc("bmean"), tile(YY + m), start=True, stop=True).then_inc(rw_pe, 1)
                pe.wait_ge(rw_act, ba + 2 * m + 1)
                pe.matmul(bank[1][:, :], cc("bmean"), tile(HS[0][0]), start=True, stop=True).then_inc(rw_pe, 1)
            bp, bd, ba = bp + 8, bd + 8, ba + 8

            pe.wait_ge(rw_dve, bd)
            mixed = [tile(OF + k) for k in range(4)] + [tile(ORW + k) for k in range(4)]
            for k in range(KD):
                product(q, [(B_WOUT + k, KD)], mixed)
                q += 1
            norm_sums(1, KD)
            norm_sums(2, KD)
            pe.wait_ge(norm_ready, 2 * KD)
            with pe.Fori(0, KF // 2) as i:
                for j in range(4):
                    product(q + j, [(B_FFN + j, KD)], XN_T, i, 4, 4)
            q += 2 * KF
            pe.wait_ge(ffn_pair, KF + 2)
            hid = [tile(16 + k) for k in range(KF)]
            for k in range(KD):
                n = B_DOWN + 3 * k
                product(q, [(n, 8), (n + 1, 8), (n + 2, KF - 16)], hid)
                q += 1
            norm_sums(3, KD)
            norm_sums(4, KD)

            pe.wait_ge(norm_ready, 3 * KD)
            H_ = HGT
            with pe.Fori(0, HG_H) as h:
                for j in range(4):
                    product(q + j, [(B_HG + j, KD)], XN_T, h, 4, 4)
                pe.wait_ge(evac, h * 4 + q + 2)
                for g in range(TT):
                    tr = pe.transpose(bank[4][:, g * P:(g + 1) * P], tile(H_["I"])[:, g * P:(g + 1) * P], cc("ident"))
                tr.then_inc(hg_pe, 1)
                pe.wait_ge(hg_dve, h * 6 + 4)
                for g in range(TT):
                    tr = pe.transpose(bank[5][:, g * P:(g + 1) * P], tile(H_["KD"])[:, g * P:(g + 1) * P], cc("ident"))
                tr.then_inc(hg_pe, 1)
                for g in range(TT):
                    cols = slice(g * P, (g + 1) * P)
                    mm = pe.matmul(bank[6][:, cols], tile(H_["KD"])[:, cols], tile(H_["QD"])[:, cols],
                                   start=True, stop=True, skip_group_check=True)
                mm.then_inc(hg_pe, 1)
                pe.wait_ge(hg_act, h * 6 + 4)
                for c in range(NCH - 1):
                    rows = slice((c % 2) * C, (c % 2 + 1) * C)
                    mm = pe.matmul(bank[4 + c % 2][:, (c // 2) * P:(c // 2 + 1) * P], v4(tile(H_["KT"]))[rows, c // 2, :],
                                   v4(tile(H_["IT"]))[rows, c // 2, :], start=True, stop=True, skip_group_check=True)
                mm.then_inc(hg_pe, 1)
                pe.wait_ge(hg_dve, h * 6 + 6)
                for g in range(TT):
                    cols = slice(g * P, (g + 1) * P)
                    pe.matmul(bank[7][:, cols], v4(tile(H_["IT"]))[:, g, :], tile(H_["AM"])[:, cols],
                              start=True, stop=False, skip_group_check=True)
                    for c in (2 * g, 2 * g + 1):
                        if c:
                            mm = pe.matmul(bank[7][:, c * C:(c + 1) * C], H_["S"](c), tile(H_["QD"])[:, c * C:(c + 1) * C],
                                           start=False, stop=(c % 2 == 1), skip_group_check=True)
                mm.then_inc(hg_pe, 1)
                pe.wait_ge(hg_act, h * 6 + 5)
                pe.matmul(bank[6][:, :], cc("ones"), tile(H_["SQ"]), start=True, stop=True).then_inc(hg_pe, 1)
            q += 4 * HG_H
            R_ = RTT
            with pe.Fori(0, RET_H) as h:
                for j in range(8):
                    product(q + j, [(B_RET + j, KD)], XN_T, h, 12, 12)
                for s in range(TT):
                    pe.wait_ge(evac, h * 12 + q + 8)
                    if s >= 1:
                        pe.wait_ge(rt_act, h * 9 + s)
                    for j in range(4):
                        tr = pe.transpose(bank[4][:, j * P:(j + 1) * P], tile(R_["VF"] + j)[:, s * P:(s + 1) * P], cc("ident"))
                    tr.then_inc(rt_pe, 1)
                for s in range(TT):
                    if s == 0:
                        pe.wait_ge(rt_dve, h * 12 + 1 + 4)
                    if s >= 2:
                        pe.wait_ge(rt_dve, h * 12 + 1 + 4 + s - 1)
                    b = bank[5 + s % 2]
                    n = T - s * P
                    for j in range(2):
                        mm = pe.matmul(b[:, 0:n], tile(R_["KR"] + j)[:, s * P:(s + 1) * P], tile(R_["QR"] + j)[:, s * P:T],
                                       start=(j == 0), stop=(j == 1))
                    mm.then_inc(rt_pe, 1)
                for j in range(4):
                    if j == 0:
                        pe.wait_ge(rt_dve, h * 12 + 1 + 8)
                        pe.wait_ge(rt_act, h * 9 + 4)
                    if j >= 1:
                        pe.wait_ge(rt_act, h * 9 + 4 + j)
                    for t in range(TT):
                        for s in range(t + 1):
                            mm = pe.matmul(bank[7][:, t * P:(t + 1) * P], tile(R_["VT"] + s)[:, j * P:(j + 1) * P],
                                           tile(R_["AM"] + s)[:, (t - s) * P:(t - s + 1) * P], start=(s == 0), stop=(s == t),
                                           skip_group_check=True)
                    mm.then_inc(rt_pe, 1)
                    pe.wait_ge(rt_act, h * 9 + 5 + j)
                    pe.matmul(bank[4][:, :], cc("ones"), tile(R_["SQ"]), start=(j == 0), stop=(j == 3)).then_inc(rt_pe, 1)
                for j in range(8, 12):
                    product(q + j, [(B_RET + j, KD)], XN_T, h, 12, 12)
            q += 12 * RET_H
            pe.wait_ge(hg_dve, 6 * HG_H + 1)
            pe.wait_ge(rt_dve, 12 * RET_H + 1)
            ohg = [tile(16 + k) for k in range(8)]
            oret = [tile(24 + k) for k in range(16)]
            for k in range(KD):
                n = B_MERGE + 5 * k
                product(q, [(n, KD)], XN_T)
                product(q + 1, [(n + 1, KD)], XN_T)
                product(q + 2, [(n + 2, KD)], ohg)
                product(q + 3, [(n + 3, KD), (n + 4, KD)], oret)
                q += 4
            pe.wait_ge(mg_dve, KD)
            merged = [tile(40 + k) for k in range(8)]
            for k in range(KD):
                product(q, [(B_WOUT2 + k, KD)], merged)
                q += 1
            norm_sums(5, KD)
            pe.wait_ge(norm_ready, 4 * KD)
            for k in range(2 * PEER_H):
                product(q, [(B_PQ + k, KD)], XN_T)
                q += 1
            pe.wait_ge(evac, q)
            for t in range(TT):
                if t >= 1:
                    pe.wait_ge(tk_act, 4 * t)
                for n in range(16):
                    if t == 0 and n % 8 == 0:
                        ready(B_SUB + n // 8)
                    mm = pe.matmul(bank[n // 4][:, (n % 4) * P:(n % 4 + 1) * P], tile(24 + n)[:, t * P:(t + 1) * P],
                                   ring[:, (B_SUB + n // 8) % RING, (n % 8) * P:(n % 8 + 1) * P],
                                   start=True, stop=True, skip_group_check=True)
                    if n % 4 == 3:
                        mm.then_inc(tk_pe, 1)
            for t in range(TT):
                pe.wait_ge(tk_dve, t + 1)
                if t >= 1:
                    pe.wait_ge(tk_act, 16 + t)
                for j in range(3):
                    tr = pe.transpose(bank[4][:, j * P:(j + 1) * P], pairs[:, j, :], cc("ident"))
                    if t == 0 and j < 2:
                        tr.then_inc(block_used, 1)
                tr.then_inc(tk_pe, 1)
            with pe.Fori(0, NTG // 2) as i:
                for u in range(2 * TG // 4):
                    pe.wait_ge(oh_dve, i * 16 + u + 1)
                    pe.wait_ge(oh_act, i * 16 + u + 1)
                    for j in range(4):
                        mm = pe.matmul(bank[5 + u % 2][:, j * P:(j + 1) * P], oneA[:, u % 2, j, :], oneB[:, u % 2, j, :],
                                       start=True, stop=True, skip_group_check=True)
                    mm.then_inc(oh_pe, 1)
            def u_block(g, j, n, it=0):
                k = g * JG + j
                if g * JG + j >= 2:
                    pe.wait_ge(ex_gelu, it * 2 * JG + k - 1)
                ready(n, it, 32)
                for kk in range(KD):
                    mm = pe.matmul(bank[j % 2][:, :], w(n, kk), XN_T[kk], start=(kk == 0), stop=(kk == KD - 1))
                mm.then_inc(block_used, 1)

            def v_half(g, half, n, it=0):
                k = 2 * g + half
                if k >= 1:
                    pe.wait_ge(ex_acc, it * 16 + 4 * k)
                for b in range(4):
                    ready(n + b, it, 32)
                    for jj in range(2):
                        j = 2 * b + jj
                        if half == 0:
                            pe.wait_ge(ex_prod, it * 2 * JG + g * JG + j + 1)
                        for d in range(4):
                            mm = pe.matmul(bank[2 + d][:, :], w(n + b, jj * 4 + d), tile(EXT["GW"] + (g % 2) * JG + j),
                                           start=(j == 0), stop=(j == JG - 1), skip_group_check=True)
                    mm.then_inc(block_used, 1)

            pe.wait_ge(oh_act, 8 * NTG + 2)
            n = B_EXP
            for j in range(JG):
                u_block(0, j, n + j)
            n += JG

            def group(g, n, last=False, it=0):
                v_half(g, 0, n, it)
                n += 4
                if not last:
                    for j in range(4):
                        u_block(g + 1, j, n + j, it)
                    n += 4
                v_half(g, 1, n, it)
                n += 4
                if not last:
                    for j in range(4, 8):
                        u_block(g + 1, j, n + j - 4, it)
                    n += 4
                return n

            n = group(0, n)
            n = group(1, n)
            with pe.Fori(0, (NJG - 4) // 2) as i:
                group(2, n, it=i)
                group(3, n + 16, it=i)
            n += 32 * ((NJG - 4) // 2)
            n = group(NJG - 2, n)
            n = group(NJG - 1, n, last=True)
            assert n == N_BLOCKS
            norm_sums(6, KD)
            for r in range(N_LOADED - N_BLOCKS):
                ready(N_BLOCKS + r)

        @block.scalar
        def _(act):
            st = Steps(act, act_s)
            nc_ = act

            def A(out_, in_, f, **kw):
                return act.activation(out_, in_, f, **kw)

            act.dma_start(arena[:, X:X + KD, :], xt.rearrange("(k p) t -> p k t", p=P)).then_inc(in_x, 16)
            act.dma_start(par[:, :], par_d).then_inc(in_par, 16)
            act.dma_start(cst[:, :], cst_d).then_inc(in_cst, 16)
            act.dma_start(arena[:, SMALL:SMALL + 3, :], small_d).then_inc(in_small, 16)
            act.dma_start(arena[32:40, SELT:SELT + 2, :].rearrange("p a b -> p (a b)"), sel_d).then_inc(in_small, 16)
            act.wait_ge(in_par, 16)

            def norm_squares(i, src, first_wait):
                for k in range(KD):
                    first_wait(k)
                    if k >= 2:
                        act.wait_ge(sq_used, (KD - 1) * i + k - 1)
                    elif i:
                        act.wait_ge(root_used, i)
                    A(tile(NT1 + k % 2), src(k), ACT.Square).then_inc(sq_ready, 1)
                act.wait_ge(sum_ready, i + 1)
                A(tile(NT1), bank[4][:, :], ACT.Sqrt, scale=1.0 / D, bias=pp("eps")).then_inc(root_ready, 1)

            act.wait_ge(in_x, 16)
            norm_squares(0, lambda k: tile(X + k), lambda k: None)
            for n in range(N_FOX + N_RW):
                act.wait_ge(block_used, n + 1)
                if n < 12:
                    dst = tile((Q0, K0, VF0)[n // 4] + n % 4)
                else:
                    if n >= 14:
                        act.wait_ge(shifted, n - 13)
                    dst = tile(RAW + n % 2)
                A(dst, bank[n % NBANK][:, :], ACT.Copy).then_inc(evac, 1)
                if n == 12:
                    act.wait_ge(shifted, 1)
                    act.wait_ge(fc_z, 1)
                    z = arena[32:40, BON + 1, :]
                    st(A(z, z, ACT.Exp, scale=-1.0))
                    A(z, z, ACT.Ln, bias=1.0).then_inc(fc_ln, 1)
            q = N_FOX + N_RW
            act.wait_ge(shifted, N_RW + 1)
            A(tile(LAT)[0:64, :], tile(LAT)[0:64, :], ACT.Tanh).then_inc(rw_act, 1)
            A(tile(GL), tile(GL), ACT.Sigmoid).then_inc(rw_act, 1)
            A(tile(GFT)[0:32, :], tile(GFT)[0:32, :], ACT.Sigmoid).then_inc(rw_act, 1)
            for s in range(TT):
                act.wait_ge(vt_ready, s + 1)
                A(tile(VT0 + s), bank[4 + s][:, :], ACT.Copy).then_inc(vt_out, 1)

            units = [(h, t) for h in range(8) for t in range(TT)]

            def fox_exp(u):
                h, t = units[u]
                n = (t + 1) * P
                act.wait_ge(fmax, u + 1)
                if u >= 2:
                    act.wait_ge(ft_ready, u - 1)
                A(tile(PR0 + u % 2)[:, 0:n], bank[u % 2][:, 0:n], ACT.Exp, scale=0.125, bias=stat[:, 32 + u:33 + u],
                  accum_out=stat[:, 64 + u % 32:65 + u % 32]).then_inc(fexp, 1)

            def fox_copy(u):
                h, t = units[u]
                n = (t + 1) * P
                act.wait_ge(ft_ready, u + 1)
                if u >= 2:
                    act.wait_ge(fo_ready, u - 1)
                A(tile(PT0 + u % 2)[:, 0:n], bank[2 + u % 2][:, 0:n], ACT.Copy).then_inc(ft_out, 1)
                if h % 2 == 1 and t == TT - 1:
                    act.wait_ge(fo_ready, u + 1)
                    m = h // 2
                    A(tile(OF + m), bank[4 + m % 2][:, :], ACT.Copy).then_inc(fo_out, 1)

            fox_exp(0)
            for u in range(len(units)):
                if u + 1 < len(units):
                    fox_exp(u + 1)
                fox_copy(u)

            for m in range(NPAIR):
                act.wait_ge(rw_pe, 3 * m + 1)
                A(tile(LW + m), bank[0][:, :], ACT.Sigmoid, bias=pp("w0", m)).then_inc(rw_act, 1)
                act.wait_ge(rw_pe, 3 * m + 2)
                A(tile(RA + m), bank[1][:, :], ACT.Sigmoid, bias=pp("a0", m)).then_inc(rw_act, 1)
                act.wait_ge(rw_pe, 3 * m + 3)
                A(tile(RG + m), bank[2][:, :], ACT.Copy).then_inc(rw_act, 1)
            for m in range(NPAIR):
                if m:
                    act.wait_ge(rw_dve, 2 * m)
                A(tile(DTMP), tile(RK + m), ACT.Square, scale=pp("k_k", m)).then_inc(rw_act, 1)
                act.wait_ge(rw_pe, 12 + 2 * m + 1)
                A(tile(74), bank[4][:, :], ACT.Sqrt).then_inc(rw_act, 1)
                act.wait_ge(cum_ready, m + 1)
                st.go(A(tile(78), tile(75), ACT.Exp))
                st.go(A(tile(79), tile(75), ACT.Exp, scale=-1.0))
                st.go(A(tile(80), tile(76), ACT.Exp))
                A(dch[:, 0, m * NCH:(m + 1) * NCH], ch(tile(77))[:, :, MID], ACT.Exp).then_inc(exp_ready, 1)
            for i, dst in enumerate((MA, MB, MK, MV)):
                for m in range(NPAIR):
                    act.wait_ge(rw_pe, 20 + 4 * i + m + 1)
                    A(tile(dst + m), bank[(4 * i + m) % 2][:, :], ACT.Copy).then_inc(rw_act, 1)
            for m in range(NPAIR):
                pb = 36 + RW_PE * m
                for lev in range(5):
                    for e in range(2):
                        hs, b0 = HS[e], 3 * e
                        b = 1 if lev % 2 == 0 else 0
                        act.wait_ge(rw_pe, pb + 2 + 4 * lev + e + 1)
                        A(tile(hs[b]), bank[b0][:, :], ACT.Copy).then_inc(rw_act, 1)
                for e in range(2):
                    hs, b0 = HS[e], 3 * e
                    act.wait_ge(rw_pe, pb + 22 + 2 * e + 1)
                    A(tile(hs[7])[:, 0:256], bank[b0][:, 0:256], ACT.Copy).then_inc(rw_act, 1)
                    act.wait_ge(rw_pe, pb + 22 + 2 * e + 2)
                    A(tile(WT + m)[e * HD:(e + 1) * HD, :], bank[b0 + 1][e * HD:(e + 1) * HD, :], ACT.Copy).then_inc(rw_act, 1)
                for e in range(2):
                    b0 = 3 * e
                    h = 2 * m + e
                    act.wait_ge(rw_pe, pb + 26 + e + 1)
                    A(arena[:, U0:U0 + 4, h * HD:(h + 1) * HD], bank[b0 + 2][:, 0:256].rearrange("p (g i) -> p g i", g=4),
                      ACT.Copy).then_inc(rw_act, 1)
            bp = 36 + RW_PE * 4 + 14
            ba = 39 + RW_ACT * 4
            for m in range(NPAIR):
                act.wait_ge(rw_pe, bp + 6 * m + 6)
                A(tile(YY + m), bank[4 + m % 2][:, :], ACT.Copy).then_inc(rw_act, 1)
            bp += 24
            ba += 4
            bd = 8 + RW_DVE * 4 + 15 + 16
            for m in range(NPAIR):
                act.wait_ge(rw_dve, bd + 2 * m + 1)
                A(tile(HS[0][0]), tile(HS[0][1]), ACT.Square).then_inc(rw_act, 1)
                act.wait_ge(rw_pe, bp + 2 * m + 2)
                A(tile(HS[0][2]), bank[1][:, :], ACT.Sqrt, bias=pp("ln_eps")).then_inc(rw_act, 1)

            for k in range(KD):
                act.wait_ge(block_used, B_WOUT + k + 1)
                A(tile(MO + k), bank[q % NBANK][:, :], ACT.Copy).then_inc(evac, 1)
                q += 1
            norm_squares(1, lambda k: tile(MO + k), lambda k: act.wait_ge(evac, q))
            norm_squares(2, lambda k: tile(X + k), lambda k: act.wait_ge(resid_ready, k + 1))
            with act.Fori(0, KF // 2) as i:
                for j in range(4):
                    act.wait_ge(block_used, i * 4 + B_FFN + j + 1)
                    act.wait_ge(ffn_pair, i * 2 + j // 2 + 1)
                    A(tile(48 + j), bank[(q + j) % NBANK][:, :], ACT.Silu if j % 2 == 0 else ACT.Copy).then_inc(evac, 1)
            q += 2 * KF
            act.wait_ge(ffn_pair, KF + 2)
            for k in range(KD):
                act.wait_ge(block_used, B_DOWN + 3 * (k + 1))
                A(tile(MO + k), bank[q % NBANK][:, :], ACT.Copy).then_inc(evac, 1)
                q += 1
            norm_squares(3, lambda k: tile(MO + k), lambda k: act.wait_ge(evac, q))
            norm_squares(4, lambda k: tile(X + k), lambda k: act.wait_ge(resid_ready, KD + k + 1))

            H_ = HGT
            act.dma_start(arena[:, RTT["COS"]:RTT["COS"] + 2, :], rot_d).then_inc(in_rot, 16)
            act.dma_start(arena[:, RTT["MASK"]:RTT["MASK"] + 4, :], rmask_d).then_inc(in_rot, 16)
            act.wait_ge(lb_ready, 1)
            A(lbt[:, 1:3, :], lbt[:, 1:3, :], ACT.Exp).then_inc(lb_ready, 1)
            with act.Fori(0, HG_H) as h:
                for j, (dst, f) in enumerate((("F", ACT.Sigmoid), ("I", ACT.Copy), ("G", ACT.Silu), ("Q", ACT.Copy))):
                    act.wait_ge(block_used, h * 4 + B_HG + j + 1)
                    act.wait_ge(hg_dve, h * 6 + 1)
                    A(tile(H_[dst]), bank[(q + j) % NBANK][:, :], f).then_inc(evac, 1)
                    if j == 1:
                        act.wait_ge(hg_dve, h * 6 + 2)
                        A(tile(H_["LF"]), tile(H_["F"]), ACT.Ln).then_inc(hg_act, 1)
                act.wait_ge(hg_dve, h * 6 + 3)
                A(dch[:, 4, 0:NCH], ch(tile(H_["CU"]))[:, :, MID], ACT.Exp).then_inc(hg_exp, 1)
                A(tile(H_["EP"]), tile(H_["CC"]), ACT.Exp).then_inc(hg_exp, 1)
                A(tile(H_["EM"]), tile(H_["CC"]), ACT.Exp, scale=-1.0).then_inc(hg_act, 1)
                act.wait_ge(hg_pe, h * 6 + 1)
                A(tile(H_["IT"]), bank[4][:, :], ACT.Copy).then_inc(hg_act, 1)
                act.wait_ge(hg_pe, h * 6 + 2)
                A(tile(H_["KT"]), bank[5][:, :], ACT.Copy).then_inc(hg_act, 1)
                act.wait_ge(hg_pe, h * 6 + 5)
                A(tile(H_["SQ"]), bank[7][:, :], ACT.Square).then_inc(hg_act, 1)
                act.wait_ge(hg_pe, h * 6 + 6)
                A(tile(H_["RT"]), bank[6][:, :], ACT.Sqrt, scale=1.0 / HG_D, bias=pp("eps")).then_inc(hg_act, 1)
            q += 4 * HG_H
            R_ = RTT
            act.wait_ge(hg_dve, 6 * HG_H + 1)
            with act.Fori(0, RET_H) as h:
                for j in range(8):
                    act.wait_ge(block_used, h * 12 + B_RET + j + 1)
                    if j == 0:
                        act.wait_ge(rt_dve, h * 12 + 1)
                    A(tile(R_["Q"] + j), bank[(q + j) % NBANK][:, :], ACT.Copy).then_inc(evac, 1)
                for s in range(TT):
                    act.wait_ge(rt_pe, h * 16 + s + 1)
                    A(tile(R_["VT"] + s), bank[4][:, :], ACT.Copy).then_inc(rt_act, 1)
                st.enter(h, 4, RET_H)
                for j in range(4):
                    act.wait_ge(rt_pe, h * 16 + 8 + 2 * j + 1)
                    if j:
                        act.wait_ge(rt_pe, h * 16 + 8 + 2 * j)
                    st.go(A(tile(R_["O"] + j), bank[7][:, :], ACT.Copy))
                    A(tile(R_["SQ"]), bank[7][:, :], ACT.Square).then_inc(rt_act, 1)
                st.leave()
                act.wait_ge(rt_pe, h * 16 + 16)
                A(tile(R_["RT"]), bank[4][:, :], ACT.Sqrt, scale=1.0 / RET_DV, bias=pp("eps")).then_inc(rt_act, 1)
                for j in range(8, 12):
                    act.wait_ge(block_used, h * 12 + B_RET + j + 1)
                    A(tile(R_["G"] + j - 8), bank[(q + j) % NBANK][:, :], ACT.Silu).then_inc(evac, 1)
            q += 12 * RET_H
            act.wait_ge(rt_dve, 12 * RET_H + 1)
            for k in range(KD):
                for j in range(4):
                    act.wait_ge(block_used, B_MERGE + 5 * k + (5 if j == 3 else j + 1))
                    if k >= 2 and j == 0:
                        act.wait_ge(mg_dve, k - 1)
                    A(tile(48 + 4 * (k % 2) + j), bank[q % NBANK][:, :], ACT.Sigmoid if j < 2 else ACT.Copy).then_inc(evac, 1)
                    q += 1
            for k in range(KD):
                act.wait_ge(block_used, B_WOUT2 + k + 1)
                if k == 0:
                    act.wait_ge(mg_dve, KD)
                A(tile(48 + k), bank[q % NBANK][:, :], ACT.Copy).then_inc(evac, 1)
                q += 1
            norm_squares(5, lambda k: tile(X + k), lambda k: act.wait_ge(resid_ready, 2 * KD + k + 1))
            for k in range(2 * PEER_H):
                act.wait_ge(block_used, B_PQ + k + 1)
                A(tile(24 + k), bank[q % NBANK][:, :], ACT.Copy).then_inc(evac, 1)
                q += 1
            for t in range(TT):
                for b in range(4):
                    act.wait_ge(tk_pe, 4 * t + b + 1)
                    A(tile(PST + 4 * t + b), bank[b][:, :], ACT.Copy).then_inc(tk_act, 1)
            for t in range(TT):
                act.wait_ge(tk_sub, t + 1)
                A(bestv[:, :, :], bestv[:, :, :], ACT.Exp).then_inc(tk_exp, 1)
                act.wait_ge(tk_pe, 16 + t + 1)
                A(arena[:, PTT:PTT + 3, t * P:(t + 1) * P], bank[4][:, 0:384].rearrange("p (j t) -> p j t", j=3),
                  ACT.Copy).then_inc(tk_act, 1)
            act.wait_ge(tk_act, 20)
            act.sem_inc(oh_act, 2)
            def gate_copies(i, first=False):
                for hb in range(2):
                    buf = arena[:, GBUF + 8 * hb:GBUF + 8 * hb + 8, :].rearrange("p a b -> p (a b)").rearrange("p (j t) -> p t j", t=TG)
                    if not first:
                        act.wait_ge(gst[hb], i * 16)
                    for u in range(8):
                        act.wait_ge(oh_pe, i * 16 + (8 * hb + u + 1))
                        A(buf[:, 4 * u:4 * u + 4, :], v4(bank[5 + u % 2][:, :]), ACT.Copy).then_inc(oh_act, 1)

            gate_copies(0, first=True)
            with act.Fori(1, NTG // 2) as i:
                gate_copies(i)
            E_ = EXT

            def gelu(g, j, n, it=0):
                act.wait_ge(block_used, it * 32 + n + 1)
                k = g * JG + j
                if k >= 2:
                    act.wait_ge(ex_prod, it * 2 * JG + k - 1)
                A(tile(E_["TMP"] + j % 2), bank[j % 2][:, :], ACT.Gelu_apprx_tanh).then_inc(ex_gelu, 1)

            for j in range(JG):
                gelu(0, j, B_EXP + j)

            def group(g, n, it=0):
                for j in range(4):
                    gelu(g + 1, j, n + 4 + j, it)
                for j in range(4, 8):
                    gelu(g + 1, j, n + 12 + j - 4, it)
                return n + 16

            n = group(0, B_EXP + JG)
            n = group(1, n)
            with act.Fori(0, (NJG - 4) // 2) as i:
                group(2, n, i)
                group(3, n + 16, i)
            n += 32 * ((NJG - 4) // 2)
            n = group(NJG - 2, n)
            norm_squares(6, lambda k: tile(X + k), lambda k: act.wait_ge(resid_ready, 3 * KD + k + 1))

        @block.gpsimd
        def _(pool):
            with pool.Fori(0, NTG // 2) as i:
                for hb in range(2):
                    pool.wait_ge(oh_act, i * 16 + (8 * hb + 10))
                    pool.dma_start(gates_d[bass.ds(i * 2 + hb, 1)].rearrange("a p n -> (a p) n"),
                                   arena[:, GBUF + 8 * hb:GBUF + 8 * hb + 8, :].rearrange("p a b -> p (a b)")
                                   ).then_inc(gst[hb], 16)
            for hb in range(2):
                pool.wait_ge(gst[hb], 16 * (NTG // 2))
            gv = gates_d.rearrange("g p (j t) -> p g (j t)", t=TG)
            E_ = EXT

            def load(par_, off):
                pool.dma_start(arena[:, E_["W"] + 8 * par_:E_["W"] + 8 * par_ + 8, :].rearrange("p a b -> p (a b)")
                               .rearrange("p (g n) -> p g n", g=NTG), gv[:, 0:NTG, off]).then_inc(gld[par_], 16)

            load(0, slice(0, JG * TG))
            load(1, slice(JG * TG, 2 * JG * TG))
            with pool.Fori(1, NJG // 2) as i:
                for par_ in range(2):
                    pool.wait_ge(ex_prod, i * 2 * JG + (par_ + 1) * JG - 2 * JG)
                    load(par_, bass.ds((i * 2 + par_) * (JG * TG), JG * TG))

        @block.vector
        def _(ve):
            st = Steps(ve, dve_s)
            TSM, TTN, STT, CP = ve.tensor_scalar, ve.tensor_tensor, ve.scalar_tensor_tensor, ve.tensor_copy

            def norm_scale(i, gain, src, dst=None, done=None, count=0):
                ve.wait_ge(root_ready, i + 1)
                ve.reciprocal(tile(RSQ), tile(NT1)).then_inc(root_used, 1)
                ve.wait_ge(root_used, i + 1)
                for k in range(KD):
                    if dst is not None:
                        STT(dst(k), src(k), pp(gain, k), tile(RSQ), ALU.mult, ALU.mult).then_inc(done, 1)
                    else:
                        st(STT(src(k), src(k), pp(gain, k), tile(RSQ), ALU.mult, ALU.mult))
                        TTN(tile(X + k), tile(X + k), src(k), ALU.add).then_inc(resid_ready, 1)
                if dst is not None:
                    ve.wait_ge(done, count)

            x_tile, xn_tile, mo_tile = (lambda k: tile(X + k)), (lambda k: tile(XN + k)), (lambda k: tile(MO + k))
            ve.wait_ge(in_x, 16)
            ve.wait_ge(in_par, 16)
            ve.wait_ge(in_cst, 16)
            norm_scale(0, "attn_pre", x_tile, xn_tile, norm_ready, KD)
            dests = [GFT, LAT, GL] + [RR + i for i in range(4)] + [RK + i for i in range(4)] + [RV + i for i in range(4)]
            for n in range(12, N_FOX + N_RW):
                ve.wait_ge(evac, n + 1)
                raw, d = tile(RAW + n % 2), tile(DTMP)
                mu = pp("mu", n - 12)
                st.go(TTN(d[:, 1:T], raw[:, 0:T - 1], raw[:, 1:T], ALU.subtract))
                st(TSM(d[:, 0:1], raw[:, 0:1], -1.0, None, ALU.mult))
                STT(tile(dests[n - 12]), d, mu, raw, ALU.mult, ALU.add).then_inc(shifted, 1)
                ve.wait_ge(shifted, n - 11)
                if n == 12:
                    z, a = arena[32:40, BON, :], arena[32:40, BON + 1, :]
                    st(TSM(z, tile(GFT)[32:40, :], par[32:40, PCOL["f_bias"]:PCOL["f_bias"] + 1], None, ALU.add))
                    st(TSM(a, z, -1.0, None, ALU.mult))
                    TTN(a, a, z, ALU.max).then_inc(fc_z, 1)
                    ve.wait_ge(fc_ln, 1)
                    st(TSM(z, z, 0.0, None, ALU.min))
                    st(TTN(z, z, a, ALU.subtract))
                    ve.tensor_tensor_scan(tile(GFT)[32:40, :], cst[32:40, CCOL["one_row"][0]:CCOL["one_row"][0] + T], z, 0.0,
                                          ALU.mult, ALU.add).then_inc(fc_ready, 1)
                    ve.wait_ge(fc_ready, 1)
            units = [(h, t) for h in range(8) for t in range(TT)]

            def fox_max(u):
                n = (units[u][1] + 1) * P
                ve.wait_ge(fs_ready, u + 1)
                st(ve.tensor_reduce(stat[:, u:u + 1], bank[u % 2][:, 0:n], AX.X, ALU.max))
                TSM(stat[:, 32 + u:33 + u], stat[:, u:u + 1], -0.125, None, ALU.mult).then_inc(fmax, 1)

            def fox_norm(u):
                n = (units[u][1] + 1) * P
                ve.wait_ge(fexp, u + 1)
                st(ve.reciprocal(stat[:, u:u + 1], stat[:, 64 + u:65 + u]))
                TSM(tile(PR0 + u % 2)[:, 0:n], tile(PR0 + u % 2)[:, 0:n], stat[:, u:u + 1], None, ALU.mult).then_inc(fnorm, 1)

            fox_max(0)
            for u in range(len(units)):
                if u + 1 < len(units):
                    fox_max(u + 1)
                fox_norm(u)

            ve.wait_ge(rw_act, 15)
            ve.wait_ge(fo_out, NPAIR)
            for m in range(NPAIR):
                R, K, V, kk, a = tile(RR + m), tile(RK + m), tile(RV + m), tile(KKT + m), tile(RA + m)
                st(TSM(tile(LW + m), tile(LW + m), -E_HALF, None, ALU.mult))
                if m:
                    ve.wait_ge(exp_ready, m)
                st(ve.tensor_tensor_scan(tile(77), cc("reset"), tile(LW + m), 0.0, ALU.mult, ALU.add))
                cu = ch(tile(77))
                st(TTN(ch(tile(75)), cu, cu[:, :, MID:MID + 1].to_broadcast([P, NCH, C]), ALU.subtract))
                TTN(tile(76), tile(75), tile(LW + m), ALU.subtract).then_inc(cum_ready, 1)
                ve.wait_ge(rw_act, 15 + 2 * m + 2)
                st(TSM(tile(74), tile(74), 1e-12, None, ALU.max))
                st(ve.reciprocal(tile(74), tile(74)))
                st.go(STT(kk, K, pp("k_k", m), tile(74), ALU.mult, ALU.mult))
                st(TSM(tile(81), a, 1.0, pp("k_a", m), ALU.subtract, ALU.mult))
                st(STT(K, tile(81), 1.0, K, ALU.add, ALU.mult))
                STT(tile(RAW), R, pp("r_k", m), K, ALU.mult, ALU.mult).then_inc(rw_dve, 1)
                ve.wait_ge(exp_ready, m + 1)
                st.go(STT(tile(TA + m), kk, -1.0, tile(80), ALU.mult, ALU.mult))
                st.go(TTN(tile(TR + m), R, tile(78), ALU.mult))
                st.go(TTN(tile(TK + m), K, tile(79), ALU.mult))
                st(TTN(kk, kk, a, ALU.mult))
                st.go(TTN(tile(TB + m), kk, tile(79), ALU.mult))
                st.go(CP(dch[:, 1, m * NCH:(m + 1) * NCH], ch(tile(78))[:, :, C - 1]))
                ve.wait_ge(rw_pe, 12 + 2 * m + 2)
                st.sync()
                TTN(tile(BON + m), bank[5][:, :], V, ALU.mult).then_inc(rw_dve, 1)
                ve.wait_ge(rw_dve, 2 * m + 2)
            dv = lambda i: dch[:, i, :].rearrange("p (m c) -> p m c", c=NCH)
            st(TTN(dv(2)[:, :, 0:NCH - 1], dv(1)[:, :, 0:NCH - 1], dv(0)[:, :, 1:NCH], ALU.mult))
            ve.wait_ge(rw_act, 39)
            for m in range(NPAIR):
                pb, ab = 36 + RW_PE * m, 39 + RW_ACT * m
                for e in range(2):
                    hs, b0 = HS[e], 3 * e
                    ve.wait_ge(rw_pe, pb + e + 1)
                    if m:
                        ve.wait_ge(rw_act, ab)
                    st.go(TTN(v4(tile(hs[0])), v4(bank[b0][:, :]), mask4("strict"), ALU.mult))
                    st(TTN(v4(tile(hs[2])), v4(bank[b0 + 1][:, :]), mask4("strict_T"), ALU.mult))
                    st.go(TTN(v4(tile(hs[6])), v4(bank[b0 + 2][:, :]), mask4("strict_T"), ALU.mult))
                    TTN(v4(tile(hs[4])), v4(tile(hs[2])), mask4("ident"), ALU.add).then_inc(rw_dve, 1)
                for lev in range(5):
                    for e in range(2):
                        hs, b0 = HS[e], 3 * e
                        a, b = (0, 1) if lev % 2 == 0 else (1, 0)
                        ve.wait_ge(rw_pe, pb + 2 + 4 * lev + e + 1)
                        st.go(CP(tile(hs[2 + b]), bank[b0 + 1][:, :]))
                    for e in range(2):
                        hs, b0 = HS[e], 3 * e
                        a, b = (0, 1) if lev % 2 == 0 else (1, 0)
                        ve.wait_ge(rw_pe, pb + 2 + 4 * lev + 2 + e + 1)
                        ve.wait_ge(rw_dve, 8 + RW_DVE * m + 2 * lev + e + 1)
                        TTN(tile(hs[4 + b]), bank[b0 + 2][:, :], tile(hs[4 + a]), ALU.add).then_inc(rw_dve, 1)
            bp, bd = 36 + RW_PE * 4, 8 + RW_DVE * 4
            shv = arena[:, SH:SH + 4, :].rearrange("p a b -> p (a b)").rearrange("p (c n) -> p c n", c=NCH)
            for c in range(NCH):
                g, p = c // 2, c % 2
                trow = slice(p * HD, (p + 1) * HD)
                if c == 0:
                    ve.wait_ge(rw_act, 39 + RW_ACT * 4)
                    CP(tile(UU + g)[trow, :], tile(U0 + g)[trow, :]).then_inc(rw_dve, 1)
                else:
                    ve.wait_ge(rw_pe, bp + 2 * c)
                    for e in range(2):
                        eh = lambda ap: ap[trow, :].rearrange("p (m e i) -> p m e i", m=4, e=2)[:, :, e, :]
                        ins = TTN(eh(tile(UU + g)), bank[6 - e][trow, 0:256].rearrange("p (m i) -> p m i", m=4),
                                  eh(tile(U0 + g)), ALU.add)
                        if e == 0:
                            st.go(ins)
                        else:
                            ins.then_inc(rw_dve, 1)
                if c == NCH - 1:
                    ve.wait_ge(rw_dve, bd + 15)
                    continue
                ve.wait_ge(rw_pe, bp + 2 * c + 1)
                s3 = lambda ap: ap.rearrange("p (m i) -> p m i", m=4)
                if c == 0:
                    st(CP(tile(74)[:, 0:256], bank[7][:, 0:256]))
                else:
                    st(TTN(tile(74)[:, 0:256], bank[7][:, 0:256], shv[:, c, :], ALU.add))
                TTN(s3(shv[:, c + 1, :]), s3(tile(74)[:, 0:256]), dv(2)[:, :, c:c + 1].to_broadcast([P, 4, HD]),
                    ALU.mult).then_inc(rw_dve, 1)
                ve.wait_ge(rw_dve, bd + 2 * c + 2)
            bp, bd = bp + 14, bd + 15
            for h in range(8):
                hs = HS[h % 2]
                for k in range(2):
                    ve.wait_ge(rw_pe, bp + 3 * h + k + 1)
                    if h >= 2:
                        ve.wait_ge(rw_pe, bp + 3 * (h - 1))
                    TTN(v4(tile(hs[k])), v4(bank[k][:, :]), mask4("incl_T"), ALU.mult).then_inc(rw_dve, 1)
            bp, bd = bp + 24, bd + 16
            ba = 39 + RW_ACT * 4 + 4
            T1, T2, T3, T4 = HS[0][1], HS[0][2], HS[0][3], HS[0][4]
            for m in range(NPAIR):
                ve.wait_ge(rw_pe, bp + 2 * m + 1)
                ve.wait_ge(rw_act, ba + 2 * m)
                TTN(tile(T1), tile(YY + m), bank[0][:, :], ALU.subtract).then_inc(rw_dve, 1)
                ve.wait_ge(rw_act, ba + 2 * m + 2)
                st(ve.reciprocal(tile(T3), tile(T2)))
                st(STT(tile(T4), tile(T1), pp("ln_w", m), tile(T3), ALU.mult, ALU.mult))
                st(STT(tile(T4), tile(T4), pp("ln_b", m), tile(BON + m), ALU.add, ALU.add))
                TTN(tile(ORW + m), tile(T4), tile(RG + m), ALU.mult).then_inc(rw_dve, 1)
                ve.wait_ge(rw_dve, bd + 2 * m + 2)

            norm_scale(1, "attn_post", mo_tile)
            norm_scale(2, "ffn_pre", x_tile, xn_tile, norm_ready, 2 * KD)
            ve.sem_inc(ffn_pair, 2)
            q = N_FOX + N_RW + KD
            with ve.Fori(0, KF // 2) as i:
                for j in range(2):
                    ve.wait_ge(evac, i * 4 + q + 2 * j + 2)
                    TTN(arena[:, bass.ds(i * 2 + (16 + j), 1), :].rearrange("p a t -> p (a t)"), tile(48 + 2 * j), tile(49 + 2 * j),
                        ALU.mult).then_inc(ffn_pair, 1)
            q += 2 * KF
            norm_scale(3, "ffn_post", mo_tile)
            st(TTN(lbt[:, 0, :], par[:, PCOL["lb0"]:PCOL["lb0"] + 8], par[:, PCOL["lb1"]:PCOL["lb1"] + 8], ALU.max))
            st(TTN(lbt[:, 1, :], par[:, PCOL["lb0"]:PCOL["lb0"] + 8], lbt[:, 0, :], ALU.subtract))
            TTN(lbt[:, 2, :], par[:, PCOL["lb1"]:PCOL["lb1"] + 8], lbt[:, 0, :], ALU.subtract).then_inc(lb_ready, 1)
            ve.wait_ge(lb_ready, 2)
            st(TTN(lbt[:, 2, :], lbt[:, 1, :], lbt[:, 2, :], ALU.add))
            st(ve.reciprocal(lbt[:, 2, :], lbt[:, 2, :]))
            st(TTN(lbt[:, 0, :], lbt[:, 1, :], lbt[:, 2, :], ALU.mult))
            TSM(lbt[:, 1, :], lbt[:, 0, :], -1.0, 1.0, ALU.mult, ALU.add).then_inc(hg_dve, 1)
            ve.wait_ge(hg_dve, 1)
            norm_scale(4, "mix_norm", x_tile, xn_tile, norm_ready, 3 * KD)

            q += KD
            H_ = HGT
            with ve.Fori(0, HG_H) as h:
                st.enter(h, 18, HG_H)
                ve.wait_ge(evac, h * 4 + q + 1)
                lb, lb1 = lbt[:, 0, bass.ds(h, 1)], lbt[:, 1, bass.ds(h, 1)]
                TSM(tile(H_["F"]), tile(H_["F"]), lb1, lb, ALU.mult, ALU.add).then_inc(hg_dve, 1)
                ve.wait_ge(hg_dve, h * 6 + 2)
                st.go(TSM(tile(H_["K"]), tile(H_["F"]), -1.0, 1.0, ALU.mult, ALU.add))
                ve.wait_ge(hg_act, h * 6 + 1)
                st(ve.tensor_tensor_scan(tile(H_["CU"]), cc("reset"), tile(H_["LF"]), 0.0, ALU.mult, ALU.add))
                cu = ch(tile(H_["CU"]))
                TTN(ch(tile(H_["CC"])), cu, cu[:, :, MID:MID + 1].to_broadcast([P, NCH, C]), ALU.subtract).then_inc(hg_dve, 1)
                ve.wait_ge(hg_act, h * 6 + 2)
                ve.wait_ge(evac, h * 4 + q + 4)
                st.go(TTN(tile(H_["KD"]), tile(H_["K"]), tile(H_["EM"]), ALU.mult))
                STT(tile(H_["QD"]), tile(H_["Q"]), HG_D ** -0.5, tile(H_["EP"]), ALU.mult, ALU.mult).then_inc(hg_dve, 1)
                ve.wait_ge(hg_exp, h * 2 + 2)
                st(TTN(dch[:, 5, 0:NCH - 1], ch(tile(H_["EP"]))[:, 0:NCH - 1, C - 1], dch[:, 4, 1:NCH], ALU.mult))
                ve.wait_ge(hg_pe, h * 6 + 3)
                TTN(v4(tile(H_["AM"])), v4(bank[6][:, :]), mask4("incl_T"), ALU.mult).then_inc(hg_dve, 1)
                ve.wait_ge(hg_pe, h * 6 + 4)
                for c in range(NCH - 1):
                    kv = bank[4 + c % 2][:, (c // 2) * P:(c // 2 + 1) * P]
                    src = kv
                    if c:
                        st(TTN(tile(H_["X"])[:, 0:P], kv, H_["S"](c), ALU.add))
                        src = tile(H_["X"])[:, 0:P]
                    ins = TSM(H_["S"](c + 1), src, dch[:, 5, c:c + 1], None, ALU.mult)
                    if c < NCH - 2:
                        st(ins)
                    else:
                        ins.then_inc(hg_dve, 1)
                ve.wait_ge(hg_act, h * 6 + 6)
                st(ve.reciprocal(tile(H_["R2"]), tile(H_["RT"])))
                wn = par[:, bass.ds(h + PCOL["hg_norm"], 1)]
                st(STT(tile(H_["R2"]), bank[7][:, :], wn, tile(H_["R2"]), ALU.mult, ALU.mult))
                TTN(arena[:, bass.ds(h + 16, 1), :].rearrange("p a t -> p (a t)"), tile(H_["R2"]), tile(H_["G"]),
                    ALU.mult).then_inc(hg_dve, 1)
                ve.wait_ge(hg_dve, h * 6 + 7)
                st.leave()
            q += 4 * HG_H
            R_ = RTT
            ve.wait_ge(in_rot, 32)
            ve.sem_inc(rt_dve, 1)
            with ve.Fori(0, RET_H) as h:
                st.enter(h, 13, RET_H)
                cos, sin = tile(R_["COS"]), tile(R_["COS"] + 1)
                n0 = 0
                for k, (src, dst) in enumerate((("Q", "QR"), ("K", "KR"))):
                    x1, x2 = tile(R_[src]), tile(R_[src] + 1)
                    sc = 1.0 if k == 0 else RET_DK ** -0.5
                    ve.wait_ge(evac, h * 12 + q + 2 * k + 2)
                    st.go(STT(tile(R_["T"]), x1, sc, cos, ALU.mult, ALU.mult))
                    st.go(STT(tile(R_["T"] + 1), x2, sc, sin, ALU.mult, ALU.mult))
                    st.go(STT(tile(R_["T"] + 2), x1, sc, sin, ALU.mult, ALU.mult))
                    st(STT(tile(R_["T"] + 3), x2, sc, cos, ALU.mult, ALU.mult))
                    TTN(tile(R_[dst]), tile(R_["T"]), tile(R_["T"] + 1), ALU.subtract).then_inc(rt_dve, 1)
                    TTN(tile(R_[dst] + 1), tile(R_["T"] + 2), tile(R_["T"] + 3), ALU.add).then_inc(rt_dve, 1)
                    ve.wait_ge(rt_dve, h * 12 + 2 * k + 3)
                for s in range(TT):
                    n = T - s * P
                    ve.wait_ge(rt_pe, h * 16 + 4 + s + 1)
                    TTN(tile(R_["AM"] + s)[:, 0:n], bank[5 + s % 2][:, 0:n],
                        arena[:, bass.ds(h + R_["MASK"], 1), 0:n].rearrange("p a t -> p (a t)"), ALU.mult).then_inc(rt_dve, 1)
                ve.wait_ge(rt_act, h * 9 + 9)
                st(ve.reciprocal(tile(R_["R2"]), tile(R_["RT"])))
                for j in range(4):
                    st(TTN(tile(R_["O"] + j), tile(R_["O"] + j), tile(R_["R2"]), ALU.mult))
                    ve.wait_ge(evac, h * 12 + q + 8 + j + 1)
                    TTN(arena[:, bass.ds(h * 4 + (24 + j), 1), :].rearrange("p a t -> p (a t)"), tile(R_["O"] + j),
                        tile(R_["G"] + j), ALU.mult).then_inc(rt_dve, 1)
                ve.wait_ge(rt_dve, h * 12 + 13)
                st.leave()
            q += 12 * RET_H
            for k in range(KD):
                ve.wait_ge(evac, q + 4)
                q += 4
                b = 48 + 4 * (k % 2)
                st.go(TTN(tile(b), tile(b), tile(b + 2), ALU.mult))
                st(TTN(tile(b + 1), tile(b + 1), tile(b + 3), ALU.mult))
                TTN(tile(40 + k), tile(b), tile(b + 1), ALU.add).then_inc(mg_dve, 1)
            for k in range(KD):
                ve.wait_ge(evac, q + 1)
                q += 1
                TTN(tile(X + k), tile(X + k), tile(48 + k), ALU.add).then_inc(resid_ready, 1)
            norm_scale(5, "ffn_norm", x_tile, xn_tile, norm_ready, 4 * KD)
            q += 2 * PEER_H

            io16 = cst[:, CCOL["iota"][0]:CCOL["iota"][0] + 16]
            big = lambda i: arena[:, PBIG + 4 * i:PBIG + 4 * i + 4, :].rearrange("p a b -> p (a b)")
            for t in range(TT):
                ve.wait_ge(tk_act, 16 if t else 4)
                if t == 0:
                    ve.wait_ge(tk_act, 16)
                sc = arena[:, PST + 4 * t:PST + 4 * t + 4, :].rearrange("p a b -> p (a b)")
                for n in range(16):
                    s = sc[:, n * P:(n + 1) * P]
                    st(ve.max(topv[:, n, 0:8], s))
                    st(ve.max_index(topi[:, n, 0:8], topv[:, n, 0:8], s))
                    st(ve.match_replace(s, topv[:, n, 0:8], s, -3.0e38))
                    st(ve.max(topv[:, n, 8:16], s))
                    st.go(ve.max_index(topi[:, n, 8:16], topv[:, n, 8:16], s))
                st.sync()
                st.go(CP(topf, topi))
                tv = topv[:, :, :].rearrange("p (h s) k -> p h s k", s=2)
                tf = topf[:, :, :].rearrange("p (h s) k -> p h s k", s=2)
                cand = big(0).rearrange("p (h a b) -> p h a b", h=8, a=16)
                st(TTN(cand, tv[:, :, 0, :].unsqueeze(3).to_broadcast([P, 8, 16, 16]),
                       tv[:, :, 1, :].unsqueeze(2).to_broadcast([P, 8, 16, 16]), ALU.add))
                if t:
                    ve.wait_ge(tk_exp, t)
                for h in range(8):
                    s = big(0)[:, h * 256:(h + 1) * 256]
                    st(ve.max(bestv[:, h, 0:8], s))
                    st(ve.max_index(besti[:, h, 0:8], bestv[:, h, 0:8], s))
                    st(ve.match_replace(s, bestv[:, h, 0:8], s, -3.0e38))
                    st(ve.max(bestv[:, h, 8:16], s))
                    st.go(ve.max_index(besti[:, h, 8:16], bestv[:, h, 8:16], s))
                st.sync()
                st(CP(gsum[:, 0, :], bestv[:, :, 0]))
                TTN(bestv[:, :, :], bestv[:, :, :], gsum[:, 0, :].unsqueeze(2).to_broadcast([P, 8, 16]),
                    ALU.subtract).then_inc(tk_sub, 1)
                st.go(TSM(bests[:, :, :], besti[:, :, :], 4, None, ALU.logical_shift_right))
                st(TSM(besti[:, :, :], besti[:, :, :], 15, None, ALU.bitwise_and))
                st.go(CP(bestf[:, 0, :, :], bests[:, :, :]))
                st(CP(bestf[:, 1, :, :], besti[:, :, :]))
                if t:
                    ve.wait_ge(tk_pe, 16 + t)
                for s in range(2):
                    hot = big(1).rearrange("p (h k a) -> p h k a", h=8, k=16)
                    st(TTN(hot, bestf[:, s, :, :].unsqueeze(3).to_broadcast([P, 8, 16, 16]),
                           io16.unsqueeze(1).unsqueeze(1).to_broadcast([P, 8, 16, 16]), ALU.is_equal))
                    st(TTN(hot, hot, tf[:, :, s, :].unsqueeze(2).to_broadcast([P, 8, 16, 16]), ALU.mult))
                    st(ve.tensor_reduce(pairs[:, s, :].rearrange("p (h k) -> p h k", h=8), hot, AX.X, ALU.add))
                ve.wait_ge(tk_exp, t + 1)
                st(ve.tensor_reduce(gsum[:, 0, :], bestv[:, :, :], AX.X, ALU.add))
                st(ve.reciprocal(gsum[:, 1, :], gsum[:, 0, :]))
                TTN(pairs[:, 2, :].rearrange("p (h k) -> p h k", h=8), bestv[:, :, :],
                    gsum[:, 1, :].unsqueeze(2).to_broadcast([P, 8, 16]), ALU.mult).then_inc(tk_dve, 1)
                ve.wait_ge(tk_dve, t + 1)
            ve.wait_ge(tk_act, 20)
            iota = cc("iota")
            with ve.Fori(0, NTG // 2) as i:
                for u in range(2 * TG // 4):
                    ve.wait_ge(oh_act, i * 16 + u + 1)
                    for j in range(4):
                        t1 = bass.ds(i * (2 * TG) + (4 * u + j), 1)
                        TSM(oneA[:, u % 2, j, :], iota, arena[:, PTT, t1], arena[:, PTT + 2, t1], ALU.is_equal, ALU.mult)
                        ins = TSM(oneB[:, u % 2, j, :], iota, arena[:, PTT + 1, t1], None, ALU.is_equal)
                    ins.then_inc(oh_dve, 1)
            E_ = EXT
            for d in range(KD):
                st.go(ve.memset(tile(E_["ACC"] + d), 0.0))
            st.sync()

            def prod(g, j, it=0, gl=None):
                if j == 0:
                    ve.wait_ge(gld[g % 2], it * 16 + 16 * (g // 2 + 1))
                ve.wait_ge(ex_gelu, it * 2 * JG + g * JG + j + 1)
                wv = arena[:, E_["W"] + 8 * (g % 2):E_["W"] + 8 * (g % 2) + 8, :].rearrange("p a b -> p (a b)").rearrange(
                    "p (g j t) -> p g j t", g=NTG, j=JG)[:, :, j, :]
                TTN(tile(E_["GW"] + (g % 2) * JG + j).rearrange("p (g t) -> p g t", g=NTG),
                    tile(E_["TMP"] + j % 2).rearrange("p (g t) -> p g t", g=NTG), wv, ALU.mult).then_inc(ex_prod, 1)

            def acc(g, half, it=0, last=False):
                n = B_EXP + JG + 16 * g + (4 if half == 0 else 8 if last else 12)
                ve.wait_ge(block_used, it * 32 + n)
                if 2 * g + half >= 2:
                    ve.wait_ge(ex_acc, it * 16 + 4 * (2 * g + half - 1))
                for d in range(4):
                    o = tile(E_["ACC"] + 4 * half + d)
                    TTN(o, o, bank[2 + d][:, :], ALU.add).then_inc(ex_acc, 1)

            for j in range(JG):
                prod(0, j)

            def group(g, it=0, last=False):
                acc(g, 0, it)
                if not last:
                    for j in range(4):
                        prod(g + 1, j, it)
                acc(g, 1, it, last)
                if not last:
                    for j in range(4, 8):
                        prod(g + 1, j, it)

            group(0)
            group(1)
            with ve.Fori(0, (NJG - 4) // 2) as i:
                group(2, i)
                group(3, i)
            group(NJG - 2)
            group(NJG - 1, last=True)
            ve.wait_ge(ex_acc, 8 * NJG)
            for k in range(KD):
                TTN(tile(X + k), tile(X + k), tile(E_["ACC"] + k), ALU.add).then_inc(resid_ready, 1)
            norm_scale(6, "final_norm", x_tile, xn_tile, out_ready, KD)


def _tiles(w, order=None):
    k, n = w.shape
    return w.reshape(k // P, P, n // P, P).transpose(2, 1, 0, 3).reshape(n // P, P, k)


def _constants():
    i = np.arange(P)
    same = (i[:, None] // C) == (i[None, :] // C)
    lower = i[:, None] > i[None, :]
    c = {
        "ident": np.eye(P), "ones": np.ones((P, P)), "bones": same, "bmean": same / HD,
        "strict_T": same & lower.T, "strict": same & lower, "incl_T": same & ~lower,
        "neg": np.where(i[:, None] >= i[None, :], 0.0, NEG), "iota": np.tile(i, (P, 1)),
        "reset": np.tile((np.arange(T) % C != 0), (P, 1)), "one_row": np.ones((P, T)),
    }
    table = np.concatenate([np.asarray(c[n], np.float32) for n, _ in CONSTS], axis=1)
    select = np.zeros((8, 8, P), np.float32)
    select[np.arange(8), np.arange(8)] = -8.0
    half = RET_DK // 2
    inv = np.float32(10000.0) ** (-np.arange(half, dtype=np.float32) / half)
    ang = inv.astype(np.float32)[:, None] * np.arange(T, dtype=np.float32)[None, :]
    rotary = np.stack([np.cos(ang), np.sin(ang)], axis=1).astype(np.float32)
    log_g = np.log1p(-np.exp2(-5.0 - np.arange(RET_H)))
    rel = np.arange(T)[None, :] - i[:, None]
    decay = np.where(rel[:, None, :] >= 0, np.exp(log_g[None, :, None] * np.maximum(rel, 0)[:, None, :]), 0.0)
    return table, select.reshape(8, 8 * P), rotary, decay.astype(np.float32)


def _stream(a):
    w_in = a["w_in"][0]
    fw, rw = 3 * 512, 3 * 512 + 8
    gf = np.zeros((D, P), np.float32)
    gf[:, 0:32] = w_in[:, rw + 1536 + 128 + 128:]
    gf[:, 32:40] = w_in[:, fw:fw + 8]
    parts = [_tiles(w_in[:, 0:fw]), _tiles(gf), _tiles(w_in[:, rw + 1536:rw + 1536 + 256]), _tiles(w_in[:, rw:rw + 1536])]
    parts.append(_tiles(a["w_out"][0]))
    gate, up = _tiles(a["ffn_w_gate"][0]), _tiles(a["ffn_w_up"][0])
    parts.append(np.stack([gate, up], axis=1).reshape(2 * KF, P, D))
    down = np.zeros((KD, P, 3 * D), np.float32)
    down[:, :, 0:FF] = _tiles(a["ffn_w_down"][0])
    parts.append(down.reshape(KD, P, 3, D).transpose(0, 2, 1, 3).reshape(3 * KD, P, D))
    w2 = _tiles(a["w_in_2"][0])
    hq, hf, hi, hg = (w2[8 * i:8 * i + 8] for i in range(4))
    parts.append(np.stack([hf, hi, hg, hq], axis=1).reshape(4 * HG_H, P, D))
    rq, rk = (w2[o:o + 8].reshape(4, 2, P, D) for o in (32, 40))
    rv, rg = (w2[o:o + 16].reshape(4, 4, P, D) for o in (48, 64))
    parts.append(np.concatenate([rq, rk, rv, rg], axis=1).reshape(12 * RET_H, P, D))
    ret = _tiles(a["w_branch_ret_2"][0]).reshape(KD, P, 2, D).transpose(0, 2, 1, 3)
    merge = np.concatenate([w2[80:88, None], w2[88:96, None], _tiles(a["w_branch_hg_2"][0])[:, None], ret], axis=1)
    parts.append(merge.reshape(5 * KD, P, D))
    parts.append(_tiles(a["w_out_2"][0]))
    parts.append(_tiles(a["peer_w_q_2"][0]))
    keys = a["peer_sub_keys_2"][0].reshape(2, 8, NKEY, P)
    parts.append(keys.transpose(0, 3, 1, 2).reshape(2, P, D))
    u = a["expert_u_2"][0].reshape(NKEY, NKEY, KD, P).transpose(1, 3, 2, 0).reshape(NJG, JG, P, D)
    v = a["expert_v_2"][0].reshape(NKEY, NJG, 4, 2, 2, 512).transpose(1, 4, 2, 0, 3, 5).reshape(NJG, 2, 4, P, D)
    parts.append(u[0])
    for g in range(NJG):
        parts.append(v[g, 0])
        if g + 1 < NJG:
            parts.append(u[g + 1, 0:4])
        parts.append(v[g, 1])
        if g + 1 < NJG:
            parts.append(u[g + 1, 4:8])
    parts.append(np.zeros((N_LOADED - N_BLOCKS, P, D), np.float32))
    return np.concatenate(parts, axis=0)


def _parameters(a):
    col = lambda v: np.asarray(v, np.float32).reshape(-1, P).T
    mu = np.asarray(a["shift_mu"][0])
    mu_gf = np.zeros(P, np.float32)
    mu_gf[0:32] = mu[1536 + 256:]
    f_bias = np.zeros(P, np.float32)
    f_bias[32:40] = a["fox_forget_bias"][0]
    v = {
        "attn_pre": a["attn_norm_pre"], "attn_post": a["attn_norm_post"],
        "mu": np.concatenate([mu_gf, mu[1536:1536 + 256], mu[0:1536]]),
        "w0": a["rwkv_w0"], "a0": a["rwkv_a0"], "k_k": a["rwkv_k_k"], "k_a": a["rwkv_k_a"], "r_k": a["rwkv_r_k"],
        "ln_w": a["rwkv_ln_w"], "ln_b": a["rwkv_ln_b"], "ffn_pre": a["ffn_norm_pre"], "ffn_post": a["ffn_norm_post"],
        "mix_norm": a["norm_mix_w_2"], "lb0": a["hg_lower_bounds_2"][0], "lb1": a["hg_lower_bounds_2"][1],
        "hg_norm": a["hg_norm_w_2"], "ffn_norm": a["norm_ffn_w_2"], "final_norm": a["final_norm_w_2"], "f_bias": f_bias,
        "eps": np.full(P, 1e-6, np.float32), "ln_eps": np.full(P, 64e-5, np.float32),
    }
    return np.ascontiguousarray(np.concatenate([col(v[n]) for n, _ in PARAMS], axis=1))


def kernel(**inputs):
    import concourse.bacc as bacc
    from concourse.bass_utils import run_bass_kernel_spmd as run

    a = {n: np.asarray(v) for n, v in inputs.items()}
    table, select, rotary, decay = _constants()
    low_rank = np.zeros((P, 3, T), np.float32)
    low_rank[0:64, 0] = a["rwkv_w_up"][0]
    low_rank[64:128, 0] = a["rwkv_a_up"][0]
    low_rank[:, 1] = a["rwkv_g_up"][0][0:128]
    low_rank[0:32, 2] = a["rwkv_g_up"][0][128:160]
    arrays = {
        "x_t": np.ascontiguousarray(a["x"][0].T), "parameters": _parameters(a), "constants": table, "selectors": select,
        "rotary": rotary, "ret_decay": decay, "low_rank": low_rank, "weights": _stream(a),
    }
    nc = bacc.Bacc("TRN2", target_bir_lowering=False, num_devices=1)
    args = [nc.dram_tensor(n, v.shape, F32, kind="ExternalInput").ap() for n, v in arrays.items()]
    gates = nc.dram_tensor("gates", (NTG, P, NKEY * TG), F32, kind="Internal").ap()
    out = nc.dram_tensor("out_t", (D, T), F32, kind="ExternalOutput").ap()
    build(nc, *args, gates, out)
    r = run(nc, [arrays], core_ids=[0])
    return np.ascontiguousarray(r.results[0]["out_t"].T)[None]
```

```python
from contextlib import ExitStack

import numpy as np
import concourse.bass as bass
from concourse import mybir

ALU = mybir.AluOpType
ACT = mybir.ActivationFunctionType
AX = mybir.AxisListType
F32 = mybir.dt.float32
F32R = mybir.dt.float32r
U32 = mybir.dt.uint32

P = 128
T = 512
D = 1024
KD = D // P
TT = T // P
C = 64
NCH = T // C
HD = 64
NPAIR = 4
FF = 2816
KF = FF // P
HG_H, HG_D = 8, 128
RET_H, RET_DK, RET_DV = 4, 256, 512
PEER_H, PEER_K, NKEY = 8, 16, 128
TG = 32
NTG = T // TG
JG = 8
NJG = NKEY // JG
RING = 4
NBANK = 4
MID = C // 2 - 1
NEG = -1.0e30
E_HALF = float(np.exp(-0.5))

N_FOX = 13
N_RW = 14
B_FOX = 0
B_RW = B_FOX + N_FOX
B_WOUT = B_RW + N_RW
B_FFN = B_WOUT + KD
B_DOWN = B_FFN + 2 * KF
B_HG = B_DOWN + 3 * KD
B_RET = B_HG + 4 * HG_H
B_MERGE = B_RET + 12 * RET_H
B_WOUT2 = B_MERGE + 5 * KD
B_PQ = B_WOUT2 + KD
B_U = B_PQ + 2 * PEER_H
B_V = B_U + NKEY
N_BLOCKS = B_V + NKEY
NU_ROUTE = 12
NU_GATES = 4
NU_REST = NKEY - NU_ROUTE * TT - NU_GATES * NTG
N_LOADED = -(-N_BLOCKS // RING) * RING

PARAMS = [("attn_pre", 8), ("attn_post", 8), ("mu", 15), ("w0", 4), ("a0", 4), ("k_k", 4), ("k_a", 4),
          ("r_k", 4), ("ln_w", 4), ("ln_b", 4), ("ffn_pre", 8), ("ffn_post", 8), ("mix_norm", 8),
          ("lb0", 8), ("lb1", 8), ("hg_norm", 8), ("ffn_norm", 8), ("final_norm", 8), ("f_bias", 1),
          ("eps", 1), ("ln_eps", 1)]
PCOL, NPAR = {}, 0
for _n, _w in PARAMS:
    PCOL[_n] = NPAR
    NPAR += _w

CONSTS = [("ident", 128), ("ones", 128), ("bones", 128), ("bmean", 128), ("strict_T", 128),
          ("strict", 128), ("incl_T", 128), ("neg", 128), ("iota", 128), ("reset", 512)]
CCOL, NCST = {}, 0
for _n, _w in CONSTS:
    CCOL[_n] = (NCST, _w)
    NCST += _w


class Steps:

    def __init__(self, eng, sem):
        self.eng, self.sem, self.n, self.loop = eng, sem, 0, 0

    def go(self, ins):
        self.n += 1
        ins.then_inc(self.sem, 1)

    def sync(self):
        self.eng.wait_ge(self.sem, self.n + self.loop)

    def __call__(self, ins):
        self.go(ins)
        self.sync()

    def enter(self, it, per, count):
        self.loop, self.at, self.per, self.count = it * per, self.n, per, count

    def leave(self):
        assert self.n - self.at == self.per, (self.n - self.at, self.per)
        self.n = self.at + self.per * self.count
        self.loop = 0


def build(nc, xt, par_d, cst_d, sel_d, rot_d, rmask_d, small_d, keys_d, wstream, gates_d, hidden_d, out):
    with ExitStack() as ctx:
        def sb(name, shape, dt=F32):
            return ctx.enter_context(nc.sbuf_tensor(name, shape, dt))

        def sem(name):
            return ctx.enter_context(nc.semaphore(name))

        NT = 75
        arena = sb("arena", [P, NT, T])
        base = nc.sbuf_base - NT * T * 4

        def over(name, first, tiles, dt=F32R):
            return nc.alloc_sbuf_tensor_at(name, [P, tiles, T], dt, offset=base + first * T * 4)

        xs = over("xs", 0, 2 * KD)
        hid = over("hid", 22, 2 * KF)
        o_hi = over("o_hi", 51, 24)
        o_lo = over("o_lo", 27, 24)
        gw = over("gw", 0, 4 * JG)
        spl = over("spl", 22, 2)
        gu = over("gate_up", 16, 6, F32)
        xres = sb("xres", [P, KD, T])
        ring = sb("ring", [P, RING, D])
        ring_hi = sb("ring_hi", [P, 2, D], F32R)
        ring_lo = sb("ring_lo", [P, 2, D], F32R)
        par = sb("par", [P, NPAR])
        cst = sb("cst", [P, NCST])
        bank = [ctx.enter_context(nc.psum_tensor(f"bank{b}", [P, 512], F32)) for b in range(8)]
        stat = sb("stat", [P, 96])
        lbt = sb("lbt", [P, 4, 8])
        dch = sb("dch", [P, 6, 4 * NCH])

        def tile(i):
            return arena[:, i, :]

        def cc(name):
            a, w = CCOL[name]
            return cst[:, a:a + w]

        def pp(name, i=0):
            return par[:, PCOL[name] + i:PCOL[name] + i + 1]

        def mask4(name):
            return cc(name).unsqueeze(1).to_broadcast([P, 4, 128])

        def small(a, n, dt=None):
            ap = arena[:, 64:68, :].rearrange("p a b -> p (a b)")[:, a:a + n]
            return ap if dt is None else ap.bitcast(dt)

        topv = small(0, 256).rearrange("p (n k) -> p n k", n=16)
        topi = small(256, 256, U32).rearrange("p (n k) -> p n k", n=16)
        topf = small(512, 256).rearrange("p (n k) -> p n k", n=16)
        bestv = small(768, 128).rearrange("p (h k) -> p h k", h=8)
        besti = small(896, 128, U32).rearrange("p (h k) -> p h k", h=8)
        bests = small(1024, 128, U32).rearrange("p (h k) -> p h k", h=8)
        bestf = small(1152, 256).rearrange("p (s h k) -> p s h k", s=2, h=8)
        pairs = small(1408, 384).rearrange("p (j n) -> p j n", j=3)
        gsum = small(1792, 16).rearrange("p (s h) -> p s h", s=2)
        oneA = arena[:, 68:70, :].rearrange("p u (j n) -> p u j n", j=4)
        oneB = arena[:, 70:72, :].rearrange("p u (j n) -> p u j n", j=4)

        def v4(ap):
            return ap.rearrange("p (g t) -> p g t", g=4)

        def ch(ap):
            return ap.rearrange("p (c t) -> p c t", t=C)

        loaded = [sem(f"loaded{r}") for r in range(RING)]
        block_used = sem("block_used")
        evac = sem("evac")
        in_x, in_par, in_cst, in_small = sem("in_x"), sem("in_par"), sem("in_cst"), sem("in_small")
        in_rot = sem("in_rot")
        act_s, dve_s, pe_s = sem("act_steps"), sem("dve_steps"), sem("pe_steps")
        sq_ready, sum_ready, root_ready = sem("squares_ready"), sem("sums_ready"), sem("root_ready")
        sq_used = sem("squares_used")
        root_used = sem("root_used")
        fc_z, fc_ln = sem("forget_z"), sem("forget_ln")
        cum_ready, exp_ready, hg_exp = sem("decays_cumulated"), sem("decays_exp"), sem("hg_chunk_decays")
        lb_ready = sem("lower_bound")
        tk_sub, tk_exp = sem("route_shifted"), sem("route_exp")
        w_split = sem("weights_split")
        split_hi = sem("split_hi")
        scaled = sem("scaled")
        hi_ready = sem("hi_ready")
        xs_ready = sem("xs_ready")
        o_lo_ready, o_ready = sem("branch_lo"), sem("branch_split")
        resid_ready = sem("resid_ready")
        shifted = sem("shifted")
        ffn_pair = sem("ffn_pair")
        fc_ready, vt_ready, vt_out = sem("fox_cum_ready"), sem("fox_vt_psum"), sem("fox_v_tokens")
        fs_ready, fmax, fexp, fnorm = sem("fox_scores"), sem("fox_max"), sem("fox_exp"), sem("fox_probs")
        ft_ready, ft_out, fo_ready, fo_out = sem("fox_pT_psum"), sem("fox_pT"), sem("fox_out_psum"), sem("fox_out")
        rw_pe, rw_act, rw_dve = sem("rwkv_products"), sem("rwkv_act"), sem("rwkv_dve")
        hg_pe, hg_act, hg_dve = sem("hg_products"), sem("hg_act"), sem("hg_dve")
        rt_pe, rt_act, rt_dve = sem("ret_products"), sem("ret_act"), sem("ret_dve")
        mg_dve = sem("merged")
        tk_pe, tk_act, tk_dve = sem("route_products"), sem("route_act"), sem("route_dve")
        oh_dve, oh_pe, oh_act = sem("onehots"), sem("gate_psum"), sem("gate_tokens")
        gst = [sem("gates_stored0"), sem("gates_stored1")]
        hst = [sem("hidden_stored0"), sem("hidden_stored1")]
        gld = [sem("group_loaded0"), sem("group_loaded1")]
        in_keys = sem("in_keys")
        ex_prod, ex_hi, ex_lo = sem("gated_hidden"), sem("gated_hi"), sem("gated_lo")
        ex_acc = sem("accumulated")
        out_ready, stored = sem("out_ready"), sem("stored")

        def xr(k):
            return xres[:, k, :]

        XS = [(xs[:, k, :], xs[:, KD + k, :]) for k in range(KD)]
        GW = [[(gw[:, 16 * (1 - b) + j, :], gw[:, 16 * (1 - b) + JG + j, :]) for j in range(JG)] for b in range(2)]
        HID = [(hid[:, k, :], hid[:, KF + k, :]) for k in range(KF)]
        OHL = [(o_hi[:, k, :], o_lo[:, k, :]) for k in range(24)]
        TA, TR, TB, TK = 0, 4, 8, 12
        Q0, K0, VF0, VT0 = 16, 20, 24, 28
        RR, RK, RV, LAT, GL, GFT, RAW = 32, 36, 40, 44, 45, 46, 47
        DTMP = 49
        RA, LW, RG, KKT, BON, OF = 50, 54, 58, 24, 66, 62
        EL = 16
        MA, MB, MK, MV = 16, 20, 24, 28
        WT, U0, UU, SH = 32, 36, 54, 50
        HS = [[40, 41, 42, 43, 44, 45, 46, 47], [48, 49, 70, 71, 72, 73, 74, 50]]
        ORW = 66
        SMALL, SELT = 72, 70
        PT0, PR0 = 66, 68
        NORM = [(60, 62, 63), (66, 68, 69), (66, 68, 16), (16, 18, 19), (16, 18, 19), (16, 18, 19), (32, 34, 35)]
        MO = [None, 24, None, 66]
        YY = 16
        HGT = dict(F=16, LF=17, K=18, CU=19, CC=20, EP=21, EM=22, I=23, G=24, Q=25, KD=26, QD=27, IT=28, KT=29,
                   AM=30, SQ=31, RT=32, R2=33, X=34, S=lambda c: tile(35 + c // 4)[:, (c % 4) * P:(c % 4 + 1) * P])
        OHG, ORET = 51, 59
        RTT = dict(Q=16, K=18, VF=20, QR=24, KR=26, VT=28, AM=32, T=32, SQ=36, RT=37, R2=38, G=39, COS=43, MASK=45)
        MRG, MGT = 16, 24
        WO2 = 27
        PQ, PSUB = 32, 28
        PST, PBIG, PTT = 48, 20, 28
        UT = 72
        GBUF = 32
        HV, GV, ACC, OUT = 32, 48, 64, 40
        RW_PE, RW_ACT, RW_DVE = 28, 16, 12

        block = ctx.enter_context(nc.Block())

        @block.sync
        def _(sp):
            for r in range(RING):
                sp.dma_start(ring[:, r, :], wstream[r]).then_inc(loaded[r], 16)
            with sp.Fori(1, N_LOADED // RING) as i:
                for r in range(RING):
                    sp.wait_ge(w_split, i * RING + (r + 1 - RING))
                    sp.dma_start(ring[:, r, :], wstream[bass.ds(i * RING + r, 1)].rearrange("a p n -> (a p) n")
                                 ).then_inc(loaded[r], 16)
            sp.wait_ge(out_ready, KD)
            sp.dma_start(out.rearrange("(k p) t -> p k t", p=P), arena[:, OUT:OUT + KD, :]).then_inc(stored, 16)
            sp.wait_ge(stored, 16)

        @block.tensor
        def _(pe):
            st = Steps(pe, pe_s)
            q_at = [0]

            def ready(n, it=0, per=0):
                pe.wait_ge(w_split, it * per + (n + 1))

            def three(out_, n, k, x, start, stop):
                wh, wl = ring_hi[:, n % 2, k * P:(k + 1) * P], ring_lo[:, n % 2, k * P:(k + 1) * P]
                pe.matmul(out_, wh, x[0], start=start, stop=False, skip_group_check=True)
                pe.matmul(out_, wh, x[1], start=False, stop=False, skip_group_check=True)
                return pe.matmul(out_, wl, x[0], start=False, stop=stop, skip_group_check=True)

            def product(q, blocks, rhs, it=0, per_q=0, per_n=0, chunk_wait=None):
                if q >= NBANK:
                    pe.wait_ge(evac, it * per_q + q - NBANK + 1)
                k = 0
                total = sum(c for _, c in blocks)
                for n, c in blocks:
                    ready(n, it, per_n)
                    for j in range(c):
                        if chunk_wait is not None:
                            chunk_wait(k)
                        mm = three(bank[q % NBANK][:, :], n, j, rhs[k], k == 0, k == total - 1)
                        k += 1
                    mm.then_inc(block_used, 1)

            def norm_sums(i, parts, mat="ones"):
                for k in range(parts):
                    pe.wait_ge(sq_ready, KD * i + k + 1)
                    mm = pe.matmul(bank[4][:, :], cc(mat), tile(NORM[i][0] + k % 2), start=(k == 0), stop=(k == parts - 1))
                    if k < parts - 1:
                        mm.then_inc(sq_used, 1)
                mm.then_inc(sum_ready, 1)

            pe.wait_ge(in_cst, 16)
            norm_sums(0, KD)
            pe.wait_ge(xs_ready, KD)
            for n in range(N_FOX + N_RW):
                product(n, [(n, KD)], XS)
            q = N_FOX + N_RW

            for s in range(TT):
                pe.wait_ge(evac, 12)
                for m in range(NPAIR):
                    tr = pe.transpose(bank[4 + s][:, m * P:(m + 1) * P], tile(VF0 + m)[:, s * P:(s + 1) * P], cc("ident"))
                tr.then_inc(vt_ready, 1)
            units = [(h, t) for h in range(8) for t in range(TT)]

            def fox_scores(u):
                h, t = units[u]
                m, e = h // 2, h % 2
                n = (t + 1) * P
                b = bank[u % 2]
                if u == 0:
                    pe.wait_ge(evac, q)
                    pe.wait_ge(fc_ready, 1)
                    pe.wait_ge(in_small, 32)
                if u >= 2:
                    pe.wait_ge(fexp, u - 1)
                    pe.wait_ge(fmax, u - 1)
                rows = slice(e * HD, (e + 1) * HD)
                pe.matmul(b[:, 0:n], tile(Q0 + m)[rows, t * P:(t + 1) * P], tile(K0 + m)[rows, 0:n],
                          start=True, stop=False, skip_group_check=True)
                pe.matmul(b[:, 0:n], arena[32:40, SELT:SELT + 2, :].rearrange("p a b -> p (a b)")[:, h * P:(h + 1) * P],
                          tile(GFT)[32:40, 0:n], start=False, stop=False, skip_group_check=True)
                pe.matmul(b[:, t * P:n], cc("ident"), cc("neg"), start=False, stop=True,
                          skip_group_check=True).then_inc(fs_ready, 1)

            def fox_out(u):
                h, t = units[u]
                m, e = h // 2, h % 2
                bt, bo = bank[2 + u % 2], bank[4 + m % 2]
                pe.wait_ge(fnorm, u + 1)
                if u >= 2:
                    pe.wait_ge(ft_out, u - 1)
                for s in range(t + 1):
                    tr = pe.transpose(bt[:, s * P:(s + 1) * P], tile(PR0 + u % 2)[:, s * P:(s + 1) * P], cc("ident"))
                tr.then_inc(ft_ready, 1)
                pe.wait_ge(ft_out, u + 1)
                if u == 0:
                    pe.wait_ge(vt_out, TT)
                if e == 0 and t == 0 and m >= 2:
                    pe.wait_ge(fo_out, m - 1)
                for s in range(t + 1):
                    mm = pe.matmul(bo[e * HD:(e + 1) * HD, t * P:(t + 1) * P], tile(VT0 + s)[:, h * HD:(h + 1) * HD],
                                   tile(PT0 + u % 2)[:, s * P:(s + 1) * P], start=(s == 0), stop=(s == t),
                                   skip_group_check=True)
                mm.then_inc(fo_ready, 1)

            fox_scores(0)
            for u in range(len(units)):
                if u + 1 < len(units):
                    fox_scores(u + 1)
                fox_out(u)

            su = arena[:, SMALL:SMALL + 3, :]
            pe.wait_ge(in_small, 32)
            pe.wait_ge(fo_out, NPAIR)
            pe.wait_ge(rw_act, 3)
            for m in range(NPAIR):
                cols = slice(m * P, (m + 1) * P)
                if m >= 1:
                    pe.wait_ge(rw_act, 3 + 3 * m)
                pe.matmul(bank[0][:, :], su[0:64, 0, cols], tile(LAT)[0:64, :], start=True, stop=True).then_inc(rw_pe, 1)
                pe.matmul(bank[1][:, :], su[64:128, 0, cols], tile(LAT)[64:128, :], start=True, stop=True).then_inc(rw_pe, 1)
                pe.matmul(bank[2][:, :], su[:, 1, cols], tile(GL), start=True, stop=False)
                pe.matmul(bank[2][:, :], su[0:32, 2, cols], tile(GFT)[0:32, :], start=False, stop=True).then_inc(rw_pe, 1)
            for m in range(NPAIR):
                pe.wait_ge(rw_act, 16 + 2 * m)
                pe.matmul(bank[4][:, :], cc("bones"), tile(DTMP), start=True, stop=True).then_inc(rw_pe, 1)
                pe.wait_ge(rw_dve, 2 * m + 1)
                pe.matmul(bank[5][:, :], cc("bones"), tile(RAW), start=True, stop=True).then_inc(rw_pe, 1)
            pe.wait_ge(rw_dve, 8)
            for i, (src, _) in enumerate(((TA, MA), (TB, MB), (TK, MK), (RV, MV))):
                for m in range(NPAIR):
                    j = 4 * i + m
                    if j >= 2:
                        pe.wait_ge(rw_act, 23 + j - 1)
                    for g in range(TT):
                        tr = pe.transpose(bank[j % 2][:, g * P:(g + 1) * P], tile(src + m)[:, g * P:(g + 1) * P], cc("ident"))
                    tr.then_inc(rw_pe, 1)
            for m in range(NPAIR):
                for e in range(2):
                    rows = slice(e * HD, (e + 1) * HD)
                    if m == 0:
                        pe.wait_ge(rw_act, 39)
                    else:
                        pe.wait_ge(rw_act, 39 + RW_ACT * m)
                        pe.wait_ge(rw_dve, 8 + RW_DVE * m)
                    b0 = 3 * e
                    for k, (l, r) in enumerate(((TA, TB), (TB, TA), (TK, TA))):
                        for g in range(TT):
                            cols = slice(g * P, (g + 1) * P)
                            mm = pe.matmul(bank[b0 + k][:, cols], tile(l + m)[rows, cols], tile(r + m)[rows, cols],
                                           start=True, stop=True, skip_group_check=True)
                    mm.then_inc(rw_pe, 1)
                for lev in range(5):
                    for e in range(2):
                        hs, b0 = HS[e], 3 * e
                        a, b = (0, 1) if lev % 2 == 0 else (1, 0)
                        pe.wait_ge(rw_dve, 8 + RW_DVE * m + 2 * lev + e + 1)
                        for g in range(TT):
                            cols = slice(g * P, (g + 1) * P)
                            pe.matmul(bank[b0][:, cols], tile(hs[2 + a])[:, cols], tile(hs[a])[:, cols],
                                      start=True, stop=True, skip_group_check=True)
                            mm = pe.matmul(bank[b0 + 1][:, cols], tile(hs[a])[:, cols], tile(hs[2 + a])[:, cols],
                                           start=True, stop=True, skip_group_check=True)
                        mm.then_inc(rw_pe, 1)
                    for e in range(2):
                        hs, b0 = HS[e], 3 * e
                        a, b = (0, 1) if lev % 2 == 0 else (1, 0)
                        pe.wait_ge(rw_act, 39 + RW_ACT * m + 2 * lev + e + 1)
                        for g in range(TT):
                            cols = slice(g * P, (g + 1) * P)
                            mm = pe.matmul(bank[b0 + 2][:, cols], tile(hs[b])[:, cols], tile(hs[4 + a])[:, cols],
                                           start=True, stop=True, skip_group_check=True)
                        mm.then_inc(rw_pe, 1)
                for e in range(2):
                    hs, b0 = HS[e], 3 * e
                    cols_h = slice(e * HD, (e + 1) * HD)
                    pe.wait_ge(rw_dve, 8 + RW_DVE * m + 10 + e + 1)
                    for g in range(TT):
                        mm = pe.matmul(bank[b0][:, g * HD:(g + 1) * HD], tile(hs[6])[:, g * P:(g + 1) * P],
                                       v4(tile(MV + m))[:, g, cols_h], start=True, stop=True, skip_group_check=True)
                    mm.then_inc(rw_pe, 1)
                    for g in range(TT):
                        mm = pe.matmul(bank[b0 + 1][e * HD:(e + 1) * HD, g * P:(g + 1) * P], v4(tile(MA + m))[:, g, cols_h],
                                       tile(hs[5])[:, g * P:(g + 1) * P], start=True, stop=True, skip_group_check=True)
                    mm.then_inc(rw_pe, 1)
                for e in range(2):
                    hs, b0 = HS[e], 3 * e
                    pe.wait_ge(rw_act, 39 + RW_ACT * m + 10 + 2 * e + 1)
                    for g in range(TT):
                        mm = pe.matmul(bank[b0 + 2][:, g * HD:(g + 1) * HD], tile(hs[5])[:, g * P:(g + 1) * P],
                                       tile(hs[7])[:, g * HD:(g + 1) * HD], start=True, stop=True, skip_group_check=True)
                    mm.then_inc(rw_pe, 1)
            base_pe, base_act, base_dve = 36 + RW_PE * 4, 39 + RW_ACT * 4, 8 + RW_DVE * 4
            shv = arena[:, SH:SH + 4, :].rearrange("p a b -> p (a b)").rearrange("p (c n) -> p c n", c=NCH)
            for c in range(NCH):
                g, p = c // 2, c % 2
                trow = slice(p * HD, (p + 1) * HD)
                if c == 0:
                    pe.wait_ge(rw_act, base_act)
                    pe.wait_ge(rw_dve, base_dve)
                if c > 0:
                    pe.wait_ge(rw_dve, base_dve + 2 * c)
                    for h in range(8):
                        m, e = h // 2, h % 2
                        rows = slice(e * HD, (e + 1) * HD)
                        mm = pe.matmul(bank[6 - e][trow, m * HD:(m + 1) * HD], tile(WT + m)[rows, c * C:(c + 1) * C],
                                       shv[rows, c, m * HD:(m + 1) * HD], start=True, stop=True, skip_group_check=True)
                    mm.then_inc(rw_pe, 1)
                if c == NCH - 1:
                    continue
                pe.wait_ge(rw_dve, base_dve + 2 * c + 1)
                for h in range(8):
                    m, e = h // 2, h % 2
                    rows = slice(e * HD, (e + 1) * HD)
                    dst = bank[7][rows, m * HD:(m + 1) * HD]
                    pe.matmul(dst, v4(tile(MK + m))[trow, g, rows], v4(tile(MV + m))[trow, g, rows],
                              start=True, stop=False, skip_group_check=True)
                    mm = pe.matmul(dst, v4(tile(MB + m))[trow, g, rows], tile(UU + g)[trow, h * HD:(h + 1) * HD],
                                   start=False, stop=True, skip_group_check=True)
                mm.then_inc(rw_pe, 1)
            bp, bd, ba = base_pe + 14, base_dve + 15, base_act
            pe.wait_ge(rw_dve, bd)
            for h in range(8):
                m, e = h // 2, h % 2
                rows = slice(e * HD, (e + 1) * HD)
                if h >= 1:
                    pe.wait_ge(rw_dve, bd + 2 * h)
                for k, l in enumerate((TK, TB)):
                    for g in range(TT):
                        cols = slice(g * P, (g + 1) * P)
                        mm = pe.matmul(bank[k][:, cols], tile(l + m)[rows, cols], tile(TR + m)[rows, cols],
                                       start=True, stop=True, skip_group_check=True)
                    mm.then_inc(rw_pe, 1)
                pe.wait_ge(rw_dve, bd + 2 * h + 2)
                hs = HS[h % 2]
                yb = bank[4 + m % 2]
                if e == 0 and m >= 2:
                    pe.wait_ge(rw_act, ba + m - 1)
                for g in range(TT):
                    cols = slice(g * P, (g + 1) * P)
                    pe.matmul(yb[rows, cols], v4(tile(MV + m))[:, g, rows], tile(hs[0])[:, cols],
                              start=True, stop=False, skip_group_check=True)
                    mm = pe.matmul(yb[rows, cols], tile(UU + g)[:, h * HD:(h + 1) * HD], tile(hs[1])[:, cols],
                                   start=False, stop=False, skip_group_check=True)
                    for c in (2 * g, 2 * g + 1):
                        if c:
                            mm = pe.matmul(yb[rows, c * C:(c + 1) * C], shv[rows, c, m * HD:(m + 1) * HD],
                                           tile(TR + m)[rows, c * C:(c + 1) * C], start=False, stop=(c % 2 == 1),
                                           skip_group_check=True)
                mm.then_inc(rw_pe, 1)
            bp, bd = bp + 24, bd + 16
            ba += 4
            for m in range(NPAIR):
                pe.wait_ge(rw_act, ba + 2 * m)
                if m:
                    pe.wait_ge(rw_dve, bd + 2 * m)
                pe.matmul(bank[0][:, :], cc("bmean"), tile(YY + m), start=True, stop=True).then_inc(rw_pe, 1)
                pe.wait_ge(rw_act, ba + 2 * m + 1)
                pe.matmul(bank[1][:, :], cc("bmean"), tile(HS[0][0]), start=True, stop=True).then_inc(rw_pe, 1)
            bp, bd, ba = bp + 8, bd + 8, ba + 8

            pe.wait_ge(xs_ready, 2 * KD)
            for k in range(KD):
                product(q, [(B_WOUT + k, KD)], XS)
                q += 1
            norm_sums(1, KD)
            norm_sums(2, KD)
            pe.wait_ge(xs_ready, 3 * KD)
            with pe.Fori(0, KF // 2) as i:
                for j in range(4):
                    product(q + j, [(B_FFN + j, KD)], XS, i, 4, 4)
            q += 2 * KF
            pe.wait_ge(ffn_pair, KF + 2)
            for k in range(KD):
                n = B_DOWN + 3 * k
                product(q, [(n, 8), (n + 1, 8), (n + 2, KF - 16)], HID)
                q += 1
            norm_sums(3, KD)
            norm_sums(4, KD)

            pe.wait_ge(xs_ready, 4 * KD)
            H_ = HGT
            with pe.Fori(0, HG_H) as h:
                for j in range(4):
                    product(q + j, [(B_HG + j, KD)], XS, h, 4, 4)
                pe.wait_ge(evac, h * 4 + q + 2)
                for g in range(TT):
                    tr = pe.transpose(bank[4][:, g * P:(g + 1) * P], tile(H_["I"])[:, g * P:(g + 1) * P], cc("ident"))
                tr.then_inc(hg_pe, 1)
                pe.wait_ge(hg_dve, h * 6 + 4)
                for g in range(TT):
                    tr = pe.transpose(bank[5][:, g * P:(g + 1) * P], tile(H_["KD"])[:, g * P:(g + 1) * P], cc("ident"))
                tr.then_inc(hg_pe, 1)
                for g in range(TT):
                    cols = slice(g * P, (g + 1) * P)
                    mm = pe.matmul(bank[6][:, cols], tile(H_["KD"])[:, cols], tile(H_["QD"])[:, cols],
                                   start=True, stop=True, skip_group_check=True)
                mm.then_inc(hg_pe, 1)
                pe.wait_ge(hg_act, h * 6 + 4)
                for c in range(NCH - 1):
                    rows = slice((c % 2) * C, (c % 2 + 1) * C)
                    mm = pe.matmul(bank[4 + c % 2][:, (c // 2) * P:(c // 2 + 1) * P], v4(tile(H_["KT"]))[rows, c // 2, :],
                                   v4(tile(H_["IT"]))[rows, c // 2, :], start=True, stop=True, skip_group_check=True)
                mm.then_inc(hg_pe, 1)
                pe.wait_ge(hg_dve, h * 6 + 6)
                for g in range(TT):
                    cols = slice(g * P, (g + 1) * P)
                    pe.matmul(bank[7][:, cols], v4(tile(H_["IT"]))[:, g, :], tile(H_["AM"])[:, cols],
                              start=True, stop=False, skip_group_check=True)
                    for c in (2 * g, 2 * g + 1):
                        if c:
                            mm = pe.matmul(bank[7][:, c * C:(c + 1) * C], H_["S"](c), tile(H_["QD"])[:, c * C:(c + 1) * C],
                                           start=False, stop=(c % 2 == 1), skip_group_check=True)
                mm.then_inc(hg_pe, 1)
                pe.wait_ge(hg_act, h * 6 + 5)
                pe.matmul(bank[6][:, :], cc("ones"), tile(H_["SQ"]), start=True, stop=True).then_inc(hg_pe, 1)
            q += 4 * HG_H
            R_ = RTT
            with pe.Fori(0, RET_H) as h:
                for j in range(8):
                    product(q + j, [(B_RET + j, KD)], XS, h, 12, 12)
                for s in range(TT):
                    pe.wait_ge(evac, h * 12 + q + 8)
                    if s >= 1:
                        pe.wait_ge(rt_act, h * 9 + s)
                    for j in range(4):
                        tr = pe.transpose(bank[4][:, j * P:(j + 1) * P], tile(R_["VF"] + j)[:, s * P:(s + 1) * P], cc("ident"))
                    tr.then_inc(rt_pe, 1)
                for s in range(TT):
                    if s == 0:
                        pe.wait_ge(rt_dve, h * 12 + 1 + 4)
                    if s >= 2:
                        pe.wait_ge(rt_dve, h * 12 + 1 + 4 + s - 1)
                    b = bank[5 + s % 2]
                    n = T - s * P
                    for j in range(2):
                        mm = pe.matmul(b[:, 0:n], tile(R_["KR"] + j)[:, s * P:(s + 1) * P], tile(R_["QR"] + j)[:, s * P:T],
                                       start=(j == 0), stop=(j == 1))
                    mm.then_inc(rt_pe, 1)
                for j in range(4):
                    if j == 0:
                        pe.wait_ge(rt_dve, h * 12 + 1 + 8)
                        pe.wait_ge(rt_act, h * 9 + 4)
                    if j >= 1:
                        pe.wait_ge(rt_act, h * 9 + 4 + j)
                    for t in range(TT):
                        for s in range(t + 1):
                            mm = pe.matmul(bank[7][:, t * P:(t + 1) * P], tile(R_["VT"] + s)[:, j * P:(j + 1) * P],
                                           tile(R_["AM"] + s)[:, (t - s) * P:(t - s + 1) * P], start=(s == 0), stop=(s == t),
                                           skip_group_check=True)
                    mm.then_inc(rt_pe, 1)
                    pe.wait_ge(rt_act, h * 9 + 5 + j)
                    pe.matmul(bank[4][:, :], cc("ones"), tile(R_["SQ"]), start=(j == 0), stop=(j == 3)).then_inc(rt_pe, 1)
                for j in range(8, 12):
                    product(q + j, [(B_RET + j, KD)], XS, h, 12, 12)
            q += 12 * RET_H
            for k in range(KD):
                n = B_MERGE + 5 * k
                product(q, [(n, KD)], XS)
                product(q + 1, [(n + 1, KD)], XS)
                product(q + 2, [(n + 2, KD)], OHL[:8], chunk_wait=(lambda c: pe.wait_ge(o_ready, c + 1)) if k == 0 else None)
                product(q + 3, [(n + 3, KD), (n + 4, KD)], OHL[8:],
                        chunk_wait=(lambda c: pe.wait_ge(o_ready, 8 + c + 1)) if k == 0 else None)
                q += 4
            pe.wait_ge(xs_ready, 5 * KD)
            for k in range(KD):
                product(q, [(B_WOUT2 + k, KD)], XS)
                q += 1
            norm_sums(5, KD)
            pe.wait_ge(xs_ready, 6 * KD)
            for k in range(2 * PEER_H):
                product(q, [(B_PQ + k, KD)], XS)
                q += 1
            pe.wait_ge(evac, q)
            pe.wait_ge(in_keys, 16)
            keys = arena[:, PSUB:PSUB + 4, :].rearrange("p a b -> p (a b)")
            for t in range(TT):
                for n in range(16):
                    if t and n % 4 == 0:
                        pe.wait_ge(tk_act, 4 * (t - 1) + n // 4 + 1)
                    mm = pe.matmul(bank[4 + n // 4][:, (n % 4) * P:(n % 4 + 1) * P], tile(PQ + n)[:, t * P:(t + 1) * P],
                                   keys[:, n * P:(n + 1) * P], start=True, stop=True, skip_group_check=True)
                    if n % 4 == 3:
                        mm.then_inc(tk_pe, 1)
            with pe.Fori(0, TT) as t:
                for j in range(NU_ROUTE):
                    product(q + j, [(B_U + j, KD)], XS, t, NU_ROUTE, NU_ROUTE)
                pe.wait_ge(tk_dve, t + 1)
                pe.wait_ge(tk_act, t + 16)
                for j in range(3):
                    tr = pe.transpose(bank[4][:, j * P:(j + 1) * P], pairs[:, j, :], cc("ident"))
                tr.then_inc(tk_pe, 1)
            q += NU_ROUTE * TT
            n = B_U + NU_ROUTE * TT
            with pe.Fori(0, NTG // 2) as i:
                for b in range(2 * NU_GATES):
                    product(q + b, [(n + b, KD)], XS, i, 2 * NU_GATES, 2 * NU_GATES)
                    for u in (2 * b, 2 * b + 1):
                        pe.wait_ge(oh_dve, i * 16 + u + 1)
                        pe.wait_ge(oh_act, i * 16 + u + 1)
                        for j in range(4):
                            mm = pe.matmul(bank[5 + u % 2][:, j * P:(j + 1) * P], oneA[:, u % 2, j, :], oneB[:, u % 2, j, :],
                                           start=True, stop=True, skip_group_check=True)
                        mm.then_inc(oh_pe, 1)
            q += NU_GATES * NTG
            n += NU_GATES * NTG
            with pe.Fori(0, NU_REST // 4) as i:
                for b in range(4):
                    product(q + b, [(n + b, KD)], XS, i, 4, 4)
            q += NU_REST
            assert n + NU_REST == B_V

            def v_group(g, it=0):
                n = B_V + JG * g
                for half in range(2):
                    if g:
                        pe.wait_ge(ex_acc, it * 16 + 8 * (g - 1) + 4 * half + 4)
                    for b in range(4):
                        ready(n + 4 * half + b, it, 2 * JG)
                        for jj in range(2):
                            j = 2 * b + jj
                            if half == 0:
                                pe.wait_ge(ex_lo, it * 2 * JG + g * JG + j + 1)
                            for d in range(4):
                                mm = three(bank[4 * half + d][:, :], n + 4 * half + b, jj * 4 + d, GW[g % 2][j],
                                           j == 0, j == JG - 1)
                        mm.then_inc(block_used, 1)

            pe.wait_ge(evac, q)
            pe.wait_ge(oh_act, 8 * NTG + 2)
            v_group(0)
            v_group(1)
            with pe.Fori(0, NJG // 2 - 1) as i:
                v_group(2, i)
                v_group(3, i)
            norm_sums(6, KD)

        @block.scalar
        def _(act):
            st = Steps(act, act_s)
            nc_ = act

            def A(out_, in_, f, **kw):
                return act.activation(out_, in_, f, **kw)

            act.dma_start(xres[:, :, :], xt.rearrange("(k p) t -> p k t", p=P)).then_inc(in_x, 16)
            act.dma_start(par[:, :], par_d).then_inc(in_par, 16)
            act.dma_start(cst[:, :], cst_d).then_inc(in_cst, 16)
            act.dma_start(arena[:, SMALL:SMALL + 3, :], small_d).then_inc(in_small, 16)
            act.dma_start(arena[32:40, SELT:SELT + 2, :].rearrange("p a b -> p (a b)"), sel_d).then_inc(in_small, 16)
            act.wait_ge(in_par, 16)

            def norm_squares(i, src, first_wait):
                for k in range(KD):
                    first_wait(k)
                    if k >= 2:
                        act.wait_ge(sq_used, (KD - 1) * i + k - 1)
                    elif i:
                        act.wait_ge(root_used, i)
                    A(tile(NORM[i][0] + k % 2), src(k), ACT.Square).then_inc(sq_ready, 1)
                act.wait_ge(sum_ready, i + 1)
                A(tile(NORM[i][0]), bank[4][:, :], ACT.Sqrt, scale=1.0 / D, bias=pp("eps")).then_inc(root_ready, 1)

            def xs_hi(src, wait):
                for k in range(KD):
                    wait(k)
                    A(XS[k][0], src(k), ACT.Copy).then_inc(hi_ready, 1)

            def norm_hi(i, count):
                xs_hi(lambda k: tile(NORM[i][2] + k % 2), lambda k: act.wait_ge(scaled, count + k + 1))

            act.wait_ge(in_x, 16)
            norm_squares(0, xr, lambda k: None)
            norm_hi(0, 0)
            for n in range(N_FOX + N_RW):
                act.wait_ge(block_used, n + 1)
                if n < 12:
                    dst = tile((Q0, K0, VF0)[n // 4] + n % 4)
                else:
                    if n >= 14:
                        act.wait_ge(shifted, n - 13)
                    dst = tile(RAW + n % 2)
                A(dst, bank[n % NBANK][:, :], ACT.Copy).then_inc(evac, 1)
                if n == 12:
                    act.wait_ge(shifted, 1)
                    act.wait_ge(fc_z, 1)
                    z = arena[32:40, BON + 1, :]
                    st(A(z, z, ACT.Exp, scale=-1.0))
                    A(z, z, ACT.Ln, bias=1.0).then_inc(fc_ln, 1)
            q = N_FOX + N_RW
            act.wait_ge(shifted, N_RW + 1)
            A(tile(LAT)[0:64, :], tile(LAT)[0:64, :], ACT.Tanh).then_inc(rw_act, 1)
            A(tile(GL), tile(GL), ACT.Sigmoid).then_inc(rw_act, 1)
            A(tile(GFT)[0:32, :], tile(GFT)[0:32, :], ACT.Sigmoid).then_inc(rw_act, 1)
            for s in range(TT):
                act.wait_ge(vt_ready, s + 1)
                A(tile(VT0 + s), bank[4 + s][:, :], ACT.Copy).then_inc(vt_out, 1)

            units = [(h, t) for h in range(8) for t in range(TT)]

            def fox_exp(u):
                h, t = units[u]
                n = (t + 1) * P
                act.wait_ge(fmax, u + 1)
                if u >= 2:
                    act.wait_ge(ft_ready, u - 1)
                A(tile(PR0 + u % 2)[:, 0:n], bank[u % 2][:, 0:n], ACT.Exp, scale=0.125, bias=stat[:, 32 + u:33 + u],
                  accum_out=stat[:, 64 + u % 32:65 + u % 32]).then_inc(fexp, 1)

            def fox_copy(u):
                h, t = units[u]
                n = (t + 1) * P
                act.wait_ge(ft_ready, u + 1)
                if u >= 2:
                    act.wait_ge(fo_ready, u - 1)
                A(tile(PT0 + u % 2)[:, 0:n], bank[2 + u % 2][:, 0:n], ACT.Copy).then_inc(ft_out, 1)
                if h % 2 == 1 and t == TT - 1:
                    act.wait_ge(fo_ready, u + 1)
                    m = h // 2
                    A(tile(OF + m), bank[4 + m % 2][:, :], ACT.Copy).then_inc(fo_out, 1)

            fox_exp(0)
            for u in range(len(units)):
                if u + 1 < len(units):
                    fox_exp(u + 1)
                fox_copy(u)

            for m in range(NPAIR):
                act.wait_ge(rw_pe, 3 * m + 1)
                A(tile(LW + m), bank[0][:, :], ACT.Sigmoid, bias=pp("w0", m)).then_inc(rw_act, 1)
                act.wait_ge(rw_pe, 3 * m + 2)
                A(tile(RA + m), bank[1][:, :], ACT.Sigmoid, bias=pp("a0", m)).then_inc(rw_act, 1)
                act.wait_ge(rw_pe, 3 * m + 3)
                A(tile(RG + m), bank[2][:, :], ACT.Copy).then_inc(rw_act, 1)
            for m in range(NPAIR):
                if m:
                    act.wait_ge(rw_dve, 2 * m)
                A(tile(DTMP), tile(RK + m), ACT.Square, scale=pp("k_k", m)).then_inc(rw_act, 1)
                act.wait_ge(rw_pe, 12 + 2 * m + 1)
                A(tile(EL), bank[4][:, :], ACT.Sqrt).then_inc(rw_act, 1)
                act.wait_ge(cum_ready, m + 1)
                st.go(A(tile(EL + 4), tile(EL + 1), ACT.Exp))
                st.go(A(tile(EL + 5), tile(EL + 1), ACT.Exp, scale=-1.0))
                st.go(A(tile(EL + 6), tile(EL + 2), ACT.Exp))
                A(dch[:, 0, m * NCH:(m + 1) * NCH], ch(tile(EL + 3))[:, :, MID], ACT.Exp).then_inc(exp_ready, 1)
            for i, dst in enumerate((MA, MB, MK, MV)):
                for m in range(NPAIR):
                    act.wait_ge(rw_pe, 20 + 4 * i + m + 1)
                    A(tile(dst + m), bank[(4 * i + m) % 2][:, :], ACT.Copy).then_inc(rw_act, 1)
            for m in range(NPAIR):
                pb = 36 + RW_PE * m
                for lev in range(5):
                    for e in range(2):
                        hs, b0 = HS[e], 3 * e
                        b = 1 if lev % 2 == 0 else 0
                        act.wait_ge(rw_pe, pb + 2 + 4 * lev + e + 1)
                        A(tile(hs[b]), bank[b0][:, :], ACT.Copy).then_inc(rw_act, 1)
                for e in range(2):
                    hs, b0 = HS[e], 3 * e
                    act.wait_ge(rw_pe, pb + 22 + 2 * e + 1)
                    A(tile(hs[7])[:, 0:256], bank[b0][:, 0:256], ACT.Copy).then_inc(rw_act, 1)
                    act.wait_ge(rw_pe, pb + 22 + 2 * e + 2)
                    A(tile(WT + m)[e * HD:(e + 1) * HD, :], bank[b0 + 1][e * HD:(e + 1) * HD, :], ACT.Copy).then_inc(rw_act, 1)
                for e in range(2):
                    b0 = 3 * e
                    h = 2 * m + e
                    act.wait_ge(rw_pe, pb + 26 + e + 1)
                    A(arena[:, U0:U0 + 4, h * HD:(h + 1) * HD], bank[b0 + 2][:, 0:256].rearrange("p (g i) -> p g i", g=4),
                      ACT.Copy).then_inc(rw_act, 1)
            bp = 36 + RW_PE * 4 + 14
            ba = 39 + RW_ACT * 4
            for m in range(NPAIR):
                act.wait_ge(rw_pe, bp + 6 * m + 6)
                A(tile(YY + m), bank[4 + m % 2][:, :], ACT.Copy).then_inc(rw_act, 1)
            bp += 24
            ba += 4
            bd = 8 + RW_DVE * 4 + 15 + 16
            for m in range(NPAIR):
                act.wait_ge(rw_dve, bd + 2 * m + 1)
                A(tile(HS[0][0]), tile(HS[0][1]), ACT.Square).then_inc(rw_act, 1)
                act.wait_ge(rw_pe, bp + 2 * m + 2)
                A(tile(HS[0][2]), bank[1][:, :], ACT.Sqrt, bias=pp("ln_eps")).then_inc(rw_act, 1)

            xs_hi(lambda k: tile(OF + k if k < 4 else ORW + k - 4), lambda k: act.wait_ge(rw_dve, bd + 8))
            for k in range(KD):
                act.wait_ge(block_used, B_WOUT + k + 1)
                A(tile(MO[1] + k), bank[q % NBANK][:, :], ACT.Copy).then_inc(evac, 1)
                q += 1
            norm_squares(1, lambda k: tile(MO[1] + k), lambda k: act.wait_ge(evac, q))
            norm_squares(2, xr, lambda k: act.wait_ge(resid_ready, k + 1))
            norm_hi(2, KD)
            with act.Fori(0, KF // 2) as i:
                for j in range(4):
                    act.wait_ge(block_used, i * 4 + B_FFN + j + 1)
                    act.wait_ge(ffn_pair, i * 2 + j // 2 + 1)
                    A(gu[:, j, :], bank[(q + j) % NBANK][:, :], ACT.Silu if j % 2 == 0 else ACT.Copy).then_inc(evac, 1)
            q += 2 * KF
            act.wait_ge(ffn_pair, KF + 2)
            for k in range(KD):
                act.wait_ge(block_used, B_DOWN + 3 * (k + 1))
                A(tile(MO[3] + k), bank[q % NBANK][:, :], ACT.Copy).then_inc(evac, 1)
                q += 1
            norm_squares(3, lambda k: tile(MO[3] + k), lambda k: act.wait_ge(evac, q))
            norm_squares(4, xr, lambda k: act.wait_ge(resid_ready, KD + k + 1))

            H_ = HGT
            act.dma_start(arena[:, RTT["COS"]:RTT["COS"] + 2, :], rot_d).then_inc(in_rot, 16)
            act.dma_start(arena[:, RTT["MASK"]:RTT["MASK"] + 4, :], rmask_d).then_inc(in_rot, 16)
            act.wait_ge(lb_ready, 1)
            A(lbt[:, 1:3, :], lbt[:, 1:3, :], ACT.Exp).then_inc(lb_ready, 1)
            norm_hi(4, 2 * KD)
            with act.Fori(0, HG_H) as h:
                for j, (dst, f) in enumerate((("F", ACT.Sigmoid), ("I", ACT.Copy), ("G", ACT.Silu), ("Q", ACT.Copy))):
                    act.wait_ge(block_used, h * 4 + B_HG + j + 1)
                    act.wait_ge(hg_dve, h * 6 + 1)
                    A(tile(H_[dst]), bank[(q + j) % NBANK][:, :], f).then_inc(evac, 1)
                    if j == 1:
                        act.wait_ge(hg_dve, h * 6 + 2)
                        A(tile(H_["LF"]), tile(H_["F"]), ACT.Ln).then_inc(hg_act, 1)
                act.wait_ge(hg_dve, h * 6 + 3)
                A(dch[:, 4, 0:NCH], ch(tile(H_["CU"]))[:, :, MID], ACT.Exp).then_inc(hg_exp, 1)
                A(tile(H_["EP"]), tile(H_["CC"]), ACT.Exp).then_inc(hg_exp, 1)
                A(tile(H_["EM"]), tile(H_["CC"]), ACT.Exp, scale=-1.0).then_inc(hg_act, 1)
                act.wait_ge(hg_pe, h * 6 + 1)
                A(tile(H_["IT"]), bank[4][:, :], ACT.Copy).then_inc(hg_act, 1)
                act.wait_ge(hg_pe, h * 6 + 2)
                A(tile(H_["KT"]), bank[5][:, :], ACT.Copy).then_inc(hg_act, 1)
                act.wait_ge(hg_pe, h * 6 + 5)
                A(tile(H_["SQ"]), bank[7][:, :], ACT.Square).then_inc(hg_act, 1)
                act.wait_ge(hg_pe, h * 6 + 6)
                A(tile(H_["RT"]), bank[6][:, :], ACT.Sqrt, scale=1.0 / HG_D, bias=pp("eps")).then_inc(hg_act, 1)
            q += 4 * HG_H
            R_ = RTT
            act.wait_ge(hg_dve, 6 * HG_H + 1)
            with act.Fori(0, RET_H) as h:
                for j in range(8):
                    act.wait_ge(block_used, h * 12 + B_RET + j + 1)
                    if j == 0:
                        act.wait_ge(rt_dve, h * 12 + 1)
                    A(tile(R_["Q"] + j), bank[(q + j) % NBANK][:, :], ACT.Copy).then_inc(evac, 1)
                for s in range(TT):
                    act.wait_ge(rt_pe, h * 16 + s + 1)
                    A(tile(R_["VT"] + s), bank[4][:, :], ACT.Copy).then_inc(rt_act, 1)
                st.enter(h, 4, RET_H)
                for j in range(4):
                    act.wait_ge(rt_pe, h * 16 + 8 + 2 * j + 1)
                    if j:
                        act.wait_ge(rt_pe, h * 16 + 8 + 2 * j)
                    st.go(A(arena[:, bass.ds(h * 4 + (ORET + j), 1), :].rearrange("p a t -> p (a t)"), bank[7][:, :], ACT.Copy))
                    A(tile(R_["SQ"]), bank[7][:, :], ACT.Square).then_inc(rt_act, 1)
                st.leave()
                act.wait_ge(rt_pe, h * 16 + 16)
                A(tile(R_["RT"]), bank[4][:, :], ACT.Sqrt, scale=1.0 / RET_DV, bias=pp("eps")).then_inc(rt_act, 1)
                for j in range(8, 12):
                    act.wait_ge(block_used, h * 12 + B_RET + j + 1)
                    A(tile(R_["G"] + j - 8), bank[(q + j) % NBANK][:, :], ACT.Silu).then_inc(evac, 1)
            q += 12 * RET_H
            for k in range(24):
                act.wait_ge(o_lo_ready, k + 1)
                A(OHL[k][0], spl[:, k % 2, :].bitcast(F32), ACT.Copy).then_inc(o_ready, 1)
            for k in range(KD):
                for j in range(4):
                    act.wait_ge(block_used, B_MERGE + 5 * k + (5 if j == 3 else j + 1))
                    if k and j == 0:
                        act.wait_ge(mg_dve, k)
                    A(tile(MGT + j if j < 3 else MRG + k), bank[q % NBANK][:, :], ACT.Sigmoid if j < 2 else ACT.Copy
                      ).then_inc(evac, 1)
                    q += 1
            xs_hi(lambda k: tile(MRG + k), lambda k: act.wait_ge(mg_dve, KD))
            for k in range(KD):
                act.wait_ge(block_used, B_WOUT2 + k + 1)
                A(tile(WO2 + k), bank[q % NBANK][:, :], ACT.Copy).then_inc(evac, 1)
                q += 1
            norm_squares(5, xr, lambda k: act.wait_ge(resid_ready, 2 * KD + k + 1))
            act.dma_start(arena[:, PSUB:PSUB + 4, :].rearrange("p a b -> p (a b)"), keys_d).then_inc(in_keys, 16)
            norm_hi(5, 3 * KD)
            for k in range(2 * PEER_H):
                act.wait_ge(block_used, B_PQ + k + 1)
                A(tile(PQ + k), bank[q % NBANK][:, :], ACT.Copy).then_inc(evac, 1)
                q += 1
            for t in range(TT):
                for b in range(4):
                    act.wait_ge(tk_pe, 4 * t + b + 1)
                    A(tile(PST + 4 * t + b), bank[4 + b][:, :], ACT.Copy).then_inc(tk_act, 1)

            def gelu(n, b, j, it=0, per=0):
                act.wait_ge(block_used, it * per + n + 1)
                act.wait_ge(hst[j % 2], it * (8 * per) + (16 * (j // 2) + 16))
                A(tile(UT + j % 2), bank[b % NBANK][:, :], ACT.Gelu_apprx_tanh).then_inc(evac, 1)
                act.wait_ge(evac, it * per + b + 1)
                act.dma_start(hidden_d[bass.ds(it * per + j, 1)].rearrange("a p n -> (a p) n"), tile(UT + j % 2)
                              ).then_inc(hst[j % 2], 16)

            for x in hst + gst:
                act.sem_inc(x, 16)
            with act.Fori(0, TT) as t:
                for j in range(NU_ROUTE):
                    gelu(B_U + j, q + j, j, t, NU_ROUTE)
                    if j == NU_ROUTE - 4:
                        act.wait_ge(tk_sub, t + 1)
                        A(bestv[:, :, :], bestv[:, :, :], ACT.Exp).then_inc(tk_exp, 1)
                act.wait_ge(tk_pe, t + 17)
                A(arena[:, PTT:PTT + 3, bass.ds(t * P, P)], bank[4][:, 0:384].rearrange("p (j t) -> p j t", j=3),
                  ACT.Copy).then_inc(tk_act, 1)
            j0 = NU_ROUTE * TT
            q += j0
            act.wait_ge(tk_act, 20)
            act.sem_inc(oh_act, 2)
            with act.Fori(0, NTG // 2) as i:
                for hb in range(2):
                    gbuf = arena[:, GBUF + 8 * hb:GBUF + 8 * hb + 8, :].rearrange("p a b -> p (a b)")
                    by_token = gbuf.rearrange("p (j t) -> p t j", t=TG)
                    act.wait_ge(gst[hb], i * 16 + 16)
                    for b in range(NU_GATES):
                        bb = NU_GATES * hb + b
                        gelu(B_U + j0 + bb, q + bb, j0 + bb, i, 2 * NU_GATES)
                        for u in (2 * b, 2 * b + 1):
                            act.wait_ge(oh_pe, i * 16 + (8 * hb + u + 1))
                            A(by_token[:, 4 * u:4 * u + 4, :], v4(bank[5 + u % 2][:, :]), ACT.Copy).then_inc(oh_act, 1)
                    act.wait_ge(oh_act, i * 16 + (8 * hb + 10))
                    act.dma_start(gates_d[bass.ds(i * 2 + hb, 1)].rearrange("a p n -> (a p) n"), gbuf).then_inc(gst[hb], 16)
            j0 += NU_GATES * NTG
            q += NU_GATES * NTG
            for hb in range(2):
                act.wait_ge(gst[hb], 16 * (NTG // 2) + 16)
            gv = gates_d.rearrange("g p (j t) -> p g (j t)", t=TG)
            hv = hidden_d.rearrange("j p t -> p j t")

            def load(g, it=0):
                b = g % 2
                if g > 1:
                    act.wait_ge(ex_lo, it * 2 * JG + (g - 1) * JG)
                act.dma_start(arena[:, HV + 8 * b:HV + 8 * b + 8, :], hv[:, bass.ds(it * 2 * JG + g * JG, JG), :]
                              ).then_inc(gld[b], 16)
                act.dma_start(arena[:, GV + 8 * b:GV + 8 * b + 8, :].rearrange("p a b -> p (a b)").rearrange(
                    "p (g n) -> p g n", g=NTG), gv[:, 0:NTG, bass.ds(it * (2 * JG * TG) + g * (JG * TG), JG * TG)]
                              ).then_inc(gld[b], 16)

            def gated_hi(g, it=0):
                for j in range(JG):
                    act.wait_ge(ex_prod, it * 2 * JG + g * JG + j + 1)
                    A(GW[g % 2][j][0], tile(HV + 8 * (g % 2) + j), ACT.Copy).then_inc(ex_hi, 1)

            load(0)
            load(1)
            with act.Fori(0, NU_REST // 4 - 1) as i:
                for b in range(4):
                    gelu(B_U + j0 + b, q + b, j0 + b, i, 4)
            j0 += NU_REST - 4
            q += NU_REST - 4
            gated_hi(0)
            for b in range(4):
                gelu(B_U + j0 + b, q + b, j0 + b)
            for b in range(2):
                act.wait_ge(hst[b], 16 * (NKEY // 2 + 1))
            load(2)
            gated_hi(1)
            load(3)
            with act.Fori(0, NJG // 2 - 2) as i:
                gated_hi(2, i)
                load(4, i)
                gated_hi(3, i)
                load(5, i)
            gated_hi(NJG - 2)
            gated_hi(NJG - 1)
            norm_squares(6, xr, lambda k: act.wait_ge(resid_ready, 3 * KD + k + 1))

        @block.gpsimd
        def _(pool):
            one = cst[:, CCOL["ones"][0]:CCOL["ones"][0] + 1].to_broadcast([P, D])

            def split(r, it=None):
                n = r if it is None else it * RING + r
                if it is None:
                    pool.wait_ge(loaded[r], 16)
                else:
                    pool.wait_ge(loaded[r], it * 16 + 16)
                if it is not None or r >= 2:
                    pool.wait_ge(block_used, n - 1)
                pool.tensor_tensor(ring_hi[:, r % 2, :], ring[:, r, :], one, ALU.mult).then_inc(split_hi, 1)
                pool.wait_ge(split_hi, n + 1)
                pool.tensor_tensor(ring_lo[:, r % 2, :], ring[:, r, :], ring_hi[:, r % 2, :].bitcast(F32), ALU.subtract
                                   ).then_inc(w_split, 1)

            pool.wait_ge(in_cst, 16)
            for r in range(RING):
                split(r)
            with pool.Fori(1, N_LOADED // RING) as i:
                for r in range(RING):
                    split(r, i)

        @block.vector
        def _(ve):
            st = Steps(ve, dve_s)
            TSM, TTN, STT, CP = ve.tensor_scalar, ve.tensor_tensor, ve.scalar_tensor_tensor, ve.tensor_copy

            def xs_lo(u, src, k, done=None):
                ve.wait_ge(hi_ready, KD * u + k + 1)
                TTN(XS[k][1], src(k), XS[k][0].bitcast(F32), ALU.subtract).then_inc(xs_ready, 1)

            def norm_root(i):
                ve.wait_ge(root_ready, i + 1)
                ve.reciprocal(tile(NORM[i][1]), tile(NORM[i][0])).then_inc(root_used, 1)
                ve.wait_ge(root_used, i + 1)

            def norm_add(i, gain, src):
                norm_root(i)
                for k in range(KD):
                    st(STT(src(k), src(k), pp(gain, k), tile(NORM[i][1]), ALU.mult, ALU.mult))
                    TTN(xr(k), xr(k), src(k), ALU.add).then_inc(resid_ready, 1)

            def norm_scale(i, gain, u, count):
                norm_root(i)
                dst = lambda k: tile(NORM[i][2] + k % 2)
                for k in range(KD + 1):
                    if k < KD:
                        if k >= 2:
                            ve.wait_ge(xs_ready, KD * u + k - 1)
                        STT(dst(k), xr(k), pp(gain, k), tile(NORM[i][1]), ALU.mult, ALU.mult).then_inc(scaled, 1)
                    if k:
                        ve.wait_ge(scaled, count + k)
                        xs_lo(u, dst, k - 1)

            ve.wait_ge(in_x, 16)
            ve.wait_ge(in_par, 16)
            ve.wait_ge(in_cst, 16)
            norm_scale(0, "attn_pre", 0, 0)
            dests = [GFT, LAT, GL] + [RR + i for i in range(4)] + [RK + i for i in range(4)] + [RV + i for i in range(4)]
            for n in range(12, N_FOX + N_RW):
                ve.wait_ge(evac, n + 1)
                raw, d = tile(RAW + n % 2), tile(DTMP)
                mu = pp("mu", n - 12)
                st.go(TTN(d[:, 1:T], raw[:, 0:T - 1], raw[:, 1:T], ALU.subtract))
                st(TSM(d[:, 0:1], raw[:, 0:1], -1.0, None, ALU.mult))
                STT(tile(dests[n - 12]), d, mu, raw, ALU.mult, ALU.add).then_inc(shifted, 1)
                ve.wait_ge(shifted, n - 11)
                if n == 12:
                    z, a = arena[32:40, BON, :], arena[32:40, BON + 1, :]
                    st(TSM(z, tile(GFT)[32:40, :], par[32:40, PCOL["f_bias"]:PCOL["f_bias"] + 1], None, ALU.add))
                    st(TSM(a, z, -1.0, None, ALU.mult))
                    TTN(a, a, z, ALU.max).then_inc(fc_z, 1)
                    ve.wait_ge(fc_ln, 1)
                    st(TSM(z, z, 0.0, None, ALU.min))
                    st(TTN(z, z, a, ALU.subtract))
                    ve.tensor_tensor_scan(tile(GFT)[32:40, :], cst[32:40, CCOL["ones"][0]:CCOL["ones"][0] + 1].to_broadcast([8, T]), z, 0.0,
                                          ALU.mult, ALU.add).then_inc(fc_ready, 1)
                    ve.wait_ge(fc_ready, 1)
            units = [(h, t) for h in range(8) for t in range(TT)]

            def fox_max(u):
                n = (units[u][1] + 1) * P
                ve.wait_ge(fs_ready, u + 1)
                st(ve.tensor_reduce(stat[:, u:u + 1], bank[u % 2][:, 0:n], AX.X, ALU.max))
                TSM(stat[:, 32 + u:33 + u], stat[:, u:u + 1], -0.125, None, ALU.mult).then_inc(fmax, 1)

            def fox_norm(u):
                n = (units[u][1] + 1) * P
                ve.wait_ge(fexp, u + 1)
                st(ve.reciprocal(stat[:, u:u + 1], stat[:, 64 + u:65 + u]))
                TSM(tile(PR0 + u % 2)[:, 0:n], tile(PR0 + u % 2)[:, 0:n], stat[:, u:u + 1], None, ALU.mult).then_inc(fnorm, 1)

            fox_max(0)
            for u in range(len(units)):
                if u + 1 < len(units):
                    fox_max(u + 1)
                fox_norm(u)

            ve.wait_ge(rw_act, 15)
            ve.wait_ge(fo_out, NPAIR)
            for m in range(NPAIR):
                R, K, V, kk, a = tile(RR + m), tile(RK + m), tile(RV + m), tile(KKT + m), tile(RA + m)
                st(TSM(tile(LW + m), tile(LW + m), -E_HALF, None, ALU.mult))
                if m:
                    ve.wait_ge(exp_ready, m)
                st(ve.tensor_tensor_scan(tile(EL + 3), cc("reset"), tile(LW + m), 0.0, ALU.mult, ALU.add))
                cu = ch(tile(EL + 3))
                st(TTN(ch(tile(EL + 1)), cu, cu[:, :, MID:MID + 1].to_broadcast([P, NCH, C]), ALU.subtract))
                TTN(tile(EL + 2), tile(EL + 1), tile(LW + m), ALU.subtract).then_inc(cum_ready, 1)
                ve.wait_ge(rw_act, 15 + 2 * m + 2)
                st(TSM(tile(EL), tile(EL), 1e-12, None, ALU.max))
                st(ve.reciprocal(tile(EL), tile(EL)))
                st.go(STT(kk, K, pp("k_k", m), tile(EL), ALU.mult, ALU.mult))
                st(TSM(tile(EL + 7), a, 1.0, pp("k_a", m), ALU.subtract, ALU.mult))
                st(STT(K, tile(EL + 7), 1.0, K, ALU.add, ALU.mult))
                STT(tile(RAW), R, pp("r_k", m), K, ALU.mult, ALU.mult).then_inc(rw_dve, 1)
                ve.wait_ge(exp_ready, m + 1)
                st.go(STT(tile(TA + m), kk, -1.0, tile(EL + 6), ALU.mult, ALU.mult))
                st.go(TTN(tile(TR + m), R, tile(EL + 4), ALU.mult))
                st.go(TTN(tile(TK + m), K, tile(EL + 5), ALU.mult))
                st(TTN(kk, kk, a, ALU.mult))
                st.go(TTN(tile(TB + m), kk, tile(EL + 5), ALU.mult))
                st.go(CP(dch[:, 1, m * NCH:(m + 1) * NCH], ch(tile(EL + 4))[:, :, C - 1]))
                ve.wait_ge(rw_pe, 12 + 2 * m + 2)
                st.sync()
                TTN(tile(BON + m), bank[5][:, :], V, ALU.mult).then_inc(rw_dve, 1)
                ve.wait_ge(rw_dve, 2 * m + 2)
            dv = lambda i: dch[:, i, :].rearrange("p (m c) -> p m c", c=NCH)
            st(TTN(dv(2)[:, :, 0:NCH - 1], dv(1)[:, :, 0:NCH - 1], dv(0)[:, :, 1:NCH], ALU.mult))
            ve.wait_ge(rw_act, 39)
            for m in range(NPAIR):
                pb, ab = 36 + RW_PE * m, 39 + RW_ACT * m
                for e in range(2):
                    hs, b0 = HS[e], 3 * e
                    ve.wait_ge(rw_pe, pb + e + 1)
                    if m:
                        ve.wait_ge(rw_act, ab)
                    st.go(TTN(v4(tile(hs[0])), v4(bank[b0][:, :]), mask4("strict"), ALU.mult))
                    st(TTN(v4(tile(hs[2])), v4(bank[b0 + 1][:, :]), mask4("strict_T"), ALU.mult))
                    st.go(TTN(v4(tile(hs[6])), v4(bank[b0 + 2][:, :]), mask4("strict_T"), ALU.mult))
                    TTN(v4(tile(hs[4])), v4(tile(hs[2])), mask4("ident"), ALU.add).then_inc(rw_dve, 1)
                for lev in range(5):
                    for e in range(2):
                        hs, b0 = HS[e], 3 * e
                        a, b = (0, 1) if lev % 2 == 0 else (1, 0)
                        ve.wait_ge(rw_pe, pb + 2 + 4 * lev + e + 1)
                        st.go(CP(tile(hs[2 + b]), bank[b0 + 1][:, :]))
                    for e in range(2):
                        hs, b0 = HS[e], 3 * e
                        a, b = (0, 1) if lev % 2 == 0 else (1, 0)
                        ve.wait_ge(rw_pe, pb + 2 + 4 * lev + 2 + e + 1)
                        ve.wait_ge(rw_dve, 8 + RW_DVE * m + 2 * lev + e + 1)
                        TTN(tile(hs[4 + b]), bank[b0 + 2][:, :], tile(hs[4 + a]), ALU.add).then_inc(rw_dve, 1)
            bp, bd = 36 + RW_PE * 4, 8 + RW_DVE * 4
            shv = arena[:, SH:SH + 4, :].rearrange("p a b -> p (a b)").rearrange("p (c n) -> p c n", c=NCH)
            for c in range(NCH):
                g, p = c // 2, c % 2
                trow = slice(p * HD, (p + 1) * HD)
                if c == 0:
                    ve.wait_ge(rw_act, 39 + RW_ACT * 4)
                    CP(tile(UU + g)[trow, :], tile(U0 + g)[trow, :]).then_inc(rw_dve, 1)
                else:
                    ve.wait_ge(rw_pe, bp + 2 * c)
                    for e in range(2):
                        eh = lambda ap: ap[trow, :].rearrange("p (m e i) -> p m e i", m=4, e=2)[:, :, e, :]
                        ins = TTN(eh(tile(UU + g)), bank[6 - e][trow, 0:256].rearrange("p (m i) -> p m i", m=4),
                                  eh(tile(U0 + g)), ALU.add)
                        if e == 0:
                            st.go(ins)
                        else:
                            ins.then_inc(rw_dve, 1)
                if c == NCH - 1:
                    ve.wait_ge(rw_dve, bd + 15)
                    continue
                ve.wait_ge(rw_pe, bp + 2 * c + 1)
                s3 = lambda ap: ap.rearrange("p (m i) -> p m i", m=4)
                if c == 0:
                    st(CP(tile(74)[:, 0:256], bank[7][:, 0:256]))
                else:
                    st(TTN(tile(74)[:, 0:256], bank[7][:, 0:256], shv[:, c, :], ALU.add))
                TTN(s3(shv[:, c + 1, :]), s3(tile(74)[:, 0:256]), dv(2)[:, :, c:c + 1].to_broadcast([P, 4, HD]),
                    ALU.mult).then_inc(rw_dve, 1)
                ve.wait_ge(rw_dve, bd + 2 * c + 2)
            bp, bd = bp + 14, bd + 15
            for h in range(8):
                hs = HS[h % 2]
                for k in range(2):
                    ve.wait_ge(rw_pe, bp + 3 * h + k + 1)
                    if h >= 2:
                        ve.wait_ge(rw_pe, bp + 3 * (h - 1))
                    TTN(v4(tile(hs[k])), v4(bank[k][:, :]), mask4("incl_T"), ALU.mult).then_inc(rw_dve, 1)
            bp, bd = bp + 24, bd + 16
            ba = 39 + RW_ACT * 4 + 4
            T1, T2, T3, T4 = HS[0][1], HS[0][2], HS[0][3], HS[0][4]
            for m in range(NPAIR):
                ve.wait_ge(rw_pe, bp + 2 * m + 1)
                ve.wait_ge(rw_act, ba + 2 * m)
                TTN(tile(T1), tile(YY + m), bank[0][:, :], ALU.subtract).then_inc(rw_dve, 1)
                ve.wait_ge(rw_act, ba + 2 * m + 2)
                st(ve.reciprocal(tile(T3), tile(T2)))
                st(STT(tile(T4), tile(T1), pp("ln_w", m), tile(T3), ALU.mult, ALU.mult))
                st(STT(tile(T4), tile(T4), pp("ln_b", m), tile(BON + m), ALU.add, ALU.add))
                TTN(tile(ORW + m), tile(T4), tile(RG + m), ALU.mult).then_inc(rw_dve, 1)
                ve.wait_ge(rw_dve, bd + 2 * m + 2)

            for k in range(KD):
                xs_lo(1, lambda k: tile(OF + k if k < 4 else ORW + k - 4), k)
            norm_add(1, "attn_post", lambda k: tile(MO[1] + k))
            norm_scale(2, "ffn_pre", 2, KD)
            ve.sem_inc(ffn_pair, 2)
            q = N_FOX + N_RW + KD
            with ve.Fori(0, KF // 2) as i:
                st.enter(i, 4, KF // 2)
                for j in range(2):
                    ve.wait_ge(evac, i * 4 + q + 2 * j + 2)
                    ve.wait_ge(ffn_pair, i * 2 + j + 1)
                    hi = hid[:, bass.ds(i * 2 + j, 1), :].rearrange("p a t -> p (a t)")
                    lo = hid[:, bass.ds(i * 2 + (KF + j), 1), :].rearrange("p a t -> p (a t)")
                    st(TTN(gu[:, 4 + j, :], gu[:, 2 * j, :], gu[:, 2 * j + 1, :], ALU.mult))
                    st(CP(hi, gu[:, 4 + j, :]))
                    TTN(lo, gu[:, 4 + j, :], hi.bitcast(F32), ALU.subtract).then_inc(ffn_pair, 1)
                st.leave()
            q += 2 * KF
            norm_add(3, "ffn_post", lambda k: tile(MO[3] + k))
            st(TTN(lbt[:, 0, :], par[:, PCOL["lb0"]:PCOL["lb0"] + 8], par[:, PCOL["lb1"]:PCOL["lb1"] + 8], ALU.max))
            st(TTN(lbt[:, 1, :], par[:, PCOL["lb0"]:PCOL["lb0"] + 8], lbt[:, 0, :], ALU.subtract))
            TTN(lbt[:, 2, :], par[:, PCOL["lb1"]:PCOL["lb1"] + 8], lbt[:, 0, :], ALU.subtract).then_inc(lb_ready, 1)
            ve.wait_ge(lb_ready, 2)
            st(TTN(lbt[:, 2, :], lbt[:, 1, :], lbt[:, 2, :], ALU.add))
            st(ve.reciprocal(lbt[:, 2, :], lbt[:, 2, :]))
            st(TTN(lbt[:, 0, :], lbt[:, 1, :], lbt[:, 2, :], ALU.mult))
            TSM(lbt[:, 1, :], lbt[:, 0, :], -1.0, 1.0, ALU.mult, ALU.add).then_inc(hg_dve, 1)
            ve.wait_ge(hg_dve, 1)
            norm_scale(4, "mix_norm", 3, 2 * KD)

            q += KD
            H_ = HGT
            with ve.Fori(0, HG_H) as h:
                st.enter(h, 18, HG_H)
                ve.wait_ge(evac, h * 4 + q + 1)
                lb, lb1 = lbt[:, 0, bass.ds(h, 1)], lbt[:, 1, bass.ds(h, 1)]
                TSM(tile(H_["F"]), tile(H_["F"]), lb1, lb, ALU.mult, ALU.add).then_inc(hg_dve, 1)
                ve.wait_ge(hg_dve, h * 6 + 2)
                st.go(TSM(tile(H_["K"]), tile(H_["F"]), -1.0, 1.0, ALU.mult, ALU.add))
                ve.wait_ge(hg_act, h * 6 + 1)
                st(ve.tensor_tensor_scan(tile(H_["CU"]), cc("reset"), tile(H_["LF"]), 0.0, ALU.mult, ALU.add))
                cu = ch(tile(H_["CU"]))
                TTN(ch(tile(H_["CC"])), cu, cu[:, :, MID:MID + 1].to_broadcast([P, NCH, C]), ALU.subtract).then_inc(hg_dve, 1)
                ve.wait_ge(hg_act, h * 6 + 2)
                ve.wait_ge(evac, h * 4 + q + 4)
                st.go(TTN(tile(H_["KD"]), tile(H_["K"]), tile(H_["EM"]), ALU.mult))
                STT(tile(H_["QD"]), tile(H_["Q"]), HG_D ** -0.5, tile(H_["EP"]), ALU.mult, ALU.mult).then_inc(hg_dve, 1)
                ve.wait_ge(hg_exp, h * 2 + 2)
                st(TTN(dch[:, 5, 0:NCH - 1], ch(tile(H_["EP"]))[:, 0:NCH - 1, C - 1], dch[:, 4, 1:NCH], ALU.mult))
                ve.wait_ge(hg_pe, h * 6 + 3)
                TTN(v4(tile(H_["AM"])), v4(bank[6][:, :]), mask4("incl_T"), ALU.mult).then_inc(hg_dve, 1)
                ve.wait_ge(hg_pe, h * 6 + 4)
                for c in range(NCH - 1):
                    kv = bank[4 + c % 2][:, (c // 2) * P:(c // 2 + 1) * P]
                    src = kv
                    if c:
                        st(TTN(tile(H_["X"])[:, 0:P], kv, H_["S"](c), ALU.add))
                        src = tile(H_["X"])[:, 0:P]
                    ins = TSM(H_["S"](c + 1), src, dch[:, 5, c:c + 1], None, ALU.mult)
                    if c < NCH - 2:
                        st(ins)
                    else:
                        ins.then_inc(hg_dve, 1)
                ve.wait_ge(hg_act, h * 6 + 6)
                st(ve.reciprocal(tile(H_["R2"]), tile(H_["RT"])))
                wn = par[:, bass.ds(h + PCOL["hg_norm"], 1)]
                st(STT(tile(H_["R2"]), bank[7][:, :], wn, tile(H_["R2"]), ALU.mult, ALU.mult))
                TTN(arena[:, bass.ds(h + OHG, 1), :].rearrange("p a t -> p (a t)"), tile(H_["R2"]), tile(H_["G"]),
                    ALU.mult).then_inc(hg_dve, 1)
                ve.wait_ge(hg_dve, h * 6 + 7)
                st.leave()
            q += 4 * HG_H
            R_ = RTT
            ve.wait_ge(in_rot, 32)
            ve.sem_inc(rt_dve, 1)
            with ve.Fori(0, RET_H) as h:
                st.enter(h, 13, RET_H)
                cos, sin = tile(R_["COS"]), tile(R_["COS"] + 1)
                n0 = 0
                for k, (src, dst) in enumerate((("Q", "QR"), ("K", "KR"))):
                    x1, x2 = tile(R_[src]), tile(R_[src] + 1)
                    sc = 1.0 if k == 0 else RET_DK ** -0.5
                    ve.wait_ge(evac, h * 12 + q + 2 * k + 2)
                    st.go(STT(tile(R_["T"]), x1, sc, cos, ALU.mult, ALU.mult))
                    st.go(STT(tile(R_["T"] + 1), x2, sc, sin, ALU.mult, ALU.mult))
                    st.go(STT(tile(R_["T"] + 2), x1, sc, sin, ALU.mult, ALU.mult))
                    st(STT(tile(R_["T"] + 3), x2, sc, cos, ALU.mult, ALU.mult))
                    TTN(tile(R_[dst]), tile(R_["T"]), tile(R_["T"] + 1), ALU.subtract).then_inc(rt_dve, 1)
                    TTN(tile(R_[dst] + 1), tile(R_["T"] + 2), tile(R_["T"] + 3), ALU.add).then_inc(rt_dve, 1)
                    ve.wait_ge(rt_dve, h * 12 + 2 * k + 3)
                for s in range(TT):
                    n = T - s * P
                    ve.wait_ge(rt_pe, h * 16 + 4 + s + 1)
                    TTN(tile(R_["AM"] + s)[:, 0:n], bank[5 + s % 2][:, 0:n],
                        arena[:, bass.ds(h + R_["MASK"], 1), 0:n].rearrange("p a t -> p (a t)"), ALU.mult).then_inc(rt_dve, 1)
                ve.wait_ge(rt_act, h * 9 + 9)
                st(ve.reciprocal(tile(R_["R2"]), tile(R_["RT"])))
                for j in range(4):
                    o = arena[:, bass.ds(h * 4 + (ORET + j), 1), :].rearrange("p a t -> p (a t)")
                    st(TTN(o, o, tile(R_["R2"]), ALU.mult))
                    ve.wait_ge(evac, h * 12 + q + 8 + j + 1)
                    TTN(o, o, tile(R_["G"] + j), ALU.mult).then_inc(rt_dve, 1)
                ve.wait_ge(rt_dve, h * 12 + 13)
                st.leave()
            q += 12 * RET_H
            for k in range(24):
                if k >= 2:
                    ve.wait_ge(o_ready, k - 1)
                st(CP(spl[:, k % 2, :], tile(OHG + k)))
                TTN(OHL[k][1], tile(OHG + k), spl[:, k % 2, :].bitcast(F32), ALU.subtract).then_inc(o_lo_ready, 1)
            for k in range(KD):
                ve.wait_ge(evac, q + 4)
                q += 4
                st.go(TTN(tile(MGT), tile(MGT), tile(MGT + 2), ALU.mult))
                st(TTN(tile(MRG + k), tile(MRG + k), tile(MGT + 1), ALU.mult))
                TTN(tile(MRG + k), tile(MRG + k), tile(MGT), ALU.add).then_inc(mg_dve, 1)
            for k in range(KD):
                xs_lo(4, lambda k: tile(MRG + k), k)
            for k in range(KD):
                ve.wait_ge(evac, q + 1)
                q += 1
                TTN(xr(k), xr(k), tile(WO2 + k), ALU.add).then_inc(resid_ready, 1)
            norm_scale(5, "ffn_norm", 5, 3 * KD)
            q += 2 * PEER_H

            io16 = cst[:, CCOL["iota"][0]:CCOL["iota"][0] + 16]
            big = lambda i: arena[:, PBIG + 4 * i:PBIG + 4 * i + 4, :].rearrange("p a b -> p (a b)")
            for t in range(TT):
                ve.wait_ge(tk_act, 4 * (t + 1))
                sc = arena[:, PST + 4 * t:PST + 4 * t + 4, :].rearrange("p a b -> p (a b)")
                for n in range(16):
                    s = sc[:, n * P:(n + 1) * P]
                    st(ve.max(topv[:, n, 0:8], s))
                    st(ve.max_index(topi[:, n, 0:8], topv[:, n, 0:8], s))
                    st(ve.match_replace(s, topv[:, n, 0:8], s, -3.0e38))
                    st(ve.max(topv[:, n, 8:16], s))
                    st.go(ve.max_index(topi[:, n, 8:16], topv[:, n, 8:16], s))
                st.sync()
                st.go(CP(topf, topi))
                tv = topv[:, :, :].rearrange("p (h s) k -> p h s k", s=2)
                tf = topf[:, :, :].rearrange("p (h s) k -> p h s k", s=2)
                cand = big(0).rearrange("p (h a b) -> p h a b", h=8, a=16)
                st(TTN(cand, tv[:, :, 0, :].unsqueeze(3).to_broadcast([P, 8, 16, 16]),
                       tv[:, :, 1, :].unsqueeze(2).to_broadcast([P, 8, 16, 16]), ALU.add))
                if t:
                    ve.wait_ge(tk_exp, t)
                for h in range(8):
                    s = big(0)[:, h * 256:(h + 1) * 256]
                    st(ve.max(bestv[:, h, 0:8], s))
                    st(ve.max_index(besti[:, h, 0:8], bestv[:, h, 0:8], s))
                    st(ve.match_replace(s, bestv[:, h, 0:8], s, -3.0e38))
                    st(ve.max(bestv[:, h, 8:16], s))
                    st.go(ve.max_index(besti[:, h, 8:16], bestv[:, h, 8:16], s))
                st.sync()
                st(CP(gsum[:, 0, :], bestv[:, :, 0]))
                TTN(bestv[:, :, :], bestv[:, :, :], gsum[:, 0, :].unsqueeze(2).to_broadcast([P, 8, 16]),
                    ALU.subtract).then_inc(tk_sub, 1)
                st.go(TSM(bests[:, :, :], besti[:, :, :], 4, None, ALU.logical_shift_right))
                st(TSM(besti[:, :, :], besti[:, :, :], 15, None, ALU.bitwise_and))
                st.go(CP(bestf[:, 0, :, :], bests[:, :, :]))
                st(CP(bestf[:, 1, :, :], besti[:, :, :]))
                if t:
                    ve.wait_ge(tk_pe, 16 + t)
                for s in range(2):
                    hot = big(1).rearrange("p (h k a) -> p h k a", h=8, k=16)
                    st(TTN(hot, bestf[:, s, :, :].unsqueeze(3).to_broadcast([P, 8, 16, 16]),
                           io16.unsqueeze(1).unsqueeze(1).to_broadcast([P, 8, 16, 16]), ALU.is_equal))
                    st(TTN(hot, hot, tf[:, :, s, :].unsqueeze(2).to_broadcast([P, 8, 16, 16]), ALU.mult))
                    st(ve.tensor_reduce(pairs[:, s, :].rearrange("p (h k) -> p h k", h=8), hot, AX.X, ALU.add))
                ve.wait_ge(tk_exp, t + 1)
                st(ve.tensor_reduce(gsum[:, 0, :], bestv[:, :, :], AX.X, ALU.add))
                st(ve.reciprocal(gsum[:, 1, :], gsum[:, 0, :]))
                TTN(pairs[:, 2, :].rearrange("p (h k) -> p h k", h=8), bestv[:, :, :],
                    gsum[:, 1, :].unsqueeze(2).to_broadcast([P, 8, 16]), ALU.mult).then_inc(tk_dve, 1)
                ve.wait_ge(tk_dve, t + 1)
            ve.wait_ge(tk_act, 20)
            iota = cc("iota")
            with ve.Fori(0, NTG // 2) as i:
                for u in range(2 * TG // 4):
                    ve.wait_ge(oh_act, i * 16 + u + 1)
                    for j in range(4):
                        t1 = bass.ds(i * (2 * TG) + (4 * u + j), 1)
                        TSM(oneA[:, u % 2, j, :], iota, arena[:, PTT, t1], arena[:, PTT + 2, t1], ALU.is_equal, ALU.mult)
                        ins = TSM(oneB[:, u % 2, j, :], iota, arena[:, PTT + 1, t1], None, ALU.is_equal)
                    ins.then_inc(oh_dve, 1)
            ve.wait_ge(oh_act, 8 * NTG + 2)
            for d in range(KD):
                st.go(ve.memset(tile(ACC + d), 0.0))
            st.sync()

            def gated(g, it=0):
                b = g % 2
                ve.wait_ge(gld[b], it * 32 + 32 * (g // 2 + 1))
                gates = arena[:, GV + 8 * b:GV + 8 * b + 8, :].rearrange("p a b -> p (a b)").rearrange(
                    "p (g j t) -> p g j t", g=NTG, j=JG)
                by_store = lambda ap: ap.rearrange("p (g t) -> p g t", g=NTG)
                for j in range(JG):
                    h = by_store(tile(HV + 8 * b + j))
                    TTN(h, h, gates[:, :, j, :], ALU.mult).then_inc(ex_prod, 1)
                for j in range(JG):
                    ve.wait_ge(ex_hi, it * 2 * JG + g * JG + j + 1)
                    TTN(GW[b][j][1], tile(HV + 8 * b + j), GW[b][j][0].bitcast(F32), ALU.subtract).then_inc(ex_lo, 1)

            def acc(g, it=0):
                for half in range(2):
                    ve.wait_ge(block_used, it * 2 * JG + B_V + g * JG + 4 * half + 4)
                    if g:
                        ve.wait_ge(ex_acc, it * 16 + 8 * (g - 1) + 4 * half + 4)
                    for d in range(4):
                        o = tile(ACC + 4 * half + d)
                        TTN(o, o, bank[4 * half + d][:, :], ALU.add).then_inc(ex_acc, 1)

            gated(0)
            ve.wait_ge(block_used, B_V)
            gated(1)
            acc(0)
            gated(2)
            acc(1)
            gated(3)
            with ve.Fori(0, NJG // 2 - 2) as i:
                acc(2, i)
                gated(4, i)
                acc(3, i)
                gated(5, i)
            acc(NJG - 2)
            acc(NJG - 1)
            ve.wait_ge(ex_acc, 8 * NJG)
            for k in range(KD):
                TTN(xr(k), xr(k), tile(ACC + k), ALU.add).then_inc(resid_ready, 1)
            norm_root(6)
            for k in range(KD):
                STT(tile(OUT + k), xr(k), pp("final_norm", k), tile(NORM[6][1]), ALU.mult, ALU.mult).then_inc(out_ready, 1)


def _tiles(w, order=None):
    k, n = w.shape
    return w.reshape(k // P, P, n // P, P).transpose(2, 1, 0, 3).reshape(n // P, P, k)


def _constants():
    i = np.arange(P)
    same = (i[:, None] // C) == (i[None, :] // C)
    lower = i[:, None] > i[None, :]
    c = {
        "ident": np.eye(P), "ones": np.ones((P, P)), "bones": same, "bmean": same / HD,
        "strict_T": same & lower.T, "strict": same & lower, "incl_T": same & ~lower,
        "neg": np.where(i[:, None] >= i[None, :], 0.0, NEG), "iota": np.tile(i, (P, 1)),
        "reset": np.tile((np.arange(T) % C != 0), (P, 1)),
    }
    table = np.concatenate([np.asarray(c[n], np.float32) for n, _ in CONSTS], axis=1)
    select = np.zeros((8, 8, P), np.float32)
    select[np.arange(8), np.arange(8)] = -8.0
    half = RET_DK // 2
    inv = np.float32(10000.0) ** (-np.arange(half, dtype=np.float32) / half)
    ang = inv.astype(np.float32)[:, None] * np.arange(T, dtype=np.float32)[None, :]
    rotary = np.stack([np.cos(ang), np.sin(ang)], axis=1).astype(np.float32)
    log_g = np.log1p(-np.exp2(-5.0 - np.arange(RET_H)))
    rel = np.arange(T)[None, :] - i[:, None]
    decay = np.where(rel[:, None, :] >= 0, np.exp(log_g[None, :, None] * np.maximum(rel, 0)[:, None, :]), 0.0)
    return table, select.reshape(8, 8 * P), rotary, decay.astype(np.float32)


def _stream(a):
    w_in = a["w_in"][0]
    fw, rw = 3 * 512, 3 * 512 + 8
    gf = np.zeros((D, P), np.float32)
    gf[:, 0:32] = w_in[:, rw + 1536 + 128 + 128:]
    gf[:, 32:40] = w_in[:, fw:fw + 8]
    parts = [_tiles(w_in[:, 0:fw]), _tiles(gf), _tiles(w_in[:, rw + 1536:rw + 1536 + 256]), _tiles(w_in[:, rw:rw + 1536])]
    parts.append(_tiles(a["w_out"][0]))
    gate, up = _tiles(a["ffn_w_gate"][0]), _tiles(a["ffn_w_up"][0])
    parts.append(np.stack([gate, up], axis=1).reshape(2 * KF, P, D))
    down = np.zeros((KD, P, 3 * D), np.float32)
    down[:, :, 0:FF] = _tiles(a["ffn_w_down"][0])
    parts.append(down.reshape(KD, P, 3, D).transpose(0, 2, 1, 3).reshape(3 * KD, P, D))
    w2 = _tiles(a["w_in_2"][0])
    hq, hf, hi, hg = (w2[8 * i:8 * i + 8] for i in range(4))
    parts.append(np.stack([hf, hi, hg, hq], axis=1).reshape(4 * HG_H, P, D))
    rq, rk = (w2[o:o + 8].reshape(4, 2, P, D) for o in (32, 40))
    rv, rg = (w2[o:o + 16].reshape(4, 4, P, D) for o in (48, 64))
    parts.append(np.concatenate([rq, rk, rv, rg], axis=1).reshape(12 * RET_H, P, D))
    ret = _tiles(a["w_branch_ret_2"][0]).reshape(KD, P, 2, D).transpose(0, 2, 1, 3)
    merge = np.concatenate([w2[80:88, None], w2[88:96, None], _tiles(a["w_branch_hg_2"][0])[:, None], ret], axis=1)
    parts.append(merge.reshape(5 * KD, P, D))
    parts.append(_tiles(a["w_out_2"][0]))
    parts.append(_tiles(a["peer_w_q_2"][0]))
    parts.append(a["expert_u_2"][0].reshape(NKEY, NKEY, KD, P).transpose(1, 3, 2, 0).reshape(NKEY, P, D))
    v = a["expert_v_2"][0].reshape(NKEY, NJG, 4, 2, 2, 512).transpose(1, 4, 2, 0, 3, 5)
    parts.append(v.reshape(NKEY, P, D))
    parts.append(np.zeros((N_LOADED - N_BLOCKS, P, D), np.float32))
    return np.concatenate(parts, axis=0)


def _parameters(a):
    col = lambda v: np.asarray(v, np.float32).reshape(-1, P).T
    mu = np.asarray(a["shift_mu"][0])
    mu_gf = np.zeros(P, np.float32)
    mu_gf[0:32] = mu[1536 + 256:]
    f_bias = np.zeros(P, np.float32)
    f_bias[32:40] = a["fox_forget_bias"][0]
    v = {
        "attn_pre": a["attn_norm_pre"], "attn_post": a["attn_norm_post"],
        "mu": np.concatenate([mu_gf, mu[1536:1536 + 256], mu[0:1536]]),
        "w0": a["rwkv_w0"], "a0": a["rwkv_a0"], "k_k": a["rwkv_k_k"], "k_a": a["rwkv_k_a"], "r_k": a["rwkv_r_k"],
        "ln_w": a["rwkv_ln_w"], "ln_b": a["rwkv_ln_b"], "ffn_pre": a["ffn_norm_pre"], "ffn_post": a["ffn_norm_post"],
        "mix_norm": a["norm_mix_w_2"], "lb0": a["hg_lower_bounds_2"][0], "lb1": a["hg_lower_bounds_2"][1],
        "hg_norm": a["hg_norm_w_2"], "ffn_norm": a["norm_ffn_w_2"], "final_norm": a["final_norm_w_2"], "f_bias": f_bias,
        "eps": np.full(P, 1e-6, np.float32), "ln_eps": np.full(P, 64e-5, np.float32),
    }
    return np.ascontiguousarray(np.concatenate([col(v[n]) for n, _ in PARAMS], axis=1))


def kernel(**inputs):
    import concourse.bacc as bacc
    from concourse.bass_utils import run_bass_kernel_spmd as run

    a = {n: np.asarray(v) for n, v in inputs.items()}
    table, select, rotary, decay = _constants()
    low_rank = np.zeros((P, 3, T), np.float32)
    low_rank[0:64, 0] = a["rwkv_w_up"][0]
    low_rank[64:128, 0] = a["rwkv_a_up"][0]
    low_rank[:, 1] = a["rwkv_g_up"][0][0:128]
    low_rank[0:32, 2] = a["rwkv_g_up"][0][128:160]
    arrays = {
        "x_t": np.ascontiguousarray(a["x"][0].T), "parameters": _parameters(a), "constants": table, "selectors": select,
        "rotary": rotary, "ret_decay": decay, "low_rank": low_rank,
        "sub_keys": np.ascontiguousarray(a["peer_sub_keys_2"][0].reshape(16, NKEY, P).transpose(2, 0, 1).reshape(P, 16 * NKEY)),
        "weights": _stream(a),
    }
    nc = bacc.Bacc("TRN2", target_bir_lowering=False, num_devices=1)
    args = [nc.dram_tensor(n, v.shape, F32, kind="ExternalInput").ap() for n, v in arrays.items()]
    gates = nc.dram_tensor("gates", (NTG, P, NKEY * TG), F32, kind="Internal").ap()
    hidden = nc.dram_tensor("hidden", (NKEY, P, T), F32, kind="Internal").ap()
    out = nc.dram_tensor("out_t", (D, T), F32, kind="ExternalOutput").ap()
    build(nc, *args, gates, hidden, out)
    r = run(nc, [arrays], core_ids=[0])
    return np.ascontiguousarray(r.results[0]["out_t"].T)[None]
```

```python
from contextlib import ExitStack

import numpy as np
import concourse.bass as bass
from concourse import mybir

ALU = mybir.AluOpType
ACT = mybir.ActivationFunctionType
AX = mybir.AxisListType
F32 = mybir.dt.float32
F32R = mybir.dt.float32r
U32 = mybir.dt.uint32

P = 128
T = 512
D = 1024
KD = D // P
TT = T // P
C = 64
NCH = T // C
HD = 64
NPAIR = 4
FF = 2816
KF = FF // P
HG_H, HG_D = 8, 128
RET_H, RET_DK, RET_DV = 4, 256, 512
PEER_H, PEER_K, NKEY = 8, 16, 128
TG = 32
NTG = T // TG
JG = 8
NJG = NKEY // JG
RING = 4
NBANK = 4
MID = C // 2 - 1
NEG = -1.0e30
E_HALF = float(np.exp(-0.5))

N_FOX = 13
N_RW = 14
B_FOX = 0
B_RW = B_FOX + N_FOX
B_WOUT = B_RW + N_RW
B_FFN = B_WOUT + KD
B_DOWN = B_FFN + 2 * KF
B_HG = B_DOWN + 3 * KD
B_RET = B_HG + 4 * HG_H
B_MERGE = B_RET + 12 * RET_H
B_WOUT2 = B_MERGE + 5 * KD
B_PQ = B_WOUT2 + KD
B_U = B_PQ + 2 * PEER_H
B_V = B_U + NKEY
N_BLOCKS = B_V + NKEY
NU_ROUTE = 12
NU_GATES = 4
NU_REST = NKEY - NU_ROUTE * TT - NU_GATES * NTG
N_LOADED = -(-N_BLOCKS // RING) * RING

PARAMS = [("attn_pre", 8), ("attn_post", 8), ("mu", 15), ("w0", 4), ("a0", 4), ("k_k", 4), ("k_a", 4),
          ("r_k", 4), ("ln_w", 4), ("ln_b", 4), ("ffn_pre", 8), ("ffn_post", 8), ("mix_norm", 8),
          ("lb0", 8), ("lb1", 8), ("hg_norm", 8), ("ffn_norm", 8), ("final_norm", 8), ("f_bias", 1),
          ("eps", 1), ("ln_eps", 1)]
PCOL, NPAR = {}, 0
for _n, _w in PARAMS:
    PCOL[_n] = NPAR
    NPAR += _w

CONSTS = [("ident", 128), ("ones", 128), ("bones", 128), ("bmean", 128), ("strict_T", 128),
          ("strict", 128), ("incl_T", 128), ("neg", 128), ("iota", 128), ("reset", 512)]
CCOL, NCST = {}, 0
for _n, _w in CONSTS:
    CCOL[_n] = (NCST, _w)
    NCST += _w


class Steps:

    def __init__(self, eng, sem):
        self.eng, self.sem, self.n, self.loop = eng, sem, 0, 0

    def go(self, ins):
        self.n += 1
        ins.then_inc(self.sem, 1)

    def sync(self):
        self.eng.wait_ge(self.sem, self.n + self.loop)

    def __call__(self, ins):
        self.go(ins)
        self.sync()

    def enter(self, it, per, count):
        self.loop, self.at, self.per, self.count = it * per, self.n, per, count

    def leave(self):
        assert self.n - self.at == self.per, (self.n - self.at, self.per)
        self.n = self.at + self.per * self.count
        self.loop = 0


def build(nc, xt, par_d, cst_d, sel_d, rot_d, rmask_d, small_d, keys_d, wstream, gates_d, hidden_d, out):
    with ExitStack() as ctx:
        def sb(name, shape, dt=F32):
            return ctx.enter_context(nc.sbuf_tensor(name, shape, dt))

        def sem(name):
            return ctx.enter_context(nc.semaphore(name))

        NT = 75
        arena = sb("arena", [P, NT, T])
        base = nc.sbuf_base - NT * T * 4

        def over(name, first, tiles, dt=F32R):
            return nc.alloc_sbuf_tensor_at(name, [P, tiles, T], dt, offset=base + first * T * 4)

        xs = over("xs", 0, 2 * KD)
        hid = over("hid", 22, 2 * KF)
        o_hi = over("o_hi", 51, 24)
        o_lo = over("o_lo", 27, 24)
        gw = over("gw", 0, 4 * JG)
        ghi = over("ghi", 31, 1)
        spl = over("spl", 22, 2)
        gu = over("gate_up", 16, 6, F32)
        selr = over("selr", 70, 2)
        cumr = over("cumr", 50, 2)
        maskr = over("maskr", 52, 1)
        xres = sb("xres", [P, KD, T])
        ring = sb("ring", [P, RING, D])
        ring_hi = sb("ring_hi", [P, 2, D], F32R)
        ring_lo = sb("ring_lo", [P, 2, D], F32R)
        par = sb("par", [P, NPAR])
        cst = sb("cst", [P, NCST])
        bank = [ctx.enter_context(nc.psum_tensor(f"bank{b}", [P, 512], F32)) for b in range(8)]
        stat = sb("stat", [P, 96])
        roots = sb("roots", [P, 2, TT * 8])
        lbt = sb("lbt", [P, 4, 8])
        dch = sb("dch", [P, 6, 4 * NCH])

        def tile(i):
            return arena[:, i, :]

        def cc(name):
            a, w = CCOL[name]
            return cst[:, a:a + w]

        def pp(name, i=0):
            return par[:, PCOL[name] + i:PCOL[name] + i + 1]

        def mask4(name):
            return cc(name).unsqueeze(1).to_broadcast([P, 4, 128])

        def small(a, n, dt=None):
            ap = arena[:, 64:68, :].rearrange("p a b -> p (a b)")[:, a:a + n]
            return ap if dt is None else ap.bitcast(dt)

        topv = small(0, 256).rearrange("p (n k) -> p n k", n=16)
        topi = small(256, 256, U32).rearrange("p (n k) -> p n k", n=16)
        topf = small(512, 256).rearrange("p (n k) -> p n k", n=16)
        bestv = small(768, 128).rearrange("p (h k) -> p h k", h=8)
        besti = small(896, 128, U32).rearrange("p (h k) -> p h k", h=8)
        bests = small(1024, 128, U32).rearrange("p (h k) -> p h k", h=8)
        bestf = small(1152, 256).rearrange("p (s h k) -> p s h k", s=2, h=8)
        pairs = small(1408, 384).rearrange("p (j n) -> p j n", j=3)
        gsum = small(1792, 16).rearrange("p (s h) -> p s h", s=2)
        oneH, oneL, oneB = (over(n, i, 2).rearrange("p u (j n) -> p u j n", j=4) for n, i in (
            ("oneH", 68), ("oneL", 70), ("oneB", 66)))

        def v4(ap):
            return ap.rearrange("p (g t) -> p g t", g=4)

        def ch(ap):
            return ap.rearrange("p (c t) -> p c t", t=C)

        loaded = [sem(f"loaded{r}") for r in range(RING)]
        block_used = sem("block_used")
        evac = sem("evac")
        in_x = [sem(f"in_x{i}") for i in range(4)]
        in_par, in_cst, in_small = sem("in_par"), sem("in_cst"), sem("in_small")
        in_rot = sem("in_rot")
        act_s, dve_s, pe_s = sem("act_steps"), sem("dve_steps"), sem("pe_steps")
        sq_ready, sum_ready, root_ready = sem("squares_ready"), sem("sums_ready"), sem("root_ready")
        sq_used = sem("squares_used")
        root_used = sem("root_used")
        fc_z, fc_ln = sem("forget_z"), sem("forget_ln")
        cum_ready, exp_ready, hg_exp = sem("decays_cumulated"), sem("decays_exp"), sem("hg_chunk_decays")
        lb_ready = sem("lower_bound")
        tk_sub, tk_exp = sem("route_shifted"), sem("route_exp")
        w_split = sem("weights_split")
        split_hi = sem("split_hi")
        scaled = sem("scaled")
        hi_ready = sem("hi_ready")
        xs_ready = sem("xs_ready")
        o_lo_ready, o_ready = sem("branch_lo"), sem("branch_split")
        resid_ready = sem("resid_ready")
        shifted = sem("shifted")
        ffn_pair = sem("ffn_pair")
        fc_ready, vt_ready, vt_out = sem("fox_cum_ready"), sem("fox_vt_psum"), sem("fox_v_tokens")
        fs_ready, fmax, fexp, fnorm = sem("fox_scores"), sem("fox_max"), sem("fox_exp"), sem("fox_probs")
        ft_ready, ft_out, fo_ready, fo_out = sem("fox_pT_psum"), sem("fox_pT"), sem("fox_out_psum"), sem("fox_out")
        rw_inv, rw_inv_out = sem("rwkv_inverse_roots"), sem("rwkv_roots_spread")
        rw_pe, rw_act, rw_dve = sem("rwkv_products"), sem("rwkv_act"), sem("rwkv_dve")
        hg_pe, hg_act, hg_dve = sem("hg_products"), sem("hg_act"), sem("hg_dve")
        rt_pe, rt_act, rt_dve = sem("ret_products"), sem("ret_act"), sem("ret_dve")
        mg_dve = sem("merged")
        tk_pe, tk_act, tk_dve = sem("route_products"), sem("route_act"), sem("route_dve")
        oh_dve, oh_pe, oh_act = sem("onehots"), sem("gate_psum"), sem("gate_tokens")
        gst = [sem("gates_stored0"), sem("gates_stored1")]
        hst = [sem("hidden_stored0"), sem("hidden_stored1")]
        gld = [sem("group_loaded0"), sem("group_loaded1")]
        in_keys = sem("in_keys")
        ex_prod, ex_hi, ex_lo = sem("gated_hidden"), sem("gated_hi"), sem("gated_lo")
        ex_acc = sem("accumulated")
        out_ready, stored = sem("out_ready"), sem("stored")

        def xr(k):
            return xres[:, k, :]

        XS = [(xs[:, k, :], xs[:, KD + k, :]) for k in range(KD)]
        GW = [[(gw[:, 16 * (1 - b) + j, :], gw[:, 16 * (1 - b) + JG + j, :]) for j in range(JG)] for b in range(2)]
        HID = [(hid[:, k, :], hid[:, KF + k, :]) for k in range(KF)]
        OHL = [(o_hi[:, k, :], o_lo[:, k, :]) for k in range(24)]
        TA, TR, TB, TK = 0, 4, 8, 12
        Q0, K0, VF0, VT0 = 16, 20, 24, 28
        RR, RK, RV, LAT, GL, GFT, RAW = 32, 36, 40, 44, 45, 46, 47
        DTMP = 49
        RA, LW, RG, KKT, BON, OF = 50, 54, 58, 24, 66, 62
        DT4, RT4 = (48, 49, 24, 25), 66
        EL = 16
        MA, MB, MK, MV = 16, 20, 24, 28
        WT, U0, UU, SH = 32, 36, 54, 50
        HS = [[40, 41, 42, 43, 44, 45, 46, 47], [48, 49, 70, 71, 72, 73, 74, 50]]
        ORW = 66
        SMALL, SELT = 72, 70
        PT0, PR0 = 66, 68
        NORM = [(60, 62, 63), (66, 68, 69), (66, 68, 16), (16, 18, 19), (16, 18, 19), (16, 18, 19), (32, 34, 35)]
        MO = [None, 24, None, 66]
        YY = 36
        MS = [(40, 41), (42, 43), (44, 45), (46, 47), (48, 49), (70, 71), (72, 73), (16, 17)]
        GND, GNS, GNR = 40, 44, 70
        HGT = dict(F=16, LF=17, K=18, CU=19, CC=20, EP=21, EM=22, I=23, G=24, Q=25, KD=26, QD=27, IT=28, KT=29,
                   AM=30, SQ=31, RT=32, R2=33, X=34, S=lambda c: tile(35 + c // 4)[:, (c % 4) * P:(c % 4 + 1) * P])
        OHG, ORET = 51, 59
        RTT = dict(Q=16, K=18, VF=20, QR=24, KR=26, VT=28, AM=32, T=32, SQ=36, RT=37, R2=38, G=39, COS=43, MASK=45)
        MRG, MGT = 16, 24
        WO2 = 27
        PQ, PSUB = 32, 28
        PST, PBIG, PTT = 48, 20, 28
        UT = 72
        GBUF = 32
        HV, GV, ACC, OUT = 32, 48, 64, 40
        RW_PE, RW_ACT, RW_DVE = 28, 16, 12

        block = ctx.enter_context(nc.Block())

        @block.sync
        def _(sp):
            sp.wait_ge(in_x[2], 16)
            for r in range(RING):
                sp.dma_start(ring[:, r, :], wstream[r]).then_inc(loaded[r], 16)
            with sp.Fori(1, N_LOADED // RING) as i:
                for r in range(RING):
                    sp.wait_ge(w_split, i * RING + (r + 1 - RING))
                    sp.dma_start(ring[:, r, :], wstream[bass.ds(i * RING + r, 1)].rearrange("a p n -> (a p) n")
                                 ).then_inc(loaded[r], 16)
            sp.wait_ge(out_ready, KD)
            sp.dma_start(out.rearrange("(k p) t -> p k t", p=P), arena[:, OUT:OUT + KD, :]).then_inc(stored, 16)
            sp.wait_ge(stored, 16)

        @block.tensor
        def _(pe):
            st = Steps(pe, pe_s)

            def ready(n, it=0, per=0):
                pe.wait_ge(w_split, it * per + (n + 1))

            def three(out_, n, k, x, start, stop):
                wh, wl = ring_hi[:, n % 2, k * P:(k + 1) * P], ring_lo[:, n % 2, k * P:(k + 1) * P]
                pe.matmul(out_, wh, x[0], start=start, stop=False, skip_group_check=True)
                pe.matmul(out_, wh, x[1], start=False, stop=False, skip_group_check=True)
                return pe.matmul(out_, wl, x[0], start=False, stop=stop, skip_group_check=True)

            def product(q, blocks, rhs, it=0, per_q=0, per_n=0, chunk_wait=None):
                if q >= NBANK:
                    pe.wait_ge(evac, it * per_q + q - NBANK + 1)
                k = 0
                total = sum(c for _, c in blocks)
                for n, c in blocks:
                    ready(n, it, per_n)
                    for j in range(c):
                        if chunk_wait is not None:
                            chunk_wait(k)
                        mm = three(bank[q % NBANK][:, :], n, j, rhs[k], k == 0, k == total - 1)
                        k += 1
                    mm.then_inc(block_used, 1)

            def norm_sum(i, k):
                pe.wait_ge(sq_ready, KD * i + k + 1)
                mm = pe.matmul(bank[4][:, :], cc("ones"), tile(NORM[i][0] + k % 2), start=(k == 0), stop=(k == KD - 1),
                               skip_group_check=True)
                mm.then_inc(sq_used if k < KD - 1 else sum_ready, 1)

            def norm_sums(i, parts):
                for k in range(parts):
                    norm_sum(i, k)

            pe.wait_ge(in_cst, 16)
            norm_sums(0, KD)
            def xs_chunks(u):
                return lambda k: pe.wait_ge(xs_ready, KD * u + k + 1)

            for n in range(N_FOX):
                product(n, [(n, KD)], XS, chunk_wait=xs_chunks(0) if n == 0 else None)
            q = N_FOX + N_RW

            def rw_quarter(i):
                n, part = N_FOX + i // 4, i % 4
                if part == 0:
                    pe.wait_ge(evac, n - 1)
                    ready(n)
                for k in (2 * part, 2 * part + 1):
                    mm = three(bank[n % 2][:, :], n, k, XS[k], k == 0, k == KD - 1)
                if part == 3:
                    mm.then_inc(block_used, 1)


            for s in range(TT):
                pe.wait_ge(evac, N_FOX)
                for m in range(NPAIR):
                    tr = pe.transpose(bank[4 + s][:, m * P:(m + 1) * P], tile(VF0 + m)[:, s * P:(s + 1) * P], cc("ident"))
                tr.then_inc(vt_ready, 1)
            units = [(h, t) for h in range(8) for t in range(TT)]

            def fox_scores(u):
                h, t = units[u]
                m, e = h // 2, h % 2
                n = (t + 1) * P
                b = bank[4 + u % 2]
                if u < 2:
                    pe.wait_ge(vt_out, TT)
                if u == 0:
                    pe.wait_ge(fc_ready, 1)
                    pe.wait_ge(in_small, 32)
                if u >= 2:
                    pe.wait_ge(fexp, u - 1)
                    pe.wait_ge(fmax, u - 1)
                rows = slice(e * HD, (e + 1) * HD)
                pe.matmul(b[:, 0:n], tile(Q0 + m)[rows, t * P:(t + 1) * P], tile(K0 + m)[rows, 0:n],
                          start=True, stop=False, skip_group_check=True)
                sel = selr[32:40, h // 4, (h % 4) * P:(h % 4 + 1) * P]
                for part in range(2):
                    pe.matmul(b[:, 0:n], sel, cumr[32:40, part, 0:n], start=False, stop=False, skip_group_check=True)
                pe.matmul(b[:, t * P:n], maskr[:, 0, 0:P], maskr[:, 0, P:2 * P], start=False, stop=True,
                          skip_group_check=True).then_inc(fs_ready, 1)

            def fox_out(u):
                h, t = units[u]
                m, e = h // 2, h % 2
                bt, bo = bank[6 + u % 2], bank[2 + m % 2]
                if u < 2 * N_RW:
                    rw_quarter(2 * u)
                pe.wait_ge(fnorm, u + 1)
                if u >= 2:
                    pe.wait_ge(ft_out, u - 1)
                for s in range(t + 1):
                    tr = pe.transpose(bt[:, s * P:(s + 1) * P], tile(PR0 + u % 2)[:, s * P:(s + 1) * P], cc("ident"))
                tr.then_inc(ft_ready, 1)
                if u < 2 * N_RW:
                    rw_quarter(2 * u + 1)
                pe.wait_ge(ft_out, u + 1)
                if u == 0:
                    pe.wait_ge(evac, N_FOX)
                if e == 0 and t == 0 and m >= 2:
                    pe.wait_ge(fo_out, m - 1)
                for s in range(t + 1):
                    mm = pe.matmul(bo[e * HD:(e + 1) * HD, t * P:(t + 1) * P], tile(VT0 + s)[:, h * HD:(h + 1) * HD],
                                   tile(PT0 + u % 2)[:, s * P:(s + 1) * P], start=(s == 0), stop=(s == t),
                                   skip_group_check=True)
                mm.then_inc(fo_ready, 1)

            fox_scores(0)
            for u in range(len(units)):
                if u + 1 < len(units):
                    fox_scores(u + 1)
                fox_out(u)

            def head_sums(b, m, src):
                for t in range(TT):
                    mm = pe.matmul(bank[b][:, t * 8 + 2 * m:t * 8 + 2 * m + 2], src[:, t * P:(t + 1) * P],
                                   cc("bones").rearrange("p (e d) -> p e d", e=2)[:, :, 0], start=True, stop=True,
                                   skip_group_check=True)
                return mm

            def spread(first, banks):
                for m in range(NPAIR):
                    for t in range(TT):
                        mm = pe.transpose(bank[banks[m]][:, t * P:(t + 1) * P], tile(first + t)[:, m * P:(m + 1) * P], cc("ident"))
                return mm

            su = arena[:, SMALL:SMALL + 3, :]
            pe.wait_ge(in_small, 32)
            pe.wait_ge(fo_out, NPAIR)
            pe.wait_ge(rw_act, 3)
            for m in range(NPAIR):
                cols = slice(m * P, (m + 1) * P)
                if m >= 1:
                    pe.wait_ge(rw_act, 3 + 3 * m)
                pe.matmul(bank[0][:, :], su[0:64, 0, cols], tile(LAT)[0:64, :], start=True, stop=True).then_inc(rw_pe, 1)
                pe.matmul(bank[1][:, :], su[64:128, 0, cols], tile(LAT)[64:128, :], start=True, stop=True).then_inc(rw_pe, 1)
                pe.matmul(bank[2][:, :], su[:, 1, cols], tile(GL), start=True, stop=False)
                pe.matmul(bank[2][:, :], su[0:32, 2, cols], tile(GFT)[0:32, :], start=False, stop=True).then_inc(rw_pe, 1)
            for m in range(NPAIR):
                pe.wait_ge(rw_act, 15 + m + 1)
                head_sums(4, m, tile(DT4[m])).then_inc(rw_pe, 1)
            pe.wait_ge(rw_inv, 1)
            spread(RT4, (0, 1, 2, 3)).then_inc(rw_inv_out, 1)
            for m in range(NPAIR):
                pe.wait_ge(rw_dve, 2 * m + 1)
                pe.matmul(bank[5][:, :], cc("bones"), tile(RAW), start=True, stop=True).then_inc(rw_pe, 1)
            pe.wait_ge(rw_dve, 8)
            for i, (src, _) in enumerate(((TA, MA), (TB, MB), (TK, MK), (RV, MV))):
                for m in range(NPAIR):
                    j = 4 * i + m
                    if j >= 2:
                        pe.wait_ge(rw_act, 20 + j - 1)
                    for g in range(TT):
                        tr = pe.transpose(bank[j % 2][:, g * P:(g + 1) * P], tile(src + m)[:, g * P:(g + 1) * P], cc("ident"))
                    tr.then_inc(rw_pe, 1)
            for m in range(NPAIR):
                for e in range(2):
                    rows = slice(e * HD, (e + 1) * HD)
                    if m == 0:
                        pe.wait_ge(rw_act, 36)
                    else:
                        pe.wait_ge(rw_act, 36 + RW_ACT * m)
                        pe.wait_ge(rw_dve, 8 + RW_DVE * m)
                    b0 = 3 * e
                    for k, (l, r) in enumerate(((TA, TB), (TB, TA), (TK, TA))):
                        for g in range(TT):
                            cols = slice(g * P, (g + 1) * P)
                            mm = pe.matmul(bank[b0 + k][:, cols], tile(l + m)[rows, cols], tile(r + m)[rows, cols],
                                           start=True, stop=True, skip_group_check=True)
                    mm.then_inc(rw_pe, 1)
                for lev in range(5):
                    for e in range(2):
                        hs, b0 = HS[e], 3 * e
                        a, b = (0, 1) if lev % 2 == 0 else (1, 0)
                        pe.wait_ge(rw_dve, 8 + RW_DVE * m + 2 * lev + e + 1)
                        for g in range(TT):
                            cols = slice(g * P, (g + 1) * P)
                            mm = pe.matmul(bank[b0][:, cols], tile(hs[2 + a])[:, cols], tile(hs[a])[:, cols],
                                           start=True, stop=True, skip_group_check=True)
                            if lev == 4:
                                continue
                            mm = pe.matmul(bank[b0 + 1][:, cols], tile(hs[a])[:, cols], tile(hs[2 + a])[:, cols],
                                           start=True, stop=True, skip_group_check=True)
                        mm.then_inc(rw_pe, 1)
                    for e in range(2):
                        hs, b0 = HS[e], 3 * e
                        a, b = (0, 1) if lev % 2 == 0 else (1, 0)
                        pe.wait_ge(rw_act, 36 + RW_ACT * m + 2 * lev + e + 1)
                        for g in range(TT):
                            cols = slice(g * P, (g + 1) * P)
                            mm = pe.matmul(bank[b0 + 2][:, cols], tile(hs[b])[:, cols], tile(hs[4 + a])[:, cols],
                                           start=True, stop=True, skip_group_check=True)
                        mm.then_inc(rw_pe, 1)
                for e in range(2):
                    hs, b0 = HS[e], 3 * e
                    cols_h = slice(e * HD, (e + 1) * HD)
                    pe.wait_ge(rw_dve, 8 + RW_DVE * m + 10 + e + 1)
                    for g in range(TT):
                        mm = pe.matmul(bank[b0][:, g * HD:(g + 1) * HD], tile(hs[6])[:, g * P:(g + 1) * P],
                                       v4(tile(MV + m))[:, g, cols_h], start=True, stop=True, skip_group_check=True)
                    mm.then_inc(rw_pe, 1)
                    for g in range(TT):
                        mm = pe.matmul(bank[b0 + 1][e * HD:(e + 1) * HD, g * P:(g + 1) * P], v4(tile(MA + m))[:, g, cols_h],
                                       tile(hs[5])[:, g * P:(g + 1) * P], start=True, stop=True, skip_group_check=True)
                    mm.then_inc(rw_pe, 1)
                for e in range(2):
                    hs, b0 = HS[e], 3 * e
                    pe.wait_ge(rw_act, 36 + RW_ACT * m + 10 + 2 * e + 1)
                    for g in range(TT):
                        mm = pe.matmul(bank[b0 + 2][:, g * HD:(g + 1) * HD], tile(hs[5])[:, g * P:(g + 1) * P],
                                       tile(hs[7])[:, g * HD:(g + 1) * HD], start=True, stop=True, skip_group_check=True)
                    mm.then_inc(rw_pe, 1)
            base_pe, base_act, base_dve = 36 + RW_PE * 4, 36 + RW_ACT * 4, 8 + RW_DVE * 4
            shv = arena[:, SH:SH + 4, :].rearrange("p a b -> p (a b)").rearrange("p (c n) -> p c n", c=NCH)
            def head_scores(h, k):
                m, e = h // 2, h % 2
                rows = slice(e * HD, (e + 1) * HD)
                for g in range(TT):
                    cols = slice(g * P, (g + 1) * P)
                    mm = pe.matmul(bank[2 * e + k][:, cols], tile((TK, TB)[k] + m)[rows, cols], tile(TR + m)[rows, cols],
                                   start=True, stop=True, skip_group_check=True)
                mm.then_inc(rw_pe, 1)

            pe.wait_ge(rw_act, base_act)
            pe.wait_ge(rw_dve, base_dve)
            for c in range(NCH):
                g, p = c // 2, c % 2
                trow = slice(p * HD, (p + 1) * HD)
                if c > 0:
                    pe.wait_ge(rw_dve, base_dve + 4 * c - 1)
                    for h in range(8):
                        m, e = h // 2, h % 2
                        rows = slice(e * HD, (e + 1) * HD)
                        mm = pe.matmul(bank[6 - e][trow, m * HD:(m + 1) * HD], tile(WT + m)[rows, c * C:(c + 1) * C],
                                       shv[rows, c, m * HD:(m + 1) * HD], start=True, stop=True, skip_group_check=True)
                    mm.then_inc(rw_pe, 1)
                head_scores(c, 0)
                if c < NCH - 1:
                    pe.wait_ge(rw_dve, base_dve + 4 * c + 1)
                    for h in range(8):
                        m, e = h // 2, h % 2
                        rows = slice(e * HD, (e + 1) * HD)
                        dst = bank[7][rows, m * HD:(m + 1) * HD]
                        pe.matmul(dst, v4(tile(MK + m))[trow, g, rows], v4(tile(MV + m))[trow, g, rows],
                                  start=True, stop=False, skip_group_check=True)
                        mm = pe.matmul(dst, v4(tile(MB + m))[trow, g, rows], tile(UU + g)[trow, h * HD:(h + 1) * HD],
                                       start=False, stop=True, skip_group_check=True)
                    mm.then_inc(rw_pe, 1)
                head_scores(c, 1)
            bp, bd, ba = base_pe + 30, base_dve + 31, base_act
            pe.wait_ge(rw_dve, bd)
            for h in range(8):
                m, e = h // 2, h % 2
                rows = slice(e * HD, (e + 1) * HD)
                yb = bank[4 + m % 2]
                if e == 0 and m >= 2:
                    pe.wait_ge(rw_act, ba + m - 1)
                for g in range(TT):
                    cols = slice(g * P, (g + 1) * P)
                    pe.matmul(yb[rows, cols], v4(tile(MV + m))[:, g, rows], tile(MS[h][0])[:, cols],
                              start=True, stop=False, skip_group_check=True)
                    mm = pe.matmul(yb[rows, cols], tile(UU + g)[:, h * HD:(h + 1) * HD], tile(MS[h][1])[:, cols],
                                   start=False, stop=False, skip_group_check=True)
                    for c in (2 * g, 2 * g + 1):
                        if c:
                            mm = pe.matmul(yb[rows, c * C:(c + 1) * C], shv[rows, c, m * HD:(m + 1) * HD],
                                           tile(TR + m)[rows, c * C:(c + 1) * C], start=False, stop=(c % 2 == 1),
                                           skip_group_check=True)
                mm.then_inc(rw_pe, 1)
            bp += 8
            for m in range(NPAIR):
                pe.wait_ge(rw_act, ba + 4)
                pe.matmul(bank[4 + m][:, :], cc("bmean"), tile(YY + m), start=True, stop=True).then_inc(rw_pe, 1)
            ba += 4

            def w_out_block(b):
                n, part = B_WOUT + b, b // 2 % 2
                ready(n)
                for a in range(2):
                    k = 4 * (b // 4) + 2 * (b % 2) + a
                    if part == 0:
                        pe.wait_ge(evac, q + max(k - 3, 0))
                    for j in range(4):
                        if b in (0, 2) and a == 0:
                            pe.wait_ge(xs_ready, KD + 4 * part + j + 1)
                        mm = three(bank[(q + k) % NBANK][:, :], n, 4 * a + j, XS[4 * part + j], part == 0 and j == 0,
                                   part == 1 and j == 3)
                mm.then_inc(block_used, 1)

            w_out_block(0)
            for m in range(NPAIR):
                pe.wait_ge(rw_act, ba + m + 1)
                head_sums(4, m, tile(GNS + m)).then_inc(rw_pe, 1)
            w_out_block(1)
            pe.wait_ge(rw_inv, 2)
            spread(GNR, (4, 5, 6, 7)).then_inc(rw_inv_out, 1)
            bp, bd, ba = bp + 8, bd + 8, ba + 8

            for b in range(2, KD):
                w_out_block(b)
                for k in {4: (0, 1), 5: (2, 3), 7: (4, 5, 6, 7)}.get(b, ()):
                    norm_sum(1, k)
            q += KD
            norm_sums(2, KD)
            with pe.Fori(0, KF // 2) as i:
                for j in range(4):
                    product(q + j, [(B_FFN + j, KD)], XS, i, 4, 4, xs_chunks(2) if j == 0 else None)
            q += 2 * KF
            pe.wait_ge(ffn_pair, KF + 2)
            for k in range(KD):
                n = B_DOWN + 3 * k
                product(q, [(n, 8), (n + 1, 8), (n + 2, KF - 16)], HID)
                q += 1
                if k:
                    norm_sum(3, k - 1)
            norm_sum(3, KD - 1)
            norm_sums(4, KD)

            H_ = HGT
            with pe.Fori(0, HG_H) as h:
                for j in range(3):
                    product(q + j, [(B_HG + j, KD)], XS, h, 4, 4, xs_chunks(3) if j == 0 else None)
                pe.wait_ge(evac, h * 4 + q + 2)
                for g in range(TT):
                    tr = pe.transpose(bank[4][:, g * P:(g + 1) * P], tile(H_["I"])[:, g * P:(g + 1) * P], cc("ident"))
                tr.then_inc(hg_pe, 1)
                pe.wait_ge(hg_dve, h * 6 + 4)
                for g in range(TT):
                    tr = pe.transpose(bank[5][:, g * P:(g + 1) * P], tile(H_["KD"])[:, g * P:(g + 1) * P], cc("ident"))
                tr.then_inc(hg_pe, 1)
                for g in range(TT):
                    cols = slice(g * P, (g + 1) * P)
                    mm = pe.matmul(bank[6][:, cols], tile(H_["KD"])[:, cols], tile(H_["QD"])[:, cols],
                                   start=True, stop=True, skip_group_check=True)
                mm.then_inc(hg_pe, 1)
                pe.wait_ge(hg_act, h * 6 + 4)
                for c in range(NCH - 1):
                    rows = slice((c % 2) * C, (c % 2 + 1) * C)
                    mm = pe.matmul(bank[4 + c % 2][:, (c // 2) * P:(c // 2 + 1) * P], v4(tile(H_["KT"]))[rows, c // 2, :],
                                   v4(tile(H_["IT"]))[rows, c // 2, :], start=True, stop=True, skip_group_check=True)
                mm.then_inc(hg_pe, 1)
                product(q + 3, [(B_HG + 3, KD)], XS, h, 4, 4)
                pe.wait_ge(hg_dve, h * 6 + 6)
                for g in range(TT):
                    cols = slice(g * P, (g + 1) * P)
                    pe.matmul(bank[7][:, cols], v4(tile(H_["IT"]))[:, g, :], tile(H_["AM"])[:, cols],
                              start=True, stop=False, skip_group_check=True)
                    for c in (2 * g, 2 * g + 1):
                        if c:
                            mm = pe.matmul(bank[7][:, c * C:(c + 1) * C], H_["S"](c), tile(H_["QD"])[:, c * C:(c + 1) * C],
                                           start=False, stop=(c % 2 == 1), skip_group_check=True)
                mm.then_inc(hg_pe, 1)
                pe.wait_ge(hg_act, h * 6 + 5)
                pe.matmul(bank[6][:, :], cc("ones"), tile(H_["SQ"]), start=True, stop=True).then_inc(hg_pe, 1)
            q += 4 * HG_H
            R_ = RTT
            with pe.Fori(0, RET_H) as h:
                for j in range(8):
                    product(q + j, [(B_RET + j, KD)], XS, h, 12, 12)

                def v_by_token(s):
                    if s >= 2:
                        pe.wait_ge(rt_act, h * 9 + s - 1)
                    else:
                        pe.wait_ge(evac, h * 12 + q + 8)
                    for j in range(4):
                        tr = pe.transpose(bank[4 + 3 * (s % 2)][:, j * P:(j + 1) * P], tile(R_["VF"] + j)[:, s * P:(s + 1) * P],
                                          cc("ident"))
                    tr.then_inc(rt_pe, 1)

                def scores(s):
                    if s == 0:
                        pe.wait_ge(rt_dve, h * 12 + 1 + 4)
                    if s >= 2:
                        pe.wait_ge(rt_dve, h * 12 + 1 + 4 + s - 1)
                    b = bank[5 + s % 2]
                    n = T - s * P
                    for j in range(2):
                        mm = pe.matmul(b[:, 0:n], tile(R_["KR"] + j)[:, s * P:(s + 1) * P], tile(R_["QR"] + j)[:, s * P:T],
                                       start=(j == 0), stop=(j == 1))
                    mm.then_inc(rt_pe, 1)

                scores(0)
                scores(1)
                v_by_token(0)
                v_by_token(1)
                scores(2)
                scores(3)
                v_by_token(2)
                v_by_token(3)
                for j in range(4):
                    product(q + 8 + j, [(B_RET + 8 + j, KD)], XS, h, 12, 12)
                    if j == 0:
                        pe.wait_ge(rt_dve, h * 12 + 1 + 8)
                        pe.wait_ge(rt_act, h * 9 + 4)
                    else:
                        pe.wait_ge(rt_act, h * 9 + 4 + j)
                        pe.matmul(bank[4][:, :], cc("ones"), tile(R_["SQ"]), start=(j == 1), stop=False).then_inc(rt_pe, 1)
                    for t in range(TT):
                        for s in range(t + 1):
                            mm = pe.matmul(bank[7][:, t * P:(t + 1) * P], tile(R_["VT"] + s)[:, j * P:(j + 1) * P],
                                           tile(R_["AM"] + s)[:, (t - s) * P:(t - s + 1) * P], start=(s == 0), stop=(s == t),
                                           skip_group_check=True)
                    mm.then_inc(rt_pe, 1)
                pe.wait_ge(rt_act, h * 9 + 8)
                pe.matmul(bank[4][:, :], cc("ones"), tile(R_["SQ"]), start=False, stop=True).then_inc(rt_pe, 1)
            q += 12 * RET_H
            for k in range(KD):
                n = B_MERGE + 5 * k
                product(q, [(n, KD)], XS)
                product(q + 1, [(n + 1, KD)], XS)
                product(q + 2, [(n + 2, KD)], OHL[:8], chunk_wait=(lambda c: pe.wait_ge(o_ready, c + 1)) if k == 0 else None)
                product(q + 3, [(n + 3, KD), (n + 4, KD)], OHL[8:],
                        chunk_wait=(lambda c: pe.wait_ge(o_ready, 8 + c + 1)) if k == 0 else None)
                q += 4
            for k in range(KD):
                product(q, [(B_WOUT2 + k, KD)], XS, chunk_wait=xs_chunks(4) if k == 0 else None)
                q += 1
            norm_sums(5, KD)
            for k in range(2 * PEER_H):
                product(q, [(B_PQ + k, KD)], XS, chunk_wait=xs_chunks(5) if k == 0 else None)
                q += 1
            pe.wait_ge(evac, q)
            pe.wait_ge(in_keys, 16)
            keys = arena[:, PSUB:PSUB + 4, :].rearrange("p a b -> p (a b)")
            for t in range(TT):
                for n in range(16):
                    if t and n % 4 == 0:
                        pe.wait_ge(tk_act, 4 * (t - 1) + n // 4 + 1)
                    mm = pe.matmul(bank[4 + n // 4][:, (n % 4) * P:(n % 4 + 1) * P], tile(PQ + n)[:, t * P:(t + 1) * P],
                                   keys[:, n * P:(n + 1) * P], start=True, stop=True, skip_group_check=True)
                    if n % 4 == 3:
                        mm.then_inc(tk_pe, 1)
            with pe.Fori(0, TT) as t:
                for j in range(NU_ROUTE):
                    product(q + j, [(B_U + j, KD)], XS, t, NU_ROUTE, NU_ROUTE)
                pe.wait_ge(tk_dve, t + 1)
                pe.wait_ge(tk_act, t + 16)
                for j in range(3):
                    tr = pe.transpose(bank[4][:, j * P:(j + 1) * P], pairs[:, j, :], cc("ident"))
                tr.then_inc(tk_pe, 1)
            q += NU_ROUTE * TT
            n = B_U + NU_ROUTE * TT
            pe.wait_ge(tk_act, 20)
            pe.sem_inc(oh_pe, 2)
            with pe.Fori(0, NTG // 2) as i:
                for b in range(2 * NU_GATES):
                    product(q + b, [(n + b, KD)], XS, i, 2 * NU_GATES, 2 * NU_GATES)
                    for u in (2 * b, 2 * b + 1):
                        pe.wait_ge(oh_dve, i * 16 + u + 1)
                        pe.wait_ge(oh_act, i * 16 + u + 1)
                        for j in range(4):
                            dst = bank[5 + u % 2][:, j * P:(j + 1) * P]
                            pe.matmul(dst, oneH[:, u % 2, j, :], oneB[:, u % 2, j, :], start=True, stop=False,
                                      skip_group_check=True)
                            mm = pe.matmul(dst, oneL[:, u % 2, j, :], oneB[:, u % 2, j, :], start=False, stop=True,
                                           skip_group_check=True)
                        mm.then_inc(oh_pe, 1)
            q += NU_GATES * NTG
            n += NU_GATES * NTG
            with pe.Fori(0, NU_REST // 4) as i:
                for b in range(4):
                    product(q + b, [(n + b, KD)], XS, i, 4, 4)
            q += NU_REST
            assert n + NU_REST == B_V

            def v_group(g, it=0):
                n = B_V + JG * g
                for half in range(2):
                    if g:
                        pe.wait_ge(ex_acc, it * 16 + 8 * (g - 1) + 4 * half + 4)
                    for b in range(4):
                        ready(n + 4 * half + b, it, 2 * JG)
                        for jj in range(2):
                            j = 2 * b + jj
                            if half == 0:
                                pe.wait_ge(ex_lo, it * 2 * JG + g * JG + j + 1)
                            for d in range(4):
                                mm = three(bank[4 * half + d][:, :], n + 4 * half + b, jj * 4 + d, GW[g % 2][j],
                                           j == 0, j == JG - 1)
                        mm.then_inc(block_used, 1)

            pe.wait_ge(evac, q)
            pe.wait_ge(oh_act, 8 * NTG + 2)
            v_group(0)
            v_group(1)
            with pe.Fori(0, NJG // 2 - 1) as i:
                v_group(2, i)
                v_group(3, i)
            norm_sums(6, KD)

        @block.scalar
        def _(act):
            st = Steps(act, act_s)

            def A(out_, in_, f, **kw):
                return act.activation(out_, in_, f, **kw)

            act.dma_start(par[:, :], par_d).then_inc(in_par, 16)
            act.dma_start(cst[:, :], cst_d).then_inc(in_cst, 16)
            for i in range(4):
                act.dma_start(xres[:, 2 * i:2 * i + 2, :], xt.rearrange("(k p) t -> p k t", p=P)[:, 2 * i:2 * i + 2, :]
                              ).then_inc(in_x[i], 16)
            act.dma_start(arena[:, SMALL:SMALL + 3, :], small_d).then_inc(in_small, 16)
            act.dma_start(arena[32:40, SELT:SELT + 2, :].rearrange("p a b -> p (a b)"), sel_d).then_inc(in_small, 16)
            act.wait_ge(in_par, 16)

            def norm_square(i, k, src):
                if k >= 2:
                    act.wait_ge(sq_used, (KD - 1) * i + k - 1)
                elif i:
                    act.wait_ge(root_used, i)
                A(tile(NORM[i][0] + k % 2), src(k), ACT.Square).then_inc(sq_ready, 1)

            def norm_root(i):
                act.wait_ge(sum_ready, i + 1)
                A(tile(NORM[i][0]), bank[4][:, :], ACT.Sqrt, scale=1.0 / D, bias=pp("eps")).then_inc(root_ready, 1)

            def norm_squares(i, src, first_wait):
                for k in range(KD):
                    first_wait(k)
                    norm_square(i, k, src)
                norm_root(i)

            def xs_hi(src, wait):
                for k in range(KD):
                    wait(k)
                    A(XS[k][0], src(k), ACT.Copy).then_inc(hi_ready, 1)

            def norm_hi(i, count):
                xs_hi(lambda k: tile(NORM[i][2] + k % 2), lambda k: act.wait_ge(scaled, count + k + 1))

            norm_squares(0, xr, lambda k: act.wait_ge(in_x[k // 2], 16))
            norm_hi(0, 0)
            for n in range(N_FOX):
                act.wait_ge(block_used, n + 1)
                A(tile((Q0 + n, K0 + n - 4, RAW, VF0 + n - 9)[0 if n < 4 else 1 if n < 8 else 2 if n == 8 else 3]),
                  bank[n % NBANK][:, :], ACT.Copy).then_inc(evac, 1)
                if n == 10:
                    act.wait_ge(shifted, 1)
                    act.wait_ge(fc_z, 1)
                    z = arena[32:40, BON + 1, :]
                    st(A(z, z, ACT.Exp, scale=-1.0))
                    A(z, z, ACT.Ln, bias=1.0).then_inc(fc_ln, 1)
            q = N_FOX + N_RW
            for s in range(TT):
                act.wait_ge(vt_ready, s + 1)
                A(tile(VT0 + s), bank[4 + s][:, :], ACT.Copy).then_inc(vt_out, 1)

            units = [(h, t) for h in range(8) for t in range(TT)]

            def fox_exp(u):
                h, t = units[u]
                n = (t + 1) * P
                act.wait_ge(fmax, u + 1)
                if u >= 2:
                    act.wait_ge(ft_ready, u - 1)
                A(tile(PR0 + u % 2)[:, 0:n], bank[4 + u % 2][:, 0:n], ACT.Exp, scale=0.125, bias=stat[:, 32 + u:33 + u],
                  accum_out=stat[:, 64 + u % 32:65 + u % 32]).then_inc(fexp, 1)

            def fox_copy(u):
                h, t = units[u]
                n = (t + 1) * P
                act.wait_ge(ft_ready, u + 1)
                if u >= 2:
                    act.wait_ge(fo_ready, u - 1)
                A(tile(PT0 + u % 2)[:, 0:n], bank[6 + u % 2][:, 0:n], ACT.Copy).then_inc(ft_out, 1)
                if h % 2 == 1 and t == TT - 1:
                    act.wait_ge(fo_ready, u + 1)
                    m = h // 2
                    A(tile(OF + m), bank[2 + m % 2][:, :], ACT.Copy).then_inc(fo_out, 1)

            fox_exp(0)
            for u in range(len(units)):
                if u + 1 < len(units):
                    fox_exp(u + 1)
                fox_copy(u)
                if u % 2 == 1 and u < 2 * N_RW:
                    n = N_FOX + u // 2
                    act.wait_ge(block_used, n + 1)
                    if n >= 14:
                        act.wait_ge(shifted, n - 13)
                    A(tile(RAW + n % 2), bank[n % 2][:, :], ACT.Copy).then_inc(evac, 1)
            act.wait_ge(shifted, N_RW + 1)
            A(tile(LAT)[0:64, :], tile(LAT)[0:64, :], ACT.Tanh).then_inc(rw_act, 1)
            A(tile(GL), tile(GL), ACT.Sigmoid).then_inc(rw_act, 1)
            A(tile(GFT)[0:32, :], tile(GFT)[0:32, :], ACT.Sigmoid).then_inc(rw_act, 1)

            for m in range(NPAIR):
                act.wait_ge(rw_pe, 3 * m + 1)
                A(tile(LW + m), bank[0][:, :], ACT.Sigmoid, bias=pp("w0", m)).then_inc(rw_act, 1)
                act.wait_ge(rw_pe, 3 * m + 2)
                A(tile(RA + m), bank[1][:, :], ACT.Sigmoid, bias=pp("a0", m)).then_inc(rw_act, 1)
                act.wait_ge(rw_pe, 3 * m + 3)
                A(tile(RG + m), bank[2][:, :], ACT.Copy).then_inc(rw_act, 1)
            for m in range(NPAIR):
                A(tile(DT4[m]), tile(RK + m), ACT.Square, scale=pp("k_k", m)).then_inc(rw_act, 1)
            act.wait_ge(rw_pe, 16)
            A(roots[:, 0, :], bank[4][:, 0:TT * 8], ACT.Sqrt).then_inc(rw_act, 1)
            for m in range(NPAIR):
                if m:
                    act.wait_ge(rw_dve, 2 * m)
                act.wait_ge(cum_ready, m + 1)
                st.go(A(tile(EL + 4), tile(EL + 1), ACT.Exp, scale=-E_HALF))
                st.go(A(tile(EL + 5), tile(EL + 1), ACT.Exp, scale=E_HALF))
                st.go(A(tile(EL + 6), tile(EL + 2), ACT.Exp, scale=-E_HALF))
                A(dch[:, 0, m * NCH:(m + 1) * NCH], ch(tile(EL + 3))[:, :, MID], ACT.Exp, scale=-E_HALF).then_inc(exp_ready, 1)
            for i, dst in enumerate((MA, MB, MK, MV)):
                for m in range(NPAIR):
                    act.wait_ge(rw_pe, 20 + 4 * i + m + 1)
                    A(tile(dst + m), bank[(4 * i + m) % 2][:, :], ACT.Copy).then_inc(rw_act, 1)
            for m in range(NPAIR):
                pb = 36 + RW_PE * m
                for lev in range(5):
                    for e in range(2):
                        hs, b0 = HS[e], 3 * e
                        b = 1 if lev % 2 == 0 else 0
                        act.wait_ge(rw_pe, pb + 2 + 4 * lev + e + 1)
                        A(tile(hs[b]), bank[b0][:, :], ACT.Copy).then_inc(rw_act, 1)
                for e in range(2):
                    hs, b0 = HS[e], 3 * e
                    act.wait_ge(rw_pe, pb + 22 + 2 * e + 1)
                    A(tile(hs[7])[:, 0:256], bank[b0][:, 0:256], ACT.Copy).then_inc(rw_act, 1)
                    act.wait_ge(rw_pe, pb + 22 + 2 * e + 2)
                    A(tile(WT + m)[e * HD:(e + 1) * HD, :], bank[b0 + 1][e * HD:(e + 1) * HD, :], ACT.Copy).then_inc(rw_act, 1)
                for e in range(2):
                    b0 = 3 * e
                    h = 2 * m + e
                    act.wait_ge(rw_pe, pb + 26 + e + 1)
                    A(arena[:, U0:U0 + 4, h * HD:(h + 1) * HD], bank[b0 + 2][:, 0:256].rearrange("p (g i) -> p g i", g=4),
                      ACT.Copy).then_inc(rw_act, 1)
            bp = 36 + RW_PE * 4 + 30
            ba = 36 + RW_ACT * 4
            for m in range(NPAIR):
                act.wait_ge(rw_pe, bp + 2 * m + 2)
                A(tile(YY + m), bank[4 + m % 2][:, :], ACT.Copy).then_inc(rw_act, 1)
            bp += 8
            ba += 4
            bd = 8 + RW_DVE * 4 + 15 + 16
            for k in range(4):
                A(XS[k][0], tile(OF + k), ACT.Copy).then_inc(hi_ready, 1)
            for m in range(NPAIR):
                act.wait_ge(rw_dve, bd + m + 1)
                A(tile(GNS + m), tile(GND + m), ACT.Square).then_inc(rw_act, 1)
            act.wait_ge(rw_pe, bp + 8)
            A(roots[:, 0, :], bank[4][:, 0:TT * 8], ACT.Sqrt, scale=1.0 / HD, bias=pp("ln_eps")).then_inc(rw_act, 1)

            for k in range(4):
                act.wait_ge(rw_dve, bd + 4 + k + 1)
                A(XS[4 + k][0], tile(ORW + k), ACT.Copy).then_inc(hi_ready, 1)
            for k in range(KD):
                act.wait_ge(block_used, B_WOUT + 4 * (k // 4) + 2 + k % 4 // 2 + 1)
                A(tile(MO[1] + k), bank[q % NBANK][:, :], ACT.Copy).then_inc(evac, 1)
                q += 1
                act.wait_ge(evac, q)
                norm_square(1, k, lambda k: tile(MO[1] + k))
            norm_root(1)
            norm_squares(2, xr, lambda k: act.wait_ge(resid_ready, k + 1))
            norm_hi(2, KD)
            with act.Fori(0, KF // 2) as i:
                for j in range(4):
                    act.wait_ge(block_used, i * 4 + B_FFN + j + 1)
                    act.wait_ge(ffn_pair, i * 2 + j // 2 + 1)
                    A(gu[:, j, :], bank[(q + j) % NBANK][:, :], ACT.Silu if j % 2 == 0 else ACT.Copy).then_inc(evac, 1)
            q += 2 * KF
            act.wait_ge(ffn_pair, KF + 2)
            for k in range(KD):
                act.wait_ge(block_used, B_DOWN + 3 * (k + 1))
                A(tile(MO[3] + k), bank[q % NBANK][:, :], ACT.Copy).then_inc(evac, 1)
                q += 1
                act.wait_ge(evac, q)
                norm_square(3, k, lambda k: tile(MO[3] + k))
            norm_root(3)
            norm_squares(4, xr, lambda k: act.wait_ge(resid_ready, KD + k + 1))

            H_ = HGT
            act.dma_start(arena[:, RTT["COS"]:RTT["COS"] + 2, :], rot_d).then_inc(in_rot, 16)
            act.dma_start(arena[:, RTT["MASK"]:RTT["MASK"] + 4, :], rmask_d).then_inc(in_rot, 16)
            act.wait_ge(lb_ready, 1)
            A(lbt[:, 1:3, :], lbt[:, 1:3, :], ACT.Exp).then_inc(lb_ready, 1)
            norm_hi(4, 2 * KD)
            with act.Fori(0, HG_H) as h:
                act.wait_ge(block_used, h * 4 + B_HG + 1)
                A(tile(H_["F"]), bank[q % NBANK][:, :], ACT.Sigmoid).then_inc(evac, 1)
                act.wait_ge(hg_dve, h * 6 + 2)
                A(tile(H_["LF"]), tile(H_["F"]), ACT.Ln).then_inc(hg_act, 1)
                act.wait_ge(hg_dve, h * 6 + 3)
                A(dch[:, 4, 0:NCH], ch(tile(H_["CU"]))[:, :, MID], ACT.Exp).then_inc(hg_exp, 1)
                A(tile(H_["EP"]), tile(H_["CC"]), ACT.Exp).then_inc(hg_exp, 1)
                A(tile(H_["EM"]), tile(H_["CC"]), ACT.Exp, scale=-1.0).then_inc(hg_act, 1)
                for j, dst in ((1, "I"), (2, "Q")):
                    act.wait_ge(block_used, h * 4 + B_HG + j + 1)
                    A(tile(H_[dst]), bank[(q + j) % NBANK][:, :], ACT.Copy).then_inc(evac, 1)
                act.wait_ge(hg_pe, h * 6 + 1)
                A(tile(H_["IT"]), bank[4][:, :], ACT.Copy).then_inc(hg_act, 1)
                act.wait_ge(hg_pe, h * 6 + 2)
                A(tile(H_["KT"]), bank[5][:, :], ACT.Copy).then_inc(hg_act, 1)
                act.wait_ge(block_used, h * 4 + B_HG + 4)
                act.wait_ge(hg_dve, h * 6 + 1)
                A(tile(H_["G"]), bank[(q + 3) % NBANK][:, :], ACT.Silu).then_inc(evac, 1)
                act.wait_ge(hg_pe, h * 6 + 5)
                A(tile(H_["SQ"]), bank[7][:, :], ACT.Square).then_inc(hg_act, 1)
                act.wait_ge(hg_pe, h * 6 + 6)
                A(tile(H_["RT"]), bank[6][:, :], ACT.Sqrt, scale=1.0 / HG_D, bias=pp("eps")).then_inc(hg_act, 1)
            q += 4 * HG_H
            R_ = RTT
            act.wait_ge(hg_dve, 6 * HG_H + 1)
            with act.Fori(0, RET_H) as h:
                for j in range(8):
                    act.wait_ge(block_used, h * 12 + B_RET + j + 1)
                    if j == 0:
                        act.wait_ge(rt_dve, h * 12 + 1)
                    A(tile(R_["Q"] + j), bank[(q + j) % NBANK][:, :], ACT.Copy).then_inc(evac, 1)
                for s in range(TT):
                    act.wait_ge(rt_pe, h * 16 + (3, 4, 7, 8)[s])
                    A(tile(R_["VT"] + s), bank[4 + 3 * (s % 2)][:, :], ACT.Copy).then_inc(rt_act, 1)
                st.enter(h, 4, RET_H)
                for j in range(4):
                    act.wait_ge(block_used, h * 12 + B_RET + 8 + j + 1)
                    A(tile(R_["G"] + j), bank[(q + 8 + j) % NBANK][:, :], ACT.Silu).then_inc(evac, 1)
                    act.wait_ge(rt_pe, h * 16 + 8 + 2 * j + 1)
                    st.go(A(arena[:, bass.ds(h * 4 + (ORET + j), 1), :].rearrange("p a t -> p (a t)"), bank[7][:, :], ACT.Copy))
                    A(tile(R_["SQ"]), bank[7][:, :], ACT.Square).then_inc(rt_act, 1)
                st.leave()
                act.wait_ge(rt_pe, h * 16 + 16)
                A(tile(R_["RT"]), bank[4][:, :], ACT.Sqrt, scale=1.0 / RET_DV, bias=pp("eps")).then_inc(rt_act, 1)
            q += 12 * RET_H
            for k in range(24):
                act.wait_ge(o_lo_ready, k + 1)
                A(OHL[k][0], spl[:, k % 2, :].bitcast(F32), ACT.Copy).then_inc(o_ready, 1)
            for k in range(KD):
                for j in range(4):
                    act.wait_ge(block_used, B_MERGE + 5 * k + (5 if j == 3 else j + 1))
                    if k and j == 0:
                        act.wait_ge(mg_dve, k)
                    A(tile(MGT + j if j < 3 else MRG + k), bank[q % NBANK][:, :], ACT.Sigmoid if j < 2 else ACT.Copy
                      ).then_inc(evac, 1)
                    q += 1
            xs_hi(lambda k: tile(MRG + k), lambda k: act.wait_ge(mg_dve, KD))
            for k in range(KD):
                act.wait_ge(block_used, B_WOUT2 + k + 1)
                A(tile(WO2 + k), bank[q % NBANK][:, :], ACT.Copy).then_inc(evac, 1)
                q += 1
            norm_squares(5, xr, lambda k: act.wait_ge(resid_ready, 2 * KD + k + 1))
            act.dma_start(arena[:, PSUB:PSUB + 4, :].rearrange("p a b -> p (a b)"), keys_d).then_inc(in_keys, 16)
            norm_hi(5, 3 * KD)
            for k in range(2 * PEER_H):
                act.wait_ge(block_used, B_PQ + k + 1)
                A(tile(PQ + k), bank[q % NBANK][:, :], ACT.Copy).then_inc(evac, 1)
                q += 1
            for t in range(TT):
                for b in range(4):
                    act.wait_ge(tk_pe, 4 * t + b + 1)
                    A(tile(PST + 4 * t + b), bank[4 + b][:, :], ACT.Copy).then_inc(tk_act, 1)

            def gelu(n, b, j, it=0, per=0):
                act.wait_ge(block_used, it * per + n + 1)
                act.wait_ge(hst[j % 2], it * (8 * per) + (16 * (j // 2) + 16))
                A(tile(UT + j % 2), bank[b % NBANK][:, :], ACT.Gelu_apprx_tanh).then_inc(evac, 1)
                act.wait_ge(evac, it * per + b + 1)
                act.dma_start(hidden_d[bass.ds(it * per + j, 1)].rearrange("a p n -> (a p) n"), tile(UT + j % 2)
                              ).then_inc(hst[j % 2], 16)

            for x in hst + gst:
                act.sem_inc(x, 16)
            with act.Fori(0, TT) as t:
                for j in range(NU_ROUTE):
                    gelu(B_U + j, q + j, j, t, NU_ROUTE)
                    if j == NU_ROUTE - 4:
                        act.wait_ge(tk_sub, t + 1)
                        A(bestv[:, :, :], bestv[:, :, :], ACT.Exp).then_inc(tk_exp, 1)
                act.wait_ge(tk_pe, t + 17)
                A(arena[:, PTT:PTT + 3, bass.ds(t * P, P)], bank[4][:, 0:384].rearrange("p (j t) -> p j t", j=3),
                  ACT.Copy).then_inc(tk_act, 1)
            j0 = NU_ROUTE * TT
            q += j0
            act.wait_ge(tk_act, 20)
            act.sem_inc(oh_act, 2)
            with act.Fori(0, NTG // 2) as i:
                for hb in range(2):
                    gbuf = arena[:, GBUF + 8 * hb:GBUF + 8 * hb + 8, :].rearrange("p a b -> p (a b)")
                    by_token = gbuf.rearrange("p (j t) -> p t j", t=TG)
                    act.wait_ge(gst[hb], i * 16 + 16)
                    for b in range(NU_GATES):
                        bb = NU_GATES * hb + b
                        gelu(B_U + j0 + bb, q + bb, j0 + bb, i, 2 * NU_GATES)
                        for u in (2 * b, 2 * b + 1):
                            act.wait_ge(oh_pe, i * 16 + (8 * hb + u + 3))
                            A(by_token[:, 4 * u:4 * u + 4, :], v4(bank[5 + u % 2][:, :]), ACT.Copy).then_inc(oh_act, 1)
                    act.wait_ge(oh_act, i * 16 + (8 * hb + 10))
                    act.dma_start(gates_d[bass.ds(i * 2 + hb, 1)].rearrange("a p n -> (a p) n"), gbuf).then_inc(gst[hb], 16)
            j0 += NU_GATES * NTG
            q += NU_GATES * NTG
            for hb in range(2):
                act.wait_ge(gst[hb], 16 * (NTG // 2) + 16)
            gv = gates_d.rearrange("g p (j t) -> p g (j t)", t=TG)
            hv = hidden_d.rearrange("j p t -> p j t")

            def load(g, it=0):
                b = g % 2
                if g > 1:
                    act.wait_ge(ex_lo, it * 2 * JG + (g - 1) * JG)
                act.dma_start(arena[:, HV + 8 * b:HV + 8 * b + 8, :], hv[:, bass.ds(it * 2 * JG + g * JG, JG), :]
                              ).then_inc(gld[b], 16)
                act.dma_start(arena[:, GV + 8 * b:GV + 8 * b + 8, :].rearrange("p a b -> p (a b)").rearrange(
                    "p (g n) -> p g n", g=NTG), gv[:, 0:NTG, bass.ds(it * (2 * JG * TG) + g * (JG * TG), JG * TG)]
                              ).then_inc(gld[b], 16)

            def gated_hi(g, it=0):
                for j in range(JG):
                    act.wait_ge(ex_prod, it * 2 * JG + g * JG + j + 1)
                    A(GW[g % 2][j][0], tile(HV + 8 * (g % 2) + j), ACT.Copy).then_inc(ex_hi, 1)

            load(0)
            load(1)
            with act.Fori(0, NU_REST // 4 - 1) as i:
                for b in range(4):
                    gelu(B_U + j0 + b, q + b, j0 + b, i, 4)
            j0 += NU_REST - 4
            q += NU_REST - 4
            gated_hi(0)
            for b in range(4):
                gelu(B_U + j0 + b, q + b, j0 + b)
            for b in range(2):
                act.wait_ge(hst[b], 16 * (NKEY // 2 + 1))
            load(2)
            gated_hi(1)
            load(3)
            with act.Fori(0, NJG // 2 - 2) as i:
                gated_hi(2, i)
                load(4, i)
                gated_hi(3, i)
                load(5, i)
            gated_hi(NJG - 2)
            gated_hi(NJG - 1)
            norm_squares(6, xr, lambda k: act.wait_ge(resid_ready, 3 * KD + k + 1))

        @block.gpsimd
        def _(pool):
            one = cst[:, CCOL["ones"][0]:CCOL["ones"][0] + 1].to_broadcast([P, D])

            def split(r, it=None):
                n = r if it is None else it * RING + r
                if it is None:
                    pool.wait_ge(loaded[r], 16)
                else:
                    pool.wait_ge(loaded[r], it * 16 + 16)
                if it is not None or r >= 2:
                    pool.wait_ge(block_used, n - 1)
                pool.tensor_tensor(ring_hi[:, r % 2, :], ring[:, r, :], one, ALU.mult).then_inc(split_hi, 1)
                pool.wait_ge(split_hi, n + 1)
                pool.tensor_tensor(ring_lo[:, r % 2, :], ring[:, r, :], ring_hi[:, r % 2, :].bitcast(F32), ALU.subtract
                                   ).then_inc(w_split, 1)

            pool.wait_ge(in_cst, 16)
            for r in range(RING):
                split(r)
            with pool.Fori(1, N_LOADED // RING) as i:
                for r in range(RING):
                    split(r, i)

        @block.vector
        def _(ve):
            st = Steps(ve, dve_s)
            TSM, TTN, STT, CP = ve.tensor_scalar, ve.tensor_tensor, ve.scalar_tensor_tensor, ve.tensor_copy

            def xs_lo(u, src, k, done=None):
                ve.wait_ge(hi_ready, KD * u + k + 1)
                TTN(XS[k][1], src(k), XS[k][0].bitcast(F32), ALU.subtract).then_inc(xs_ready, 1)

            def norm_root(i):
                ve.wait_ge(root_ready, i + 1)
                ve.reciprocal(tile(NORM[i][1]), tile(NORM[i][0])).then_inc(root_used, 1)
                ve.wait_ge(root_used, i + 1)

            def norm_add(i, gain, src):
                norm_root(i)
                st.go(STT(src(0), src(0), pp(gain, 0), tile(NORM[i][1]), ALU.mult, ALU.mult))
                for k in range(KD):
                    st.sync()
                    if k + 1 < KD:
                        st.go(STT(src(k + 1), src(k + 1), pp(gain, k + 1), tile(NORM[i][1]), ALU.mult, ALU.mult))
                    TTN(xr(k), xr(k), src(k), ALU.add).then_inc(resid_ready, 1)

            def norm_scale(i, gain, u, count):
                norm_root(i)
                dst = lambda k: tile(NORM[i][2] + k % 2)
                for k in range(KD + 1):
                    if k < KD:
                        if k >= 2:
                            ve.wait_ge(xs_ready, KD * u + k - 1)
                        STT(dst(k), xr(k), pp(gain, k), tile(NORM[i][1]), ALU.mult, ALU.mult).then_inc(scaled, 1)
                    if k:
                        ve.wait_ge(scaled, count + k)
                        xs_lo(u, dst, k - 1)

            for x in in_x:
                ve.wait_ge(x, 16)
            ve.wait_ge(in_par, 16)
            ve.wait_ge(in_cst, 16)
            norm_scale(0, "attn_pre", 0, 0)
            dests = [GFT, LAT, GL] + [RR + i for i in range(4)] + [RK + i for i in range(4)] + [RV + i for i in range(4)]
            def shift(n, i):
                ve.wait_ge(evac, n + 1)
                raw, d = tile(RAW + n % 2), tile(DTMP)
                mu = pp("mu", i)
                st.go(TTN(d[:, 1:T], raw[:, 0:T - 1], raw[:, 1:T], ALU.subtract))
                st(TSM(d[:, 0:1], raw[:, 0:1], -1.0, None, ALU.mult))
                STT(tile(dests[i]), d, mu, raw, ALU.mult, ALU.add).then_inc(shifted, 1)
                ve.wait_ge(shifted, i + 1)

            shift(8, 0)
            z, a = arena[32:40, BON, :], arena[32:40, BON + 1, :]
            st(TSM(z, tile(GFT)[32:40, :], par[32:40, PCOL["f_bias"]:PCOL["f_bias"] + 1], None, ALU.add))
            st(TSM(a, z, -1.0, None, ALU.mult))
            TTN(a, a, z, ALU.max).then_inc(fc_z, 1)
            ve.wait_ge(fc_ln, 1)
            st(TSM(z, z, 0.0, None, ALU.min))
            st(TTN(z, z, a, ALU.subtract))
            st(ve.tensor_tensor_scan(tile(GFT)[32:40, :], cst[32:40, CCOL["ones"][0]:CCOL["ones"][0] + 1].to_broadcast([8, T]), z,
                                     0.0, ALU.mult, ALU.add))
            ve.wait_ge(in_small, 32)
            st.go(CP(selr[32:40, :, :], arena[32:40, SELT:SELT + 2, :]))
            st.go(CP(maskr[:, 0, 0:P], cc("ident")))
            st.go(CP(maskr[:, 0, P:2 * P], cc("neg")))
            st(CP(cumr[32:40, 0, :], tile(GFT)[32:40, :]))
            TTN(cumr[32:40, 1, :], tile(GFT)[32:40, :], cumr[32:40, 0, :].bitcast(F32), ALU.subtract).then_inc(fc_ready, 1)
            ve.wait_ge(fc_ready, 1)
            units = [(h, t) for h in range(8) for t in range(TT)]

            def fox_max(u):
                n = (units[u][1] + 1) * P
                ve.wait_ge(fs_ready, u + 1)
                st(ve.tensor_reduce(stat[:, u:u + 1], bank[4 + u % 2][:, 0:n], AX.X, ALU.max))
                TSM(stat[:, 32 + u:33 + u], stat[:, u:u + 1], -0.125, None, ALU.mult).then_inc(fmax, 1)

            def fox_norm(u):
                n = (units[u][1] + 1) * P
                ve.wait_ge(fexp, u + 1)
                st(ve.reciprocal(stat[:, u:u + 1], stat[:, 64 + u:65 + u]))
                TSM(tile(PR0 + u % 2)[:, 0:n], tile(PR0 + u % 2)[:, 0:n], stat[:, u:u + 1], None, ALU.mult).then_inc(fnorm, 1)

            fox_max(0)
            for u in range(len(units)):
                if u + 1 < len(units):
                    fox_max(u + 1)
                fox_norm(u)
                if u % 2 == 0 and 2 <= u <= 2 * N_RW:
                    shift(N_FOX + u // 2 - 1, u // 2)

            def inverse_roots(first, n):
                st(ve.reciprocal(roots[:, 1, :], roots[:, 0, :]))
                CP(arena[:, first:first + TT, :].rearrange("p t (h d) -> p (t h) d", h=8),
                   roots[:, 1, :].unsqueeze(2).to_broadcast([P, TT * 8, HD])).then_inc(rw_inv, 1)
                ve.wait_ge(rw_inv_out, n)

            ve.wait_ge(rw_act, 15)
            ve.wait_ge(fo_out, NPAIR)
            for m in range(NPAIR):
                R, K, V, kk, a = tile(RR + m), tile(RK + m), tile(RV + m), tile(KKT + m), tile(RA + m)
                if m:
                    ve.wait_ge(exp_ready, m)
                st(ve.tensor_tensor_scan(tile(EL + 3), cc("reset"), tile(LW + m), 0.0, ALU.mult, ALU.add))
                cu = ch(tile(EL + 3))
                st(TTN(ch(tile(EL + 1)), cu, cu[:, :, MID:MID + 1].to_broadcast([P, NCH, C]), ALU.subtract))
                TTN(tile(EL + 2), tile(EL + 1), tile(LW + m), ALU.subtract).then_inc(cum_ready, 1)
                if m == 0:
                    ve.wait_ge(rw_act, 20)
                    st(TSM(roots[:, 0, :], roots[:, 0, :], 1e-12, None, ALU.max))
                    inverse_roots(RT4, 1)
                st.go(STT(kk, K, pp("k_k", m), bank[m][:, :], ALU.mult, ALU.mult))
                st(TSM(tile(EL + 7), a, 1.0, pp("k_a", m), ALU.subtract, ALU.mult))
                st(STT(K, tile(EL + 7), 1.0, K, ALU.add, ALU.mult))
                STT(tile(RAW), R, pp("r_k", m), K, ALU.mult, ALU.mult).then_inc(rw_dve, 1)
                ve.wait_ge(exp_ready, m + 1)
                st.go(STT(tile(TA + m), kk, -1.0, tile(EL + 6), ALU.mult, ALU.mult))
                st.go(TTN(tile(TR + m), R, tile(EL + 4), ALU.mult))
                st.go(TTN(tile(TK + m), K, tile(EL + 5), ALU.mult))
                st(TTN(kk, kk, a, ALU.mult))
                st.go(TTN(tile(TB + m), kk, tile(EL + 5), ALU.mult))
                st.go(CP(dch[:, 1, m * NCH:(m + 1) * NCH], ch(tile(EL + 4))[:, :, C - 1]))
                ve.wait_ge(rw_pe, 16 + m + 1)
                st.sync()
                TTN(tile(BON + m), bank[5][:, :], V, ALU.mult).then_inc(rw_dve, 1)
                ve.wait_ge(rw_dve, 2 * m + 2)
            dv = lambda i: dch[:, i, :].rearrange("p (m c) -> p m c", c=NCH)
            st(TTN(dv(2)[:, :, 0:NCH - 1], dv(1)[:, :, 0:NCH - 1], dv(0)[:, :, 1:NCH], ALU.mult))
            ve.wait_ge(rw_act, 36)
            for m in range(NPAIR):
                pb, ab = 36 + RW_PE * m, 36 + RW_ACT * m
                for e in range(2):
                    hs, b0 = HS[e], 3 * e
                    ve.wait_ge(rw_pe, pb + e + 1)
                    if m:
                        ve.wait_ge(rw_act, ab)
                    st.go(TTN(v4(tile(hs[0])), v4(bank[b0][:, :]), mask4("strict"), ALU.mult))
                    st(TTN(v4(tile(hs[2])), v4(bank[b0 + 1][:, :]), mask4("strict_T"), ALU.mult))
                    st.go(TTN(v4(tile(hs[6])), v4(bank[b0 + 2][:, :]), mask4("strict_T"), ALU.mult))
                    TTN(v4(tile(hs[4])), v4(tile(hs[2])), mask4("ident"), ALU.add).then_inc(rw_dve, 1)
                for lev in range(5):
                    for e in range(2) if lev < 4 else ():
                        hs, b0 = HS[e], 3 * e
                        a, b = (0, 1) if lev % 2 == 0 else (1, 0)
                        ve.wait_ge(rw_pe, pb + 2 + 4 * lev + e + 1)
                        st.go(CP(tile(hs[2 + b]), bank[b0 + 1][:, :]))
                    for e in range(2):
                        hs, b0 = HS[e], 3 * e
                        a, b = (0, 1) if lev % 2 == 0 else (1, 0)
                        ve.wait_ge(rw_pe, pb + 2 + 4 * lev + 2 + e + 1)
                        ve.wait_ge(rw_dve, 8 + RW_DVE * m + 2 * lev + e + 1)
                        TTN(tile(hs[4 + b]), bank[b0 + 2][:, :], tile(hs[4 + a]), ALU.add).then_inc(rw_dve, 1)
            bp, bd = 36 + RW_PE * 4, 8 + RW_DVE * 4
            shv = arena[:, SH:SH + 4, :].rearrange("p a b -> p (a b)").rearrange("p (c n) -> p c n", c=NCH)
            def mask_scores(h, k):
                ve.wait_ge(rw_pe, bp + 4 * h + ((1, 2) if h == NCH - 1 else (1, 3))[k])
                TTN(v4(tile(MS[h][k])), v4(bank[2 * (h % 2) + k][:, :]), mask4("incl_T"), ALU.mult).then_inc(rw_dve, 1)

            for c in range(NCH):
                g, p = c // 2, c % 2
                trow = slice(p * HD, (p + 1) * HD)
                if c == 0:
                    ve.wait_ge(rw_act, 36 + RW_ACT * 4)
                    CP(tile(UU + g)[trow, :], tile(U0 + g)[trow, :]).then_inc(rw_dve, 1)
                else:
                    ve.wait_ge(rw_pe, bp + 4 * c)
                    for e in range(2):
                        eh = lambda ap: ap[trow, :].rearrange("p (m e i) -> p m e i", m=4, e=2)[:, :, e, :]
                        ins = TTN(eh(tile(UU + g)), bank[6 - e][trow, 0:256].rearrange("p (m i) -> p m i", m=4),
                                  eh(tile(U0 + g)), ALU.add)
                        if e == 0:
                            st.go(ins)
                        else:
                            ins.then_inc(rw_dve, 1)
                mask_scores(c, 0)
                if c < NCH - 1:
                    ve.wait_ge(rw_pe, bp + 4 * c + 2)
                    s3 = lambda ap: ap.rearrange("p (m i) -> p m i", m=4)
                    if c == 0:
                        st(CP(tile(74)[:, 0:256], bank[7][:, 0:256]))
                    else:
                        st(TTN(tile(74)[:, 0:256], bank[7][:, 0:256], shv[:, c, :], ALU.add))
                    TTN(s3(shv[:, c + 1, :]), s3(tile(74)[:, 0:256]), dv(2)[:, :, c:c + 1].to_broadcast([P, 4, HD]),
                        ALU.mult).then_inc(rw_dve, 1)
                    ve.wait_ge(rw_dve, bd + 4 * c + 3)
                mask_scores(c, 1)
            bp, bd = bp + 30 + 8, bd + 31
            for k in range(4):
                xs_lo(1, lambda k: tile(OF + k), k)
            ba = 36 + RW_ACT * 4 + 4
            for m in range(NPAIR):
                ve.wait_ge(rw_pe, bp + m + 1)
                TTN(tile(GND + m), tile(YY + m), bank[4 + m][:, :], ALU.subtract).then_inc(rw_dve, 1)
            ve.wait_ge(rw_act, ba + 5)
            inverse_roots(GNR, 2)
            for m in range(NPAIR):
                st(STT(tile(GND + m), tile(GND + m), pp("ln_w", m), bank[4 + m][:, :], ALU.mult, ALU.mult))
                st(STT(tile(GND + m), tile(GND + m), pp("ln_b", m), tile(BON + m), ALU.add, ALU.add))
                TTN(tile(ORW + m), tile(GND + m), tile(RG + m), ALU.mult).then_inc(rw_dve, 1)

            for k in range(4, KD):
                xs_lo(1, lambda k: tile(ORW + k - 4), k)
            norm_add(1, "attn_post", lambda k: tile(MO[1] + k))
            norm_scale(2, "ffn_pre", 2, KD)
            ve.sem_inc(ffn_pair, 2)
            q = N_FOX + N_RW + KD
            with ve.Fori(0, KF // 2) as i:
                st.enter(i, 4, KF // 2)
                for j in range(2):
                    ve.wait_ge(evac, i * 4 + q + 2 * j + 2)
                    ve.wait_ge(ffn_pair, i * 2 + j + 1)
                    hi = hid[:, bass.ds(i * 2 + j, 1), :].rearrange("p a t -> p (a t)")
                    lo = hid[:, bass.ds(i * 2 + (KF + j), 1), :].rearrange("p a t -> p (a t)")
                    st(TTN(gu[:, 4 + j, :], gu[:, 2 * j, :], gu[:, 2 * j + 1, :], ALU.mult))
                    st(CP(hi, gu[:, 4 + j, :]))
                    TTN(lo, gu[:, 4 + j, :], hi.bitcast(F32), ALU.subtract).then_inc(ffn_pair, 1)
                st.leave()
            q += 2 * KF
            norm_add(3, "ffn_post", lambda k: tile(MO[3] + k))
            st(TTN(lbt[:, 0, :], par[:, PCOL["lb0"]:PCOL["lb0"] + 8], par[:, PCOL["lb1"]:PCOL["lb1"] + 8], ALU.max))
            st(TTN(lbt[:, 1, :], par[:, PCOL["lb0"]:PCOL["lb0"] + 8], lbt[:, 0, :], ALU.subtract))
            TTN(lbt[:, 2, :], par[:, PCOL["lb1"]:PCOL["lb1"] + 8], lbt[:, 0, :], ALU.subtract).then_inc(lb_ready, 1)
            ve.wait_ge(lb_ready, 2)
            st(TTN(lbt[:, 2, :], lbt[:, 1, :], lbt[:, 2, :], ALU.add))
            st(ve.reciprocal(lbt[:, 2, :], lbt[:, 2, :]))
            st(TTN(lbt[:, 0, :], lbt[:, 1, :], lbt[:, 2, :], ALU.mult))
            TSM(lbt[:, 1, :], lbt[:, 0, :], -1.0, 1.0, ALU.mult, ALU.add).then_inc(hg_dve, 1)
            ve.wait_ge(hg_dve, 1)
            norm_scale(4, "mix_norm", 3, 2 * KD)

            q += KD
            H_ = HGT
            with ve.Fori(0, HG_H) as h:
                st.enter(h, 18, HG_H)
                ve.wait_ge(evac, h * 4 + q + 1)
                lb, lb1 = lbt[:, 0, bass.ds(h, 1)], lbt[:, 1, bass.ds(h, 1)]
                TSM(tile(H_["F"]), tile(H_["F"]), lb1, lb, ALU.mult, ALU.add).then_inc(hg_dve, 1)
                ve.wait_ge(hg_dve, h * 6 + 2)
                st.go(TSM(tile(H_["K"]), tile(H_["F"]), -1.0, 1.0, ALU.mult, ALU.add))
                ve.wait_ge(hg_act, h * 6 + 1)
                st(ve.tensor_tensor_scan(tile(H_["CU"]), cc("reset"), tile(H_["LF"]), 0.0, ALU.mult, ALU.add))
                cu = ch(tile(H_["CU"]))
                TTN(ch(tile(H_["CC"])), cu, cu[:, :, MID:MID + 1].to_broadcast([P, NCH, C]), ALU.subtract).then_inc(hg_dve, 1)
                ve.wait_ge(hg_act, h * 6 + 2)
                st.go(TTN(tile(H_["KD"]), tile(H_["K"]), tile(H_["EM"]), ALU.mult))
                ve.wait_ge(evac, h * 4 + q + 3)
                STT(tile(H_["QD"]), tile(H_["Q"]), HG_D ** -0.5, tile(H_["EP"]), ALU.mult, ALU.mult).then_inc(hg_dve, 1)
                ve.wait_ge(hg_exp, h * 2 + 2)
                st(TTN(dch[:, 5, 0:NCH - 1], ch(tile(H_["EP"]))[:, 0:NCH - 1, C - 1], dch[:, 4, 1:NCH], ALU.mult))
                ve.wait_ge(hg_pe, h * 6 + 3)
                TTN(v4(tile(H_["AM"])), v4(bank[6][:, :]), mask4("incl_T"), ALU.mult).then_inc(hg_dve, 1)
                ve.wait_ge(hg_pe, h * 6 + 4)
                for c in range(NCH - 1):
                    kv = bank[4 + c % 2][:, (c // 2) * P:(c // 2 + 1) * P]
                    src = kv
                    if c:
                        st(TTN(tile(H_["X"])[:, 0:P], kv, H_["S"](c), ALU.add))
                        src = tile(H_["X"])[:, 0:P]
                    ins = TSM(H_["S"](c + 1), src, dch[:, 5, c:c + 1], None, ALU.mult)
                    if c < NCH - 2:
                        st(ins)
                    else:
                        ins.then_inc(hg_dve, 1)
                ve.wait_ge(hg_act, h * 6 + 6)
                st(ve.reciprocal(tile(H_["R2"]), tile(H_["RT"])))
                ve.wait_ge(evac, h * 4 + q + 4)
                wn = par[:, bass.ds(h + PCOL["hg_norm"], 1)]
                st(STT(tile(H_["R2"]), bank[7][:, :], wn, tile(H_["R2"]), ALU.mult, ALU.mult))
                TTN(arena[:, bass.ds(h + OHG, 1), :].rearrange("p a t -> p (a t)"), tile(H_["R2"]), tile(H_["G"]),
                    ALU.mult).then_inc(hg_dve, 1)
                ve.wait_ge(hg_dve, h * 6 + 7)
                st.leave()
            q += 4 * HG_H
            R_ = RTT
            ve.wait_ge(in_rot, 32)
            ve.sem_inc(rt_dve, 1)
            with ve.Fori(0, RET_H) as h:
                st.enter(h, 13, RET_H)
                cos, sin = tile(R_["COS"]), tile(R_["COS"] + 1)
                for k, (src, dst) in enumerate((("Q", "QR"), ("K", "KR"))):
                    x1, x2 = tile(R_[src]), tile(R_[src] + 1)
                    sc = 1.0 if k == 0 else RET_DK ** -0.5
                    ve.wait_ge(evac, h * 12 + q + 2 * k + 2)
                    st.go(STT(tile(R_["T"]), x1, sc, cos, ALU.mult, ALU.mult))
                    st.go(STT(tile(R_["T"] + 1), x2, sc, sin, ALU.mult, ALU.mult))
                    st.go(STT(tile(R_["T"] + 2), x1, sc, sin, ALU.mult, ALU.mult))
                    st(STT(tile(R_["T"] + 3), x2, sc, cos, ALU.mult, ALU.mult))
                    TTN(tile(R_[dst]), tile(R_["T"]), tile(R_["T"] + 1), ALU.subtract).then_inc(rt_dve, 1)
                    TTN(tile(R_[dst] + 1), tile(R_["T"] + 2), tile(R_["T"] + 3), ALU.add).then_inc(rt_dve, 1)
                    ve.wait_ge(rt_dve, h * 12 + 2 * k + 3)
                for s in range(TT):
                    n = T - s * P
                    ve.wait_ge(rt_pe, h * 16 + (1, 2, 5, 6)[s])
                    TTN(tile(R_["AM"] + s)[:, 0:n], bank[5 + s % 2][:, 0:n],
                        arena[:, bass.ds(h + R_["MASK"], 1), 0:n].rearrange("p a t -> p (a t)"), ALU.mult).then_inc(rt_dve, 1)
                ve.wait_ge(rt_act, h * 9 + 9)
                st(ve.reciprocal(tile(R_["R2"]), tile(R_["RT"])))
                for j in range(4):
                    o = arena[:, bass.ds(h * 4 + (ORET + j), 1), :].rearrange("p a t -> p (a t)")
                    st(TTN(o, o, tile(R_["R2"]), ALU.mult))
                    ve.wait_ge(evac, h * 12 + q + 8 + j + 1)
                    TTN(o, o, tile(R_["G"] + j), ALU.mult).then_inc(rt_dve, 1)
                ve.wait_ge(rt_dve, h * 12 + 13)
                st.leave()
            q += 12 * RET_H
            for k in range(24):
                if k >= 2:
                    ve.wait_ge(o_ready, k - 1)
                st(CP(spl[:, k % 2, :], tile(OHG + k)))
                TTN(OHL[k][1], tile(OHG + k), spl[:, k % 2, :].bitcast(F32), ALU.subtract).then_inc(o_lo_ready, 1)
            for k in range(KD):
                ve.wait_ge(evac, q + 4)
                q += 4
                st.go(TTN(tile(MGT), tile(MGT), tile(MGT + 2), ALU.mult))
                st(TTN(tile(MRG + k), tile(MRG + k), tile(MGT + 1), ALU.mult))
                TTN(tile(MRG + k), tile(MRG + k), tile(MGT), ALU.add).then_inc(mg_dve, 1)
            for k in range(KD):
                xs_lo(4, lambda k: tile(MRG + k), k)
            for k in range(KD):
                ve.wait_ge(evac, q + 1)
                q += 1
                TTN(xr(k), xr(k), tile(WO2 + k), ALU.add).then_inc(resid_ready, 1)
            norm_scale(5, "ffn_norm", 5, 3 * KD)
            q += 2 * PEER_H

            io16 = cst[:, CCOL["iota"][0]:CCOL["iota"][0] + 16]
            big = lambda i: arena[:, PBIG + 4 * i:PBIG + 4 * i + 4, :].rearrange("p a b -> p (a b)")
            for t in range(TT):
                ve.wait_ge(tk_act, 4 * (t + 1))
                sc = arena[:, PST + 4 * t:PST + 4 * t + 4, :].rearrange("p a b -> p (a b)")
                for n in range(16):
                    s = sc[:, n * P:(n + 1) * P]
                    st(ve.max(topv[:, n, 0:8], s))
                    st(ve.max_index(topi[:, n, 0:8], topv[:, n, 0:8], s))
                    st(ve.match_replace(s, topv[:, n, 0:8], s, -3.0e38))
                    st(ve.max(topv[:, n, 8:16], s))
                    st.go(ve.max_index(topi[:, n, 8:16], topv[:, n, 8:16], s))
                st.sync()
                st.go(CP(topf, topi))
                tv = topv[:, :, :].rearrange("p (h s) k -> p h s k", s=2)
                tf = topf[:, :, :].rearrange("p (h s) k -> p h s k", s=2)
                cand = big(0).rearrange("p (h a b) -> p h a b", h=8, a=16)
                st(TTN(cand, tv[:, :, 0, :].unsqueeze(3).to_broadcast([P, 8, 16, 16]),
                       tv[:, :, 1, :].unsqueeze(2).to_broadcast([P, 8, 16, 16]), ALU.add))
                if t:
                    ve.wait_ge(tk_exp, t)
                for h in range(8):
                    s = big(0)[:, h * 256:(h + 1) * 256]
                    st(ve.max(bestv[:, h, 0:8], s))
                    st(ve.max_index(besti[:, h, 0:8], bestv[:, h, 0:8], s))
                    st(ve.match_replace(s, bestv[:, h, 0:8], s, -3.0e38))
                    st(ve.max(bestv[:, h, 8:16], s))
                    st.go(ve.max_index(besti[:, h, 8:16], bestv[:, h, 8:16], s))
                st.sync()
                st(CP(gsum[:, 0, :], bestv[:, :, 0]))
                TTN(bestv[:, :, :], bestv[:, :, :], gsum[:, 0, :].unsqueeze(2).to_broadcast([P, 8, 16]),
                    ALU.subtract).then_inc(tk_sub, 1)
                st.go(TSM(bests[:, :, :], besti[:, :, :], 4, None, ALU.logical_shift_right))
                st(TSM(besti[:, :, :], besti[:, :, :], 15, None, ALU.bitwise_and))
                st.go(CP(bestf[:, 0, :, :], bests[:, :, :]))
                st(CP(bestf[:, 1, :, :], besti[:, :, :]))
                if t:
                    ve.wait_ge(tk_pe, 16 + t)
                for s in range(2):
                    hot = big(1).rearrange("p (h k a) -> p h k a", h=8, k=16)
                    st(TTN(hot, bestf[:, s, :, :].unsqueeze(3).to_broadcast([P, 8, 16, 16]),
                           io16.unsqueeze(1).unsqueeze(1).to_broadcast([P, 8, 16, 16]), ALU.is_equal))
                    st(TTN(hot, hot, tf[:, :, s, :].unsqueeze(2).to_broadcast([P, 8, 16, 16]), ALU.mult))
                    st(ve.tensor_reduce(pairs[:, s, :].rearrange("p (h k) -> p h k", h=8), hot, AX.X, ALU.add))
                ve.wait_ge(tk_exp, t + 1)
                st(ve.tensor_reduce(gsum[:, 0, :], bestv[:, :, :], AX.X, ALU.add))
                st(ve.reciprocal(gsum[:, 1, :], gsum[:, 0, :]))
                TTN(pairs[:, 2, :].rearrange("p (h k) -> p h k", h=8), bestv[:, :, :],
                    gsum[:, 1, :].unsqueeze(2).to_broadcast([P, 8, 16]), ALU.mult).then_inc(tk_dve, 1)
                ve.wait_ge(tk_dve, t + 1)
            ve.wait_ge(tk_act, 20)
            iota = cc("iota")
            st(CP(ghi[:, 0, :], tile(PTT + 2)))
            st(TTN(tile(PTT + 2), tile(PTT + 2), ghi[:, 0, :].bitcast(F32), ALU.subtract))
            with ve.Fori(0, NTG // 2) as i:
                for u in range(2 * TG // 4):
                    ve.wait_ge(oh_pe, i * 16 + u + 1)
                    t4 = bass.ds(i * (2 * TG) + 4 * u, 4)
                    TTN(oneB[:, u % 2, :, :], iota.unsqueeze(1).to_broadcast([P, 4, P]),
                              arena[:, PTT + 1, t4].unsqueeze(2).to_broadcast([P, 4, P]), ALU.is_equal)
                    for j in range(4):
                        t1 = bass.ds(i * (2 * TG) + (4 * u + j), 1)
                        key1 = arena[:, PTT, t1]
                        TSM(oneH[:, u % 2, j, :], iota, key1, ghi[:, 0, t1].bitcast(F32), ALU.is_equal, ALU.mult)
                        ins = TSM(oneL[:, u % 2, j, :], iota, key1, arena[:, PTT + 2, t1], ALU.is_equal, ALU.mult)
                    ins.then_inc(oh_dve, 1)
            ve.wait_ge(oh_act, 8 * NTG + 2)
            for d in range(KD):
                st.go(ve.memset(tile(ACC + d), 0.0))
            st.sync()

            def gated(g, it=0):
                b = g % 2
                ve.wait_ge(gld[b], it * 32 + 32 * (g // 2 + 1))
                gates = arena[:, GV + 8 * b:GV + 8 * b + 8, :].rearrange("p a b -> p (a b)").rearrange(
                    "p (g j t) -> p g j t", g=NTG, j=JG)
                by_store = lambda ap: ap.rearrange("p (g t) -> p g t", g=NTG)
                for j in range(JG):
                    h = by_store(tile(HV + 8 * b + j))
                    TTN(h, h, gates[:, :, j, :], ALU.mult).then_inc(ex_prod, 1)
                for j in range(JG):
                    ve.wait_ge(ex_hi, it * 2 * JG + g * JG + j + 1)
                    TTN(GW[b][j][1], tile(HV + 8 * b + j), GW[b][j][0].bitcast(F32), ALU.subtract).then_inc(ex_lo, 1)

            def acc(g, it=0):
                for half in range(2):
                    ve.wait_ge(block_used, it * 2 * JG + B_V + g * JG + 4 * half + 4)
                    if g:
                        ve.wait_ge(ex_acc, it * 16 + 8 * (g - 1) + 4 * half + 4)
                    for d in range(4):
                        o = tile(ACC + 4 * half + d)
                        TTN(o, o, bank[4 * half + d][:, :], ALU.add).then_inc(ex_acc, 1)

            gated(0)
            ve.wait_ge(block_used, B_V)
            gated(1)
            acc(0)
            gated(2)
            acc(1)
            gated(3)
            with ve.Fori(0, NJG // 2 - 2) as i:
                acc(2, i)
                gated(4, i)
                acc(3, i)
                gated(5, i)
            acc(NJG - 2)
            acc(NJG - 1)
            ve.wait_ge(ex_acc, 8 * NJG)
            for k in range(KD):
                TTN(xr(k), xr(k), tile(ACC + k), ALU.add).then_inc(resid_ready, 1)
            norm_root(6)
            for k in range(KD):
                STT(tile(OUT + k), xr(k), pp("final_norm", k), tile(NORM[6][1]), ALU.mult, ALU.mult).then_inc(out_ready, 1)


def _tiles(w, order=None):
    k, n = w.shape
    return w.reshape(k // P, P, n // P, P).transpose(2, 1, 0, 3).reshape(n // P, P, k)


def _constants():
    i = np.arange(P)
    same = (i[:, None] // C) == (i[None, :] // C)
    lower = i[:, None] > i[None, :]
    c = {
        "ident": np.eye(P), "ones": np.ones((P, P)), "bones": same, "bmean": same / HD,
        "strict_T": same & lower.T, "strict": same & lower, "incl_T": same & ~lower,
        "neg": np.where(i[:, None] >= i[None, :], 0.0, NEG), "iota": np.tile(i, (P, 1)),
        "reset": np.tile((np.arange(T) % C != 0), (P, 1)),
    }
    table = np.concatenate([np.asarray(c[n], np.float32) for n, _ in CONSTS], axis=1)
    select = np.zeros((8, 8, P), np.float32)
    select[np.arange(8), np.arange(8)] = -8.0
    half = RET_DK // 2
    inv = np.float32(10000.0) ** (-np.arange(half, dtype=np.float32) / half)
    ang = inv.astype(np.float32)[:, None] * np.arange(T, dtype=np.float32)[None, :]
    rotary = np.stack([np.cos(ang), np.sin(ang)], axis=1).astype(np.float32)
    log_g = np.log1p(-np.exp2(-5.0 - np.arange(RET_H)))
    rel = np.arange(T)[None, :] - i[:, None]
    decay = np.where(rel[:, None, :] >= 0, np.exp(log_g[None, :, None] * np.maximum(rel, 0)[:, None, :]), 0.0)
    return table, select.reshape(8, 8 * P), rotary, decay.astype(np.float32)


def _stream(a):
    w_in = a["w_in"][0]
    fw, rw = 3 * 512, 3 * 512 + 8
    gf = np.zeros((D, P), np.float32)
    gf[:, 0:32] = w_in[:, rw + 1536 + 128 + 128:]
    gf[:, 32:40] = w_in[:, fw:fw + 8]
    parts = [_tiles(w_in[:, 0:1024]), _tiles(gf), _tiles(w_in[:, 1024:fw]), _tiles(w_in[:, rw + 1536:rw + 1536 + 256]), _tiles(w_in[:, rw:rw + 1536])]
    w_out = _tiles(a["w_out"][0]).reshape(2, 2, 2, P, 2, D // 2)
    parts.append(w_out.transpose(0, 4, 1, 3, 2, 5).reshape(KD, P, D))
    gate, up = _tiles(a["ffn_w_gate"][0]), _tiles(a["ffn_w_up"][0])
    parts.append(np.stack([gate, up], axis=1).reshape(2 * KF, P, D))
    down = np.zeros((KD, P, 3 * D), np.float32)
    down[:, :, 0:FF] = _tiles(a["ffn_w_down"][0])
    parts.append(down.reshape(KD, P, 3, D).transpose(0, 2, 1, 3).reshape(3 * KD, P, D))
    w2 = _tiles(a["w_in_2"][0])
    hq, hf, hi, hg = (w2[8 * i:8 * i + 8] for i in range(4))
    parts.append(np.stack([hf, hi, hq, hg], axis=1).reshape(4 * HG_H, P, D))
    rq, rk = (w2[o:o + 8].reshape(4, 2, P, D) for o in (32, 40))
    rv, rg = (w2[o:o + 16].reshape(4, 4, P, D) for o in (48, 64))
    parts.append(np.concatenate([rq, rk, rv, rg], axis=1).reshape(12 * RET_H, P, D))
    ret = _tiles(a["w_branch_ret_2"][0]).reshape(KD, P, 2, D).transpose(0, 2, 1, 3)
    merge = np.concatenate([w2[80:88, None], w2[88:96, None], _tiles(a["w_branch_hg_2"][0])[:, None], ret], axis=1)
    parts.append(merge.reshape(5 * KD, P, D))
    parts.append(_tiles(a["w_out_2"][0]))
    parts.append(_tiles(a["peer_w_q_2"][0]))
    parts.append(a["expert_u_2"][0].reshape(NKEY, NKEY, KD, P).transpose(1, 3, 2, 0).reshape(NKEY, P, D))
    v = a["expert_v_2"][0].reshape(NKEY, NJG, 4, 2, 2, 512).transpose(1, 4, 2, 0, 3, 5)
    parts.append(v.reshape(NKEY, P, D))
    parts.append(np.zeros((N_LOADED - N_BLOCKS, P, D), np.float32))
    return np.concatenate(parts, axis=0)


def _parameters(a):
    col = lambda v: np.asarray(v, np.float32).reshape(-1, P).T
    mu = np.asarray(a["shift_mu"][0])
    mu_gf = np.zeros(P, np.float32)
    mu_gf[0:32] = mu[1536 + 256:]
    f_bias = np.zeros(P, np.float32)
    f_bias[32:40] = a["fox_forget_bias"][0]
    v = {
        "attn_pre": a["attn_norm_pre"], "attn_post": a["attn_norm_post"],
        "mu": np.concatenate([mu_gf, mu[1536:1536 + 256], mu[0:1536]]),
        "w0": a["rwkv_w0"], "a0": a["rwkv_a0"], "k_k": a["rwkv_k_k"], "k_a": a["rwkv_k_a"], "r_k": a["rwkv_r_k"],
        "ln_w": a["rwkv_ln_w"], "ln_b": a["rwkv_ln_b"], "ffn_pre": a["ffn_norm_pre"], "ffn_post": a["ffn_norm_post"],
        "mix_norm": a["norm_mix_w_2"], "lb0": a["hg_lower_bounds_2"][0], "lb1": a["hg_lower_bounds_2"][1],
        "hg_norm": a["hg_norm_w_2"], "ffn_norm": a["norm_ffn_w_2"], "final_norm": a["final_norm_w_2"], "f_bias": f_bias,
        "eps": np.full(P, 1e-6, np.float32), "ln_eps": np.full(P, 64e-5, np.float32),
    }
    return np.ascontiguousarray(np.concatenate([col(v[n]) for n, _ in PARAMS], axis=1))


def kernel(**inputs):
    import concourse.bacc as bacc
    from concourse.bass_utils import run_bass_kernel_spmd as run

    a = {n: np.asarray(v) for n, v in inputs.items()}
    table, select, rotary, decay = _constants()
    low_rank = np.zeros((P, 3, T), np.float32)
    low_rank[0:64, 0] = a["rwkv_w_up"][0]
    low_rank[64:128, 0] = a["rwkv_a_up"][0]
    low_rank[:, 1] = a["rwkv_g_up"][0][0:128]
    low_rank[0:32, 2] = a["rwkv_g_up"][0][128:160]
    arrays = {
        "x_t": np.ascontiguousarray(a["x"][0].T), "parameters": _parameters(a), "constants": table, "selectors": select,
        "rotary": rotary, "ret_decay": decay, "low_rank": low_rank,
        "sub_keys": np.ascontiguousarray(a["peer_sub_keys_2"][0].reshape(16, NKEY, P).transpose(2, 0, 1).reshape(P, 16 * NKEY)),
        "weights": _stream(a),
    }
    nc = bacc.Bacc("TRN2", target_bir_lowering=False, num_devices=1)
    args = [nc.dram_tensor(n, v.shape, F32, kind="ExternalInput").ap() for n, v in arrays.items()]
    gates = nc.dram_tensor("gates", (NTG, P, NKEY * TG), F32, kind="Internal").ap()
    hidden = nc.dram_tensor("hidden", (NKEY, P, T), F32, kind="Internal").ap()
    out = nc.dram_tensor("out_t", (D, T), F32, kind="ExternalOutput").ap()
    build(nc, *args, gates, hidden, out)
    r = run(nc, [arrays], core_ids=[0])
    return np.ascontiguousarray(r.results[0]["out_t"].T)[None]
```
